# Optimizing a Trainium2 kernel written in Bass

```python
import math
import jax
import jax.numpy as jnp
from jax import lax
import numpy as np

D_MODEL = 1024
BATCH = 1
SEQ = 512
DEPTH = 1

CTX_LEN = 256
GRID_W = 64
ROPE_BASE = 10000.0
NORM_EPS = 1e-6

DA_HEADS = 4
DA_QK_DIM = 64
DA_V_DIM = 2 * DA_QK_DIM
DA_WIDTH = DA_HEADS * DA_V_DIM
Q_BLOCK = 128

GLA_HEADS = 4
GLA_K_DIM = 64
GLA_V_DIM = 128
GLA_WIDTH = GLA_HEADS * GLA_V_DIM
GLA_GATE_RANK = 16
GLA_GATE_TAU = 16.0
GLA_CHUNK = 64

MIX_WIDTH = DA_WIDTH + GLA_WIDTH
IN_PROJ_SIZES = (DA_HEADS * 2 * DA_QK_DIM, DA_HEADS * 2 * DA_QK_DIM, DA_WIDTH,
                 GLA_HEADS * GLA_K_DIM, GLA_HEADS * GLA_K_DIM, GLA_WIDTH, GLA_WIDTH,
                 GLA_GATE_RANK, GLA_GATE_RANK)
IN_PROJ_DIM = sum(IN_PROJ_SIZES)

N_GROUPS = 4
EXPERTS_PER_GROUP = 8
N_EXPERTS = N_GROUPS * EXPERTS_PER_GROUP
TOP_K = 2
EXPERT_HIDDEN = 512
DISPATCH_BLOCK = 128


def rms_norm(x, gain):
    xf = x.astype(jnp.float32)
    y = xf * lax.rsqrt(jnp.mean(xf * xf, axis=-1, keepdims=True) + NORM_EPS)
    return (y * gain.astype(jnp.float32)).astype(x.dtype)

def modulate(h, shift, scale):
    return h * (1 + scale) + shift

def split_in_proj(p):
    parts, start = [], 0
    for size in IN_PROJ_SIZES:
        parts.append(p[..., start:start + size])
        start += size
    return parts

def axial_rope_tables(rows, rot_dim):
    n_freq = rot_dim // 4
    r, col = jnp.meshgrid(jnp.arange(rows, dtype=jnp.float32),
                          jnp.arange(GRID_W, dtype=jnp.float32), indexing="ij")
    pos = jnp.stack([r.reshape(-1), col.reshape(-1)], axis=-1)
    inv_freq = jnp.power(ROPE_BASE, -jnp.arange(n_freq, dtype=jnp.float32) / n_freq)
    ang = pos[:, :, None] * inv_freq
    return jnp.cos(ang), jnp.sin(ang)

def apply_axial_rope(x, cos, sin):
    n_freq = cos.shape[-1]
    xr = x.reshape(x.shape[:-1] + (2, 2, n_freq))
    x1, x2 = xr[..., 0, :], xr[..., 1, :]
    cs, sn = cos.astype(x.dtype), sin.astype(x.dtype)
    out = jnp.stack([x1 * cs - x2 * sn, x2 * cs + x1 * sn], axis=-2)
    return out.reshape(x.shape)

def diff_attend(q, k, v, lam):
    s = jnp.einsum("bqhmd,bkhmd->bhmqk", q, k).astype(jnp.float32) * (DA_QK_DIM ** -0.5)
    p = jax.nn.softmax(s, axis=-1)
    a = p[:, :, 0] - lam * p[:, :, 1]
    return jnp.einsum("bhqk,bkhe->bqhe", a.astype(v.dtype), v)

def gla_chunked(q, k, v, log_a, s0):
    B, T, H, dk = q.shape
    dv = v.shape[-1]
    n_chunks = T // GLA_CHUNK

    def chunks(t):
        return jnp.moveaxis(t.reshape(B, n_chunks, GLA_CHUNK, H, t.shape[-1]), 1, 0)

    mask = jnp.tril(jnp.ones((GLA_CHUNK, GLA_CHUNK), dtype=bool))

    def step(state, inp):
        qi, ki, vi, gi = inp
        b = jnp.cumsum(gi.astype(jnp.float32), axis=1)
        b_last = b[:, -1]
        q_dec = qi * jnp.exp(b)
        k_inv = ki * jnp.exp(-b)
        scores = jnp.einsum("bihk,bjhk->bhij", q_dec, k_inv)
        scores = jnp.where(mask, scores, 0.0)
        o = (jnp.einsum("bhij,bjhv->bihv", scores, vi)
             + jnp.einsum("bihk,bhkv->bihv", q_dec, state))
        k_to_end = ki * jnp.exp(b_last[:, None] - b)
        new_state = (state * jnp.exp(b_last)[..., None]
                     + jnp.einsum("bjhk,bjhv->bhkv", k_to_end, vi))
        return new_state, o

    s_final, o = lax.scan(step, s0, (chunks(q), chunks(k), chunks(v), chunks(log_a)))
    o = jnp.moveaxis(o, 0, 1).reshape(B, T, H, dv)
    return o, s_final

def log_gate(lowrank, w2, b):
    return jax.nn.log_sigmoid((lowrank @ w2 + b).astype(jnp.float32)) / GLA_GATE_TAU

def token_mixer(h_lat, h_ctx, cos, sin, lambda_init, w_in, da_lambda, da_subln_g,
                gla_gate_w2, gla_gate_b, gla_norm_g, w_out, with_ctx_out):
    B, S, _ = h_lat.shape
    L = h_ctx.shape[1]
    dt = h_lat.dtype
    dq_l, dk_l, dv_l, gq_l, gk_l, gv_l, gr_l, lrf_l, lrb_l = split_in_proj(h_lat @ w_in)
    dq_c, dk_c, dv_c, gq_c, gk_c, gv_c, gr_c, lrf_c, lrb_c = split_in_proj(h_ctx @ w_in)

    cos_b, sin_b = cos[:, None, None], sin[:, None, None]
    q_l = apply_axial_rope(dq_l.reshape(B, S, DA_HEADS, 2, DA_QK_DIM), cos_b, sin_b)
    k_l = apply_axial_rope(dk_l.reshape(B, S, DA_HEADS, 2, DA_QK_DIM), cos_b, sin_b)
    v_l = dv_l.reshape(B, S, DA_HEADS, DA_V_DIM)
    k_c = dk_c.reshape(B, L, DA_HEADS, 2, DA_QK_DIM)
    v_c = dv_c.reshape(B, L, DA_HEADS, DA_V_DIM)
    lam_p = da_lambda.astype(jnp.float32)
    lam = (jnp.exp(jnp.sum(lam_p[0] * lam_p[1])) - jnp.exp(jnp.sum(lam_p[2] * lam_p[3]))
           + lambda_init)
    k_all = jnp.concatenate([k_c, k_l], axis=1)
    v_all = jnp.concatenate([v_c, v_l], axis=1)
    qb = jnp.moveaxis(q_l.reshape(B, S // Q_BLOCK, Q_BLOCK, DA_HEADS, 2, DA_QK_DIM), 1, 0)
    a_l = lax.map(lambda qi: diff_attend(qi, k_all, v_all, lam), qb)
    a_l = jnp.moveaxis(a_l, 0, 1).reshape(B, S, DA_HEADS, DA_V_DIM)
    a_l = rms_norm(a_l, da_subln_g) * (1.0 - lambda_init)

    def gla_inputs(gq, gk, gv, lrf, lrb, n):
        q = gq.reshape(B, n, GLA_HEADS, GLA_K_DIM) * (GLA_K_DIM ** -0.5)
        k = gk.reshape(B, n, GLA_HEADS, GLA_K_DIM)
        v = gv.reshape(B, n, GLA_HEADS, GLA_V_DIM)
        g_f = log_gate(lrf, gla_gate_w2[0], gla_gate_b[0]).reshape(B, n, GLA_HEADS, GLA_K_DIM)
        g_b = log_gate(lrb, gla_gate_w2[1], gla_gate_b[1]).reshape(B, n, GLA_HEADS, GLA_K_DIM)
        return q, k, v, g_f, g_b

    gql, gkl, gvl, gfl, gbl = gla_inputs(gq_l, gk_l, gv_l, lrf_l, lrb_l, S)
    gqc, gkc, gvc, gfc, gbc = gla_inputs(gq_c, gk_c, gv_c, lrf_c, lrb_c, L)
    flip = lambda t: jnp.flip(t, axis=1)
    s0 = jnp.zeros((B, GLA_HEADS, GLA_K_DIM, GLA_V_DIM), jnp.float32)
    o_cf, s_cf = gla_chunked(gqc, gkc, gvc, gfc, s0)
    o_cb, s_cb = gla_chunked(flip(gqc), flip(gkc), flip(gvc), flip(gbc), s0)
    o_lf, _ = gla_chunked(gql, gkl, gvl, gfl, s_cf)
    o_lb, _ = gla_chunked(flip(gql), flip(gkl), flip(gvl), flip(gbl), s_cb)
    o_l = (o_lf + flip(o_lb)).astype(dt)
    g_l = rms_norm(o_l, gla_norm_g) * jax.nn.silu(gr_l.reshape(B, S, GLA_HEADS, GLA_V_DIM))

    y_lat = jnp.concatenate([a_l.reshape(B, S, DA_WIDTH), g_l.reshape(B, S, GLA_WIDTH)], -1) @ w_out
    if not with_ctx_out:
        return y_lat, None

    q_c = dq_c.reshape(B, L, DA_HEADS, 2, DA_QK_DIM)
    a_c = rms_norm(diff_attend(q_c, k_c, v_c, lam), da_subln_g) * (1.0 - lambda_init)
    o_c = (o_cf + flip(o_cb)).astype(dt)
    g_c = rms_norm(o_c, gla_norm_g) * jax.nn.silu(gr_c.reshape(B, L, GLA_HEADS, GLA_V_DIM))
    y_ctx = jnp.concatenate([a_c.reshape(B, L, DA_WIDTH), g_c.reshape(B, L, GLA_WIDTH)], -1) @ w_out
    return y_lat, y_ctx

def hier_moe(h, w_rg, b_rg, w_re, b_re, w_gate, w_up, w_down):
    T, D = h.shape
    hf = h.astype(jnp.float32)
    g_logits = hf @ w_rg.astype(jnp.float32) + b_rg.astype(jnp.float32)
    g_prob = jax.nn.softmax(g_logits, axis=-1)
    g_sel = jnp.argmax(g_logits, axis=-1)
    g_w = jnp.take_along_axis(g_prob, g_sel[:, None], axis=-1)
    e_logits = (hf @ w_re.astype(jnp.float32) + b_re.astype(jnp.float32)).reshape(
        T, N_GROUPS, EXPERTS_PER_GROUP)
    e_in_group = jnp.take_along_axis(e_logits, g_sel[:, None, None], axis=1)[:, 0]
    top_v, top_i = lax.top_k(e_in_group, TOP_K)
    weights = jax.nn.softmax(top_v, axis=-1) * g_w
    expert_id = (g_sel[:, None] * EXPERTS_PER_GROUP + top_i).astype(jnp.int32)

    tk = T * TOP_K
    n_blocks = -(-(tk + N_EXPERTS * (DISPATCH_BLOCK - 1)) // DISPATCH_BLOCK)
    n_rows = n_blocks * DISPATCH_BLOCK
    flat_e = expert_id.reshape(-1)
    flat_t = jnp.repeat(jnp.arange(T, dtype=jnp.int32), TOP_K)
    flat_w = weights.reshape(-1)
    order = jnp.argsort(flat_e)
    e_sorted = flat_e[order]
    counts = jnp.bincount(flat_e, length=N_EXPERTS)
    starts = jnp.cumsum(counts) - counts
    padded = ((counts + DISPATCH_BLOCK - 1) // DISPATCH_BLOCK) * DISPATCH_BLOCK
    pad_ends = jnp.cumsum(padded)
    pad_starts = pad_ends - padded
    dest = pad_starts[e_sorted] + (jnp.arange(tk) - starts[e_sorted])
    row_tok = jnp.full((n_rows,), T, jnp.int32).at[dest].set(flat_t[order])
    row_w = jnp.zeros((n_rows,), jnp.float32).at[dest].set(flat_w[order])
    block_start = jnp.arange(n_blocks, dtype=jnp.int32) * DISPATCH_BLOCK
    block_e = jnp.minimum(jnp.searchsorted(pad_ends, block_start, side="right"), N_EXPERTS - 1)
    h_pad = jnp.concatenate([h, jnp.zeros((1, D), h.dtype)], axis=0)
    xb = h_pad[row_tok].reshape(n_blocks, DISPATCH_BLOCK, D)

    def expert_block(args):
        xi, e = args
        return (jax.nn.silu(xi @ w_gate[e]) * (xi @ w_up[e])) @ w_down[e]

    yb = lax.map(expert_block, (xb, block_e)).reshape(n_rows, D)
    y = jax.ops.segment_sum(yb * row_w[:, None].astype(yb.dtype), row_tok, num_segments=T + 1)
    return y[:T]

def first_inputs(seed: int = 0) -> dict:
    key = jax.random.key(seed)
    ks = jax.random.split(key, 24)
    f32 = jnp.float32
    D = D_MODEL
    nrm = lambda k, shape, s: jax.random.normal(k, shape, f32) * s
    gain = lambda k, shape: 1.0 + 0.02 * jax.random.normal(k, shape, f32)
    return {
        "x": nrm(ks[0], (BATCH, SEQ, D), 1.0),
        "c": nrm(ks[1], (BATCH, D), 1.0),
        "ctx": nrm(ks[2], (BATCH, CTX_LEN, D), 1.0),
        "c_ctx": nrm(ks[3], (D,), 1.0),
        "w_ada": nrm(ks[4], (DEPTH, D, 6 * D), 0.5 * D ** -0.5),
        "b_ada": nrm(ks[5], (DEPTH, 6 * D), 0.02),
        "norm_mix_g": gain(ks[6], (DEPTH, D)),
        "norm_ffn_g": gain(ks[7], (DEPTH, D)),
        "w_in": nrm(ks[8], (DEPTH, D, IN_PROJ_DIM), D ** -0.5),
        "da_lambda": nrm(ks[9], (DEPTH, 4, DA_QK_DIM), 0.1),
        "da_subln_g": gain(ks[10], (DEPTH, DA_V_DIM)),
        "gla_gate_w2": nrm(ks[11], (DEPTH, 2, GLA_GATE_RANK, GLA_HEADS * GLA_K_DIM), GLA_GATE_RANK ** -0.5),
        "gla_gate_b": nrm(ks[12], (DEPTH, 2, GLA_HEADS * GLA_K_DIM), 0.1),
        "gla_norm_g": gain(ks[13], (DEPTH, GLA_V_DIM)),
        "w_out": nrm(ks[14], (DEPTH, MIX_WIDTH, D), MIX_WIDTH ** -0.5),
        "router_group_w": nrm(ks[15], (DEPTH, D, N_GROUPS), D ** -0.5),
        "router_group_b": nrm(ks[16], (DEPTH, N_GROUPS), 0.01),
        "router_expert_w": nrm(ks[17], (DEPTH, D, N_EXPERTS), D ** -0.5),
        "router_expert_b": nrm(ks[18], (DEPTH, N_EXPERTS), 0.01),
        "expert_w_gate": nrm(ks[19], (DEPTH, N_EXPERTS, D, EXPERT_HIDDEN), D ** -0.5),
        "expert_w_up": nrm(ks[20], (DEPTH, N_EXPERTS, D, EXPERT_HIDDEN), D ** -0.5),
        "expert_w_down": nrm(ks[21], (DEPTH, N_EXPERTS, EXPERT_HIDDEN, D), EXPERT_HIDDEN ** -0.5),
        "final_norm_g": gain(ks[22], (D,)),
    }

def first_block(x, c, ctx, c_ctx, w_ada, b_ada, norm_mix_g, norm_ffn_g, w_in, da_lambda,
              da_subln_g, gla_gate_w2, gla_gate_b, gla_norm_g, w_out, router_group_w,
              router_group_b, router_expert_w, router_expert_b, expert_w_gate, expert_w_up,
              expert_w_down, final_norm_g):
    B, S, D = x.shape
    L = ctx.shape[1]
    rows = S // GRID_W
    cos, sin = axial_rope_tables(rows, DA_QK_DIM)
    for layer in range(DEPTH):
        last = layer == DEPTH - 1
        lambda_init = 0.8 - 0.6 * math.exp(-0.3 * layer)
        mod_lat = (jax.nn.silu(c) @ w_ada[layer] + b_ada[layer])[:, None, :]
        mod_ctx = jax.nn.silu(c_ctx) @ w_ada[layer] + b_ada[layer]
        sh1, sc1, gt1, sh2, sc2, gt2 = jnp.split(mod_lat, 6, axis=-1)
        csh1, csc1, cgt1, csh2, csc2, cgt2 = jnp.split(mod_ctx, 6, axis=-1)

        h_lat = modulate(rms_norm(x, norm_mix_g[layer]), sh1, sc1)
        h_ctx = modulate(rms_norm(ctx, norm_mix_g[layer]), csh1, csc1)
        y_lat, y_ctx = token_mixer(h_lat, h_ctx, cos, sin, lambda_init, w_in[layer],
                                   da_lambda[layer], da_subln_g[layer], gla_gate_w2[layer],
                                   gla_gate_b[layer], gla_norm_g[layer], w_out[layer],
                                   with_ctx_out=not last)
        x = x + gt1 * y_lat

        moe_args = (router_group_w[layer], router_group_b[layer], router_expert_w[layer],
                    router_expert_b[layer], expert_w_gate[layer], expert_w_up[layer],
                    expert_w_down[layer])
        h2 = modulate(rms_norm(x, norm_ffn_g[layer]), sh2, sc2)
        x = x + gt2 * hier_moe(h2.reshape(B * S, D), *moe_args).reshape(B, S, D)
        if not last:
            ctx = ctx + cgt1 * y_ctx
            hc2 = modulate(rms_norm(ctx, norm_ffn_g[layer]), csh2, csc2)
            ctx = ctx + cgt2 * hier_moe(hc2.reshape(B * L, D), *moe_args).reshape(B, L, D)
    return rms_norm(x, final_norm_g)


DEPTH_2 = 2

N_BRANCHES = 3
NA_HEADS = 8
NA_HEAD_DIM = 64
NA_WIDTH = NA_HEADS * NA_HEAD_DIM
NA_WIN_H = 8
NA_WIN_W = 16
GM_GROUPS = 4
GM_CHUNK = 128
GM_GROUP_DIM = 128
GM_WIDTH = GM_GROUPS * GM_GROUP_DIM
MLA_HEADS = 8
MLA_Q_RANK = 256
MLA_KV_RANK = 128
MLA_NOPE = 64
MLA_ROPE = 32
MLA_V = 64
MLA_QK = MLA_NOPE + MLA_ROPE
ROPE_AXIS_PAIRS = MLA_ROPE // 4
ROPE_THETA = 10000.0
FFN_HIDDEN = 4 * D_MODEL
NEG_INF = -1e30
MOD_SCALE = 0.5

OFF_NA_K = 0
OFF_NA_V = OFF_NA_K + NA_WIDTH
OFF_MLA_CKV = OFF_NA_V + NA_WIDTH
OFF_MLA_KR = OFF_MLA_CKV + MLA_KV_RANK
N_CTX_COLS = OFF_MLA_KR + MLA_ROPE
OFF_NA_Q = N_CTX_COLS
OFF_GM_U = OFF_NA_Q + NA_WIDTH
OFF_GM_V = OFF_GM_U + GM_WIDTH
OFF_MLA_CQ = OFF_GM_V + GM_WIDTH
OFF_GATES = OFF_MLA_CQ + MLA_Q_RANK
N_IN_COLS = OFF_GATES + N_BRANCHES * D_MODEL


def rms_norm_2(t, gain):
    tf = t.astype(jnp.float32)
    y = tf * lax.rsqrt(jnp.mean(tf * tf, axis=-1, keepdims=True) + NORM_EPS)
    return (y * gain.astype(jnp.float32)).astype(t.dtype)

def layer_norm(t, gain, bias):
    tf = t.astype(jnp.float32)
    mu = jnp.mean(tf, axis=-1, keepdims=True)
    var = jnp.mean(jnp.square(tf - mu), axis=-1, keepdims=True)
    y = (tf - mu) * lax.rsqrt(var + NORM_EPS)
    return (y * gain.astype(jnp.float32) + bias.astype(jnp.float32)).astype(t.dtype)

def modulate_2(t, shift, scale):
    return t * (1 + scale) + shift

def cols(t, off, width):
    return t[..., off:off + width]

def split_heads(t, n_heads):
    b, n, w = t.shape
    return t.reshape(b, n, n_heads, w // n_heads).transpose(0, 2, 1, 3)

def merge_heads(t):
    b, h, n, d = t.shape
    return t.transpose(0, 2, 1, 3).reshape(b, n, h * d)

def axial_rope(n_tokens):
    t = jnp.arange(n_tokens)
    rows = (t // GRID_W).astype(jnp.float32)
    colsv = (t % GRID_W).astype(jnp.float32)
    freqs = ROPE_THETA ** (-jnp.arange(ROPE_AXIS_PAIRS, dtype=jnp.float32) / ROPE_AXIS_PAIRS)
    ang = jnp.stack([rows[:, None] * freqs, colsv[:, None] * freqs], axis=1)
    return jnp.cos(ang), jnp.sin(ang)

def apply_rope_tail(t, cos, sin):
    head, tail = t[..., :-MLA_ROPE], t[..., -MLA_ROPE:]
    tr = tail.reshape(tail.shape[:-1] + (2, 2, ROPE_AXIS_PAIRS)).astype(jnp.float32)
    x1, x2 = tr[..., 0, :], tr[..., 1, :]
    c, s = cos[:, None], sin[:, None]
    rot = jnp.stack([x1 * c - x2 * s, x2 * c + x1 * s], axis=-2).reshape(tail.shape).astype(t.dtype)
    return jnp.concatenate([head, rot], axis=-1)

def dense_attention(q, k, v):
    b, h, n, d = q.shape
    scale = d ** -0.5
    qb = jnp.moveaxis(q.reshape(b, h, n // Q_BLOCK, Q_BLOCK, d), 2, 0)

    def attend(q_blk):
        s = jnp.einsum('bhqd,bhkd->bhqk', q_blk, k).astype(jnp.float32) * scale
        p = jax.nn.softmax(s, axis=-1).astype(v.dtype)
        return jnp.einsum('bhqk,bhkd->bhqd', p, v)

    out = lax.map(attend, qb)
    return jnp.moveaxis(out, 0, 2).reshape(b, h, n, v.shape[-1])

def neighbourhood_attention(q, k, v, k_ctx, v_ctx, rpb):
    b, h, n, dh = q.shape
    rows = n // GRID_W
    kh = min(NA_WIN_H, rows)
    kw = NA_WIN_W
    scale = dh ** -0.5
    qg = jnp.moveaxis(q.reshape(b, h, rows, GRID_W, dh), 2, 0)
    kg = k.reshape(b, h, rows, GRID_W, dh)
    vg = v.reshape(b, h, rows, GRID_W, dh)
    r = jnp.arange(rows)
    r0 = jnp.clip(r - kh // 2, 0, rows - kh)
    cq = jnp.arange(GRID_W)
    c0 = jnp.clip(cq - kw // 2, 0, GRID_W - kw)
    col_in = (cq[None, :] >= c0[:, None]) & (cq[None, :] < c0[:, None] + kw)
    dc = jnp.clip(cq[None, :] - cq[:, None], -(NA_WIN_W - 1), NA_WIN_W - 1) + NA_WIN_W - 1

    def row_block(args):
        q_r, r_i, r0_i = args
        k_band = lax.dynamic_slice_in_dim(kg, r0_i, kh, axis=2)
        v_band = lax.dynamic_slice_in_dim(vg, r0_i, kh, axis=2)
        dr = r0_i + jnp.arange(kh) - r_i + NA_WIN_H - 1
        bias = rpb[:, dr[None, :, None], dc[:, None, :]].astype(jnp.float32)
        s_loc = jnp.einsum('bhqd,bhkcd->bhqkc', q_r, k_band).astype(jnp.float32) * scale + bias
        s_loc = jnp.where(col_in[:, None, :], s_loc, NEG_INF).reshape(b, h, GRID_W, kh * GRID_W)
        s_ctx = jnp.einsum('bhqd,bhld->bhql', q_r, k_ctx).astype(jnp.float32) * scale
        p = jax.nn.softmax(jnp.concatenate([s_loc, s_ctx], axis=-1), axis=-1).astype(v.dtype)
        p_loc = p[..., :kh * GRID_W].reshape(b, h, GRID_W, kh, GRID_W)
        return (jnp.einsum('bhqkc,bhkcd->bhqd', p_loc, v_band)
                + jnp.einsum('bhql,bhld->bhqd', p[..., kh * GRID_W:], v_ctx))

    out = lax.map(row_block, (qg, r, r0))
    return jnp.moveaxis(out, 0, 2).reshape(b, h, n, dh)

def spatial_gating(u, v, ln_g, ln_b, w_s, b_s):
    b, n, _ = v.shape
    v = layer_norm(v, ln_g, ln_b)
    vc = v.reshape(b, n // GM_CHUNK, GM_CHUNK, GM_GROUPS, GM_GROUP_DIM)
    mixed = jnp.einsum('gpq,bnqgc->bnpgc', w_s, vc) + b_s.T[:, :, None]
    return u * mixed.reshape(b, n, GM_WIDTH)

def mla_queries(c_q, cq_gain, w_uq, q_gain, rope):
    b, n, _ = c_q.shape
    q = (rms_norm_2(c_q, cq_gain) @ w_uq).reshape(b, n, MLA_HEADS, MLA_QK)
    q = rms_norm_2(q, q_gain)
    if rope is not None:
        q = apply_rope_tail(q, rope[0], rope[1])
    return q.transpose(0, 2, 1, 3)

def mla_keys_values(c_kv, k_rope, ckv_gain, w_ukv, k_gain, rope):
    b, n, _ = c_kv.shape
    kv = (rms_norm_2(c_kv, ckv_gain) @ w_ukv).reshape(b, n, MLA_HEADS, MLA_NOPE + MLA_V)
    k_nope, v = kv[..., :MLA_NOPE], kv[..., MLA_NOPE:]
    k_r = jnp.broadcast_to(k_rope[:, :, None, :], (b, n, MLA_HEADS, MLA_ROPE))
    k = rms_norm_2(jnp.concatenate([k_nope, k_r], axis=-1), k_gain)
    if rope is not None:
        k = apply_rope_tail(k, rope[0], rope[1])
    return k.transpose(0, 2, 1, 3), v.transpose(0, 2, 1, 3)

def merge_branches(y_na, y_gm, y_mla, gate_logits, na_w_o, gm_w_o, mla_w_o, w_out):
    g = jax.nn.sigmoid(gate_logits).reshape(gate_logits.shape[:-1] + (N_BRANCHES, D_MODEL))
    y = g[..., 0, :] * (y_na @ na_w_o) + g[..., 1, :] * (y_gm @ gm_w_o) + g[..., 2, :] * (y_mla @ mla_w_o)
    return y @ w_out

def squared_relu_mlp(h, w1, w2):
    return jnp.square(jax.nn.relu(h @ w1)) @ w2

def second_inputs(seed: int = 0) -> dict:
    key = jax.random.key(seed)
    ks = jax.random.split(key, 28)
    f32 = jnp.float32

    def nrm(k, shape, scale):
        return scale * jax.random.normal(k, shape, f32)

    def gain(k, shape):
        return 1.0 + 0.02 * jax.random.normal(k, shape, f32)

    L = DEPTH_2
    return {
        'x': nrm(ks[0], (BATCH, SEQ, D_MODEL), 1.0),
        'c': nrm(ks[1], (BATCH, D_MODEL), 1.0),
        'ctx': nrm(ks[2], (BATCH, CTX_LEN, D_MODEL), 1.0),
        'c_ctx': nrm(ks[3], (D_MODEL,), 1.0),
        'w_mod': nrm(ks[4], (L, D_MODEL, 6 * D_MODEL), MOD_SCALE * D_MODEL ** -0.5),
        'b_mod': nrm(ks[5], (L, 6 * D_MODEL), 0.02),
        'g_norm1': gain(ks[6], (L, D_MODEL)),
        'g_norm2': gain(ks[7], (L, D_MODEL)),
        'w_in': nrm(ks[8], (L, D_MODEL, N_IN_COLS), D_MODEL ** -0.5),
        'na_q_gain': gain(ks[9], (L, NA_HEAD_DIM)),
        'na_k_gain': gain(ks[10], (L, NA_HEAD_DIM)),
        'na_rpb': nrm(ks[11], (L, NA_HEADS, 2 * NA_WIN_H - 1, 2 * NA_WIN_W - 1), 0.1),
        'na_w_o': nrm(ks[12], (L, NA_WIDTH, D_MODEL), NA_WIDTH ** -0.5),
        'gm_ln_g': gain(ks[13], (L, GM_WIDTH)),
        'gm_ln_b': nrm(ks[14], (L, GM_WIDTH), 0.02),
        'gm_w_s': nrm(ks[15], (L, GM_GROUPS, GM_CHUNK, GM_CHUNK), GM_CHUNK ** -0.5),
        'gm_b_s': gain(ks[16], (L, GM_GROUPS, GM_CHUNK)),
        'gm_w_o': nrm(ks[17], (L, GM_WIDTH, D_MODEL), GM_WIDTH ** -0.5),
        'mla_cq_gain': gain(ks[18], (L, MLA_Q_RANK)),
        'mla_ckv_gain': gain(ks[19], (L, MLA_KV_RANK)),
        'mla_w_uq': nrm(ks[20], (L, MLA_Q_RANK, MLA_HEADS * MLA_QK), MLA_Q_RANK ** -0.5),
        'mla_w_ukv': nrm(ks[21], (L, MLA_KV_RANK, MLA_HEADS * (MLA_NOPE + MLA_V)), MLA_KV_RANK ** -0.5),
        'mla_q_gain': gain(ks[22], (L, MLA_QK)),
        'mla_k_gain': gain(ks[23], (L, MLA_QK)),
        'mla_w_o': nrm(ks[24], (L, MLA_HEADS * MLA_V, D_MODEL), (MLA_HEADS * MLA_V) ** -0.5),
        'w_out': nrm(ks[25], (L, D_MODEL, D_MODEL), D_MODEL ** -0.5),
        'ffn_w1': nrm(ks[26], (L, D_MODEL, FFN_HIDDEN), D_MODEL ** -0.5),
        'ffn_w2': nrm(ks[27], (L, FFN_HIDDEN, D_MODEL), FFN_HIDDEN ** -0.5),
    }

def second_block(x, c, ctx, c_ctx, w_mod, b_mod, g_norm1, g_norm2, w_in, na_q_gain, na_k_gain, na_rpb,
              na_w_o, gm_ln_g, gm_ln_b, gm_w_s, gm_b_s, gm_w_o, mla_cq_gain, mla_ckv_gain, mla_w_uq,
              mla_w_ukv, mla_q_gain, mla_k_gain, mla_w_o, w_out, ffn_w1, ffn_w2):
    rope = axial_rope(x.shape[1])
    s_c = jax.nn.silu(c)
    s_ctx = jax.nn.silu(c_ctx)[None]
    for i in range(DEPTH_2):
        last = i == DEPTH_2 - 1
        mod = (s_c @ w_mod[i] + b_mod[i])[:, None, :]
        sh1, sc1, gt1, sh2, sc2, gt2 = jnp.split(mod, 6, axis=-1)
        n_mod_c = 2 * D_MODEL if last else 6 * D_MODEL
        mod_c = (s_ctx @ w_mod[i][:, :n_mod_c] + b_mod[i][:n_mod_c])[:, None, :]
        mc = jnp.split(mod_c, n_mod_c // D_MODEL, axis=-1)

        h = modulate_2(rms_norm_2(x, g_norm1[i]), sh1, sc1)
        hc = modulate_2(rms_norm_2(ctx, g_norm1[i]), mc[0], mc[1])
        p = h @ w_in[i]
        pc = hc @ w_in[i][:, :(N_CTX_COLS if last else N_IN_COLS)]

        k_na_c = rms_norm_2(split_heads(cols(pc, OFF_NA_K, NA_WIDTH), NA_HEADS), na_k_gain[i])
        v_na_c = split_heads(cols(pc, OFF_NA_V, NA_WIDTH), NA_HEADS)
        k_mla_c, v_mla_c = mla_keys_values(cols(pc, OFF_MLA_CKV, MLA_KV_RANK), cols(pc, OFF_MLA_KR, MLA_ROPE),
                                           mla_ckv_gain[i], mla_w_ukv[i], mla_k_gain[i], None)

        q_na = rms_norm_2(split_heads(cols(p, OFF_NA_Q, NA_WIDTH), NA_HEADS), na_q_gain[i])
        k_na = rms_norm_2(split_heads(cols(p, OFF_NA_K, NA_WIDTH), NA_HEADS), na_k_gain[i])
        v_na = split_heads(cols(p, OFF_NA_V, NA_WIDTH), NA_HEADS)
        y_na = merge_heads(neighbourhood_attention(q_na, k_na, v_na, k_na_c, v_na_c, na_rpb[i]))
        y_gm = spatial_gating(jax.nn.gelu(cols(p, OFF_GM_U, GM_WIDTH), approximate=False),
                              jax.nn.gelu(cols(p, OFF_GM_V, GM_WIDTH), approximate=False),
                              gm_ln_g[i], gm_ln_b[i], gm_w_s[i], gm_b_s[i])
        q_mla = mla_queries(cols(p, OFF_MLA_CQ, MLA_Q_RANK), mla_cq_gain[i], mla_w_uq[i], mla_q_gain[i], rope)
        k_mla, v_mla = mla_keys_values(cols(p, OFF_MLA_CKV, MLA_KV_RANK), cols(p, OFF_MLA_KR, MLA_ROPE),
                                       mla_ckv_gain[i], mla_w_ukv[i], mla_k_gain[i], rope)
        y_mla = merge_heads(dense_attention(q_mla, jnp.concatenate([k_mla_c, k_mla], axis=2),
                                            jnp.concatenate([v_mla_c, v_mla], axis=2)))
        mix = merge_branches(y_na, y_gm, y_mla, cols(p, OFF_GATES, N_BRANCHES * D_MODEL),
                             na_w_o[i], gm_w_o[i], mla_w_o[i], w_out[i])
        x_new = x + gt1 * mix
        x_new = x_new + gt2 * squared_relu_mlp(modulate_2(rms_norm_2(x_new, g_norm2[i]), sh2, sc2),
                                               ffn_w1[i], ffn_w2[i])

        if not last:
            q_na_c = rms_norm_2(split_heads(cols(pc, OFF_NA_Q, NA_WIDTH), NA_HEADS), na_q_gain[i])
            y_na_c = merge_heads(dense_attention(q_na_c, k_na_c, v_na_c))
            y_gm_c = spatial_gating(jax.nn.gelu(cols(pc, OFF_GM_U, GM_WIDTH), approximate=False),
                                    jax.nn.gelu(cols(pc, OFF_GM_V, GM_WIDTH), approximate=False),
                                    gm_ln_g[i], gm_ln_b[i], gm_w_s[i], gm_b_s[i])
            q_mla_c = mla_queries(cols(pc, OFF_MLA_CQ, MLA_Q_RANK), mla_cq_gain[i], mla_w_uq[i],
                                  mla_q_gain[i], None)
            y_mla_c = merge_heads(dense_attention(q_mla_c, k_mla_c, v_mla_c))
            mix_c = merge_branches(y_na_c, y_gm_c, y_mla_c, cols(pc, OFF_GATES, N_BRANCHES * D_MODEL),
                                   na_w_o[i], gm_w_o[i], mla_w_o[i], w_out[i])
            ctx = ctx + mc[2] * mix_c
            ctx = ctx + mc[5] * squared_relu_mlp(modulate_2(rms_norm_2(ctx, g_norm2[i]), mc[3], mc[4]),
                                                 ffn_w1[i], ffn_w2[i])
        x = x_new
    return x


def setup_inputs(seed=0):
    out = dict(first_inputs(seed))
    for name, value in second_inputs(seed + 1).items():
        if name != "x":
            out[name + "_2"] = value
    return out


def reference(
    x, c, ctx, c_ctx, w_ada, b_ada, norm_mix_g, norm_ffn_g, w_in, da_lambda, da_subln_g,
    gla_gate_w2, gla_gate_b, gla_norm_g, w_out, router_group_w, router_group_b, router_expert_w,
    router_expert_b, expert_w_gate, expert_w_up, expert_w_down, final_norm_g, c_2, ctx_2,
    c_ctx_2, w_mod_2, b_mod_2, g_norm1_2, g_norm2_2, w_in_2, na_q_gain_2, na_k_gain_2, na_rpb_2,
    na_w_o_2, gm_ln_g_2, gm_ln_b_2, gm_w_s_2, gm_b_s_2, gm_w_o_2, mla_cq_gain_2, mla_ckv_gain_2,
    mla_w_uq_2, mla_w_ukv_2, mla_q_gain_2, mla_k_gain_2, mla_w_o_2, w_out_2, ffn_w1_2, ffn_w2_2,
):
    x = first_block(
        x, c, ctx, c_ctx, w_ada, b_ada, norm_mix_g, norm_ffn_g, w_in, da_lambda, da_subln_g,
        gla_gate_w2, gla_gate_b, gla_norm_g, w_out, router_group_w, router_group_b,
        router_expert_w, router_expert_b, expert_w_gate, expert_w_up, expert_w_down,
        final_norm_g,
    )
    return second_block(
        x, c_2, ctx_2, c_ctx_2, w_mod_2, b_mod_2, g_norm1_2, g_norm2_2, w_in_2, na_q_gain_2,
        na_k_gain_2, na_rpb_2, na_w_o_2, gm_ln_g_2, gm_ln_b_2, gm_w_s_2, gm_b_s_2, gm_w_o_2,
        mla_cq_gain_2, mla_ckv_gain_2, mla_w_uq_2, mla_w_ukv_2, mla_q_gain_2, mla_k_gain_2,
        mla_w_o_2, w_out_2, ffn_w1_2, ffn_w2_2,
    )


_drawn_inputs = setup_inputs


def setup_inputs(seed=0):
    import zlib

    import numpy as np

    out = dict(_drawn_inputs(seed))
    spreads = {}
    factors = {'norm_mix_g': 7.044,
     'norm_ffn_g': 3.747,
     'da_lambda': 8.0,
     'da_subln_g': 8.0,
     'gla_gate_b': 5.829,
     'gla_norm_g': 8.0,
     'router_group_b': 8.0,
     'router_expert_b': 7.042,
     'final_norm_g': 2.71,
     'ctx_2': 3.259,
     'g_norm1_2': 8.0,
     'g_norm2_2': 4.594,
     'na_q_gain_2': 8.0,
     'na_k_gain_2': 8.0,
     'na_rpb_2': 34.104,
     'gm_ln_g_2': 8.0,
     'gm_ln_b_2': 8.0,
     'gm_b_s_2': 8.0,
     'mla_cq_gain_2': 8.0,
     'mla_ckv_gain_2': 8.0,
     'mla_q_gain_2': 8.0,
     'mla_k_gain_2': 8.0}
    for name, (base, spread) in spreads.items():
        noise = np.random.default_rng([zlib.crc32(name.encode()), seed]).standard_normal(out[name].shape)
        drawn = base * np.exp(spread * noise) if base else spread * noise
        out[name] = jnp.asarray(drawn.astype(out[name].dtype))
    for name, factor in factors.items():
        out[name] = (out[name] * factor).astype(out[name].dtype)
    return out
```

```python
import math
from contextlib import ExitStack

import numpy as np

import concourse.bass as bass
from concourse import mybir

F32 = mybir.dt.float32
I32 = mybir.dt.int32
U32 = mybir.dt.uint32
ALU = mybir.AluOpType
ACT = mybir.ActivationFunctionType
AX = mybir.AxisListType.X

P = 128
D = 1024
KT = D // P
TL, TC = 4, 2
TA = TL + TC
NTOK = TA * P
CHUNK = 64
EPS = 1e-6
NEG = -1e30
BANK = 512

DQ, DK, DV, GQ, GK, GV, GR, LRF, LRB, IN1 = 0, 512, 1024, 1536, 1792, 2048, 2560, 3072, 3088, 3104
NK, NV, CKV, KR, NQ, GU, GMV, CQ, GATES = 0, 512, 1024, 1152, 1184, 1696, 2208, 2720, 2976
PW = IN1
NE, NG, EH = 32, 4, 512
CAP = 64
NBLK = 48
HALF = 4096

C_ID, C_TF, C_TB, C_BLK, C_US, C_CH = 0, 128, 256, 384, 512, 640
C_R1C, C_R1S, C_R2C, C_R2S, C_NM, C_NB = 642, 898, 1154, 1282, 1410, 1474
C_I32, C_E64, C_ONE, C_ROW, C_TA, C_TZ, C_TK, C_N = 1538, 1570, 1602, 1730, 1746, 1874, 2002, 2006

R_C, R_G, R_NAQ, R_NAK, R_BS, R_N = 0, 48, 96, 98, 100, 108


def constants():
    c = np.zeros((P, C_N), np.float32)
    i = np.arange(P)
    same = i[:, None] // CHUNK == i[None, :] // CHUNK
    c[:, C_ID:C_ID + P] = np.eye(P)
    c[:, C_TF:C_TF + P] = same & (i[:, None] <= i[None, :])
    c[:, C_TB:C_TB + P] = same & (i[:, None] >= i[None, :])
    c[:, C_TK:C_TK + TL] = i[:, None] + P * np.arange(TL)
    c[:, C_TA:C_TA + P] = same & (i[:, None] > i[None, :])
    c[:, C_TZ:C_TZ + P] = same & (i[:, None] < i[None, :])
    c[:, C_BLK:C_BLK + P] = same
    c[:, C_US:C_US + P] = i[:, None] < i[None, :]
    c[:, C_CH:C_CH + 2] = i[:, None] // CHUNK == np.arange(2)
    tok = np.arange(TL * P)
    pos = np.stack([tok // 64, tok % 64], 1).astype(np.float32)
    for n, (cc, cs) in ((16, (C_R1C, C_R1S)), (8, (C_R2C, C_R2S))):
        inv = np.power(np.float32(10000.0), -np.arange(n, dtype=np.float32) / np.float32(n)).astype(np.float32)
        ang = pos[:, :, None] * inv
        cos = np.repeat(np.cos(ang)[:, :, None, :], 2, 2)
        sin = np.sin(ang)[:, :, None, :] * np.array([-1.0, 1.0], np.float32)[:, None]
        for at, t in ((cc, cos), (cs, sin)):
            c[:, at:at + TL * 4 * n] = t.reshape(TL, P, 4 * n).transpose(1, 0, 2).reshape(P, -1)
    col = i % 64
    c0 = np.clip(col - 8, 0, 48)
    kc = np.arange(64)
    inw = (kc[None] >= c0[:, None]) & (kc[None] < c0[:, None] + 16)
    c[:, C_NM:C_NM + 64] = inw
    c[:, C_NB:C_NB + 64] = np.where(inw, 0.0, NEG)
    c[:, C_I32:C_I32 + 32] = np.arange(32, 0, -1)
    c[:, C_E64:C_E64 + 32] = np.arange(32) * CAP
    c[:, C_ONE:C_ONE + P] = 1.0
    c[:, C_ROW:C_ROW + 16] = np.arange(16)
    return c


class Plan:

    def __init__(self, n, owners):
        self.mm0, self.own, self.val = n["mm"], owners, []
        for o in owners:
            if o != "-":
                n[o] += 1
            self.val.append(n.get(o, 0))
        n["mm"] += len(owners)

    def done(self, i):
        return self.mm0 + i + 1


def program(nc, I, out):
    ctx = ExitStack()
    with ctx:
        def sb(name, shape, dt=F32):
            return ctx.enter_context(nc.sbuf_tensor(name, shape, dt))

        def sem(name):
            return ctx.enter_context(nc.semaphore(name))

        ring = sb("ring", [P, 2 * HALF])
        xl = sb("xl", [P, TA, D])
        hT = sb("hT", [P, KT * NTOK])
        pj = sb("pj", [P, TA * PW])
        cst = sb("consts", [P, C_N])
        small = sb("small", [P, 1152])
        Z = sb("Z", [P, 10700])
        ps = ctx.enter_context(nc.psum_tensor("ps", [P, 8 * BANK], F32))

        hTk = hT[:, :].rearrange("p (k n) -> p k n", k=KT)
        pjt = pj[:, :].rearrange("p (t n) -> p t n", t=TA)

        def bank(b, n=BANK):
            return ps[:, b * BANK:b * BANK + n]

        def C(at, n=P):
            return cst[:, at:at + n]

        ident = C(C_ID)

        cols = small[:, 0:R_N]
        modc = small[:, 112:400].rearrange("p (l n) -> p l n", l=3)
        Ac = small[:, 400:496].rearrange("p (l w n k) -> p l w n k", l=3, w=2, n=2)
        st = small[:, 500:1100]

        modd = nc.dram_tensor("modd", (3, 2, 6 * D), F32, kind="Internal").ap()
        hTd = nc.dram_tensor("hTd", (P, KT * NTOK), F32, kind="Internal").ap()
        xnd = nc.dram_tensor("xnd", (TL * P, D), F32, kind="Internal").ap()
        rowtok = nc.dram_tensor("rowtok", (NBLK * CAP, 1), I32, kind="Internal").ap()
        ybuf = nc.dram_tensor("ybuf", (NBLK * CAP, D), F32, kind="Internal").ap()

        stage_done = sem("stage_done")
        mm_done, evac_a, evac_v = sem("mm_done"), sem("evac_a"), sem("evac_v")
        EV = {"a": evac_a, "v": evac_v}
        slot_in = [sem("slot0_in"), sem("slot1_in")]
        params_in, cols_in, mod_st, modr_in = sem("params_in"), sem("cols_in"), sem("mod_st"), sem("modr_in")
        ctx_in, x_in = sem("ctx_in"), sem("x_in")
        silu_c = sem("silu_c")
        sumsq, var, std, xn_ok = sem("sumsq"), sem("var"), sem("std"), sem("xn_ok")
        s_done, s_free_a, s_free_v = sem("s_done"), sem("s_free_a"), sem("s_free_v")
        mx_ok, e_ok, a_ok, t_done = sem("mx_ok"), sem("e_ok"), sem("a_ok"), sem("t_done")
        et_a, et_v, o_done, y_ok = sem("et_a"), sem("et_v"), sem("o_done"), sem("y_ok")
        prep_done, prep_a, prep_v = sem("prep_done"), sem("prep_a"), sem("prep_v")
        v2a, a2v, v2p, prm = sem("v2a"), sem("a2v"), sem("v2p"), sem("prm")
        out_in, gate_in = sem("out_in"), sem("gate_in")
        rparams, zero_ok, rowz, idx_ok = sem("rparams"), sem("zero_ok"), sem("rowz"), sem("idx_ok")
        scat, rows_in, xg_in, xn_st = sem("scat"), sem("rows_in"), sem("xg_in"), sem("xn_st")
        w_used = [sem(f"w_used{m}") for m in range(3)]
        w_in_ = [sem(f"w_in{m}") for m in range(6)]
        xt_done, xt_a, xt_v, silu_ok = sem("xt_done"), sem("xt_a"), sem("xt_v"), sem("silu_ok")
        hu_ok, ht_done, ht_a = sem("hu_ok"), sem("ht_done"), sem("ht_a")
        y_a, y_v, y_out, yg_free = sem("y_a"), sem("y_v"), sem("y_out"), sem("yg_free")
        prm2, rp_ok, rp_in, tb_free, tb_ok = sem("prm2"), sem("rp_ok"), sem("rp_in"), sem("tb_free"), sem("tb_ok")
        tb_in, gelu_ok = [sem("tb_in0"), sem("tb_in1")], sem("gelu_ok")
        spill, unspill = sem("spill"), sem("unspill")
        y_stored = sem("y_stored")
        ex_used, ybz = sem("ex_used"), sem("ybz")
        yg_in, fng_in = [sem("yg_in0"), sem("yg_in1")], sem("fng_in")

        def tally():
            return {k: 0 for k in ("mm", "a", "v", "fence", "chunk", "ss", "var", "std", "xn", "at", "a2v", "v2a", "v2p", "prm")}

        def fence(eng, n):
            eng.drain().then_inc(stage_done, 1)
            n["fence"] += 4
            eng.wait_ge(stage_done, n["fence"])

        def load_chunk(sp, n, dst, src, rel):
            c = n["chunk"]
            if rel[c % 2]:
                sp.wait_ge(mm_done, rel[c % 2])
            o = (c % 2) * HALF
            sp.dma_start(dst(ring[:, o:o + HALF]), src).then_inc(slot_in[c % 2], 16)
            n["chunk"] += 1

        def take_chunk(pe, n):
            c = n["chunk"]
            pe.wait_ge(slot_in[c % 2], 16 * (c // 2 + 1))
            n["chunk"] += 1
            o = (c % 2) * HALF
            return ring[:, o:o + HALF]

        WM = [I["w_ada"][0], I["w_mod_2"][0], I["w_mod_2"][1]]
        BM = [I["b_ada"][0], I["b_mod_2"][0], I["b_mod_2"][1]]
        brow = pj[:, 0:9 * BANK]
        modrow = pj[:, 9 * BANK:18 * BANK]
        sT = small[:, 1100:1148]
        rows = Z[:, 0:P]
        modr = Z[:, P:4 * P]

        def plan_mods(n):
            return Plan(n, ("a",) + ("-", "-", "-", "v") * 9 + ("a",) * 3)

        def sp_mods(sp, n, rel):
            p = plan_mods(n)
            i = 1
            for l in range(3):
                for r in range(3):
                    for q in range(4):
                        src = WM[l][256 * q:256 * q + 256, 2048 * r:2048 * r + 2048].rearrange("(k p) n -> p k n", p=P)
                        c = n["chunk"]
                        load_chunk(sp, n, lambda s: s[:, :].rearrange("p (k n) -> p k n", k=2), src, rel)
                        rel[c % 2] = p.done(i)
                        i += 1

        def pe_mods(pe, n):
            p = plan_mods(n)
            pe.wait_ge(params_in, 16)
            pe.wait_ge(cols_in, 16 * N_COLS)
            nc.tensor.transpose(bank(0, R_N), rows[0:R_N, :], ident[0:R_N, 0:R_N]).then_inc(mm_done, 1)
            pe.wait_ge(silu_c, 1)
            i = 1
            for l in range(3):
                for r in range(3):
                    g = 3 * l + r
                    b = 1 + g % 2
                    if g >= 2:
                        pe.wait_ge(evac_v, p.val[i - 8 + 3])
                    for q in range(4):
                        s = take_chunk(pe, n)
                        for kk in range(2):
                            k = 2 * q + kk
                            for j in range(4):
                                last = nc.tensor.matmul(ps[32 * j:32 * j + 2, b * BANK:(b + 1) * BANK],
                                                        sT[:, 16 * l + k:16 * l + k + 9:8],
                                                        s[:, 2048 * kk + 512 * j:2048 * kk + 512 * j + 512],
                                                        start=(k == 0), stop=(k == KT - 1))
                        last.then_inc(mm_done, 1)
                        i += 1
            pe.wait_ge(modr_in, 48)
            for l in range(3):
                nc.tensor.transpose(bank(3 + l, 96), modr[0:96, P * l:P * l + P], ident[0:96, 0:96]).then_inc(mm_done, 1)
                i += 1

        def act_mods(act, n):
            p = plan_mods(n)
            act.wait_ge(mm_done, p.done(0))
            act.activation(cols, bank(0, R_N), ACT.Copy).then_inc(evac_a, 1)
            act.wait_ge(evac_a, p.val[0])
            act.activation(sT, cols[:, 0:48], ACT.Silu).then_inc(silu_c, 1)
            for l in range(3):
                act.wait_ge(evac_v, p.val[1 + 12 * l + 11])
                for j in range(4):
                    act.dma_start(modd[l].rearrange("w (r j n) -> w r j n", r=3, j=4)[:, :, j, :],
                                  modrow[32 * j:32 * j + 2, 1536 * l:1536 * l + 1536].rearrange("w (r n) -> w r n", r=3)
                                  ).then_inc(mod_st, 16)
                act.wait_ge(mod_st, 64 * (l + 1))
                act.dma_start(modr[0:96, P * l:P * l + P], modd[l].rearrange("w (s q) -> (w s) q", q=P)).then_inc(modr_in, 16)
            for l in range(3):
                act.wait_ge(mm_done, p.done(37 + l))
                act.activation(modc[:, l, :], bank(3 + l, 96), ACT.Copy).then_inc(evac_a, 1)

        def dve_mods(dve, n):
            p = plan_mods(n)
            dve.wait_ge(cols_in, 16 * N_COLS)
            for g in range(9):
                i = 1 + 4 * g + 3
                dve.wait_ge(mm_done, p.done(i))
                for j in range(4):
                    rs = slice(32 * j, 32 * j + 2)
                    last = nc.vector.tensor_tensor(modrow[rs, BANK * g:BANK * g + BANK],
                                                   ps[rs, (1 + g % 2) * BANK:(2 + g % 2) * BANK],
                                                   brow[rs, BANK * g:BANK * g + BANK], ALU.add)
                last.then_inc(evac_v, 1)
            dve.wait_ge(evac_a, p.val[-1])
            for l in range(3):
                for w in range(2):
                    for m in range(2):
                        s = modc[:, l, 48 * w + 8 * (1 + 3 * m):48 * w + 8 * (1 + 3 * m) + 8]
                        g = cols[:, R_G + 16 * l + 8 * m:R_G + 16 * l + 8 * m + 8]
                        nc.vector.scalar_tensor_tensor(Ac[:, l, w, m, :], s, 1.0, g, ALU.add, ALU.mult)

        N_COLS = 6 + 6 + 4 + 2 + 24

        def pool_params(pool):
            pool.dma_start(cst[:, :], I["cst"]).then_inc(params_in, 16)

            def row(at, src, k):
                pool.dma_start(rows[at:at + k, :], src).then_inc(cols_in, 16)

            flat = lambda a: a.rearrange("(k p) -> k p", p=P)
            row(0, flat(I["c"][0]), 8)
            row(8, flat(I["c_ctx"]), 8)
            row(16, flat(I["c_2"][0]), 8)
            row(24, flat(I["c_ctx_2"]), 8)
            row(32, flat(I["c_2"][0]), 8)
            row(40, flat(I["c_ctx_2"]), 8)
            row(48, flat(I["norm_mix_g"][0]), 8)
            row(56, flat(I["norm_ffn_g"][0]), 8)
            for l in range(2):
                row(64 + 16 * l, flat(I["g_norm1_2"][l]), 8)
                row(72 + 16 * l, flat(I["g_norm2_2"][l]), 8)
            for m in range(2):
                pool.dma_start(rows[R_NAQ:R_NAQ + 2, 64 * m:64 * m + 64], I["na_q_gain_2"]).then_inc(cols_in, 16)
                pool.dma_start(rows[R_NAK:R_NAK + 2, 64 * m:64 * m + 64], I["na_k_gain_2"]).then_inc(cols_in, 16)
            for l in range(2):
                row(R_BS + 4 * l, I["gm_b_s_2"][l], 4)
            for l in range(3):
                for j in range(4):
                    for w in range(2):
                        pool.dma_start(brow[32 * j + w:32 * j + w + 1, 1536 * l:1536 * l + 1536].rearrange("w (r n) -> w r n", r=3),
                                       BM[l].rearrange("(w r j n) -> w r j n", w=1, r=3, j=4)[:, :, j, :]).then_inc(cols_in, 16)

        junk = Z[:, 0:D]
        xn = [Z[:, D:2 * D], Z[:, 2 * D:3 * D]]

        def plan_norm(n, nt):
            return Plan(n, "av" * nt)

        def pe_norm(pe, n, nt, keep=None):
            p = plan_norm(n, nt)
            for t in range(nt):
                pe.wait_ge(xn_ok, n["xn"] + t + 1)
                src = xn[t % 2] if keep is None else keep(t)
                for h in range(2):
                    i = 2 * t + h
                    if i >= 4:
                        pe.wait_ge(EV[p.own[i - 4]], p.val[i - 4])
                    for k in range(4):
                        last = nc.tensor.transpose(bank(i % 4)[:, 128 * k:128 * k + 128],
                                                   src[:, 512 * h + 128 * k:512 * h + 128 * k + 128], ident)
                    last.then_inc(mm_done, 1)
            n["xn"] += nt

        def act_norm(act, n, nt, l, m):
            p = plan_norm(n, nt)
            n["xn"] += nt
            for t in range(nt):
                last = act.activation(junk, xl[:, t, :], ACT.Square, accum_out=st[:, t:t + 1])
                act.drain()
            last = act.activation(st[:, 16:16 + nt], st[:, 0:nt], ACT.Copy)
            last.then_inc(sumsq, 1)
            n["var"] += 1
            act.wait_ge(var, n["var"])
            act.activation(st[:, 24:24 + nt], st[:, 8:8 + nt], ACT.Sqrt).then_inc(std, 1)
            for t in range(nt):
                i = 2 * t
                act.wait_ge(mm_done, p.done(i))
                for k in range(4):
                    last = act.activation(hTk[:, k, 128 * t:128 * t + 128], bank(i % 4)[:, 128 * k:128 * k + 128], ACT.Identity,
                                          scale=Ac[:, l, t // TL, m, k:k + 1],
                                          bias=modc[:, l, 48 * (t // TL) + 24 * m + k:48 * (t // TL) + 24 * m + k + 1])
                last.then_inc(evac_a, 1)

        def dve_norm(dve, n, nt, l, m, keep=None):
            p = plan_norm(n, nt)
            n["ss"] += 1
            dve.wait_ge(sumsq, n["ss"])
            nc.vector.tensor_scalar(st[:, 8:8 + nt], st[:, 16:16 + nt], 1.0 / D, EPS, ALU.mult, ALU.add).then_inc(var, 1)
            n["std"] += 1
            dve.wait_ge(std, n["std"])
            nc.vector.reciprocal(st[:, 32:32 + nt], st[:, 24:24 + nt])
            dve.drain()
            for t in range(nt + 1):
                if t < nt:
                    if t >= 2 and keep is None:
                        dve.wait_ge(mm_done, p.done(2 * t - 3))
                    dst = xn[t % 2] if keep is None else keep(t)
                    nc.vector.tensor_scalar(dst, xl[:, t, :], st[:, 32 + t:33 + t], None, ALU.mult).then_inc(xn_ok, 1)
                if t >= 1:
                    u = t - 1
                    i = 2 * u + 1
                    dve.wait_ge(mm_done, p.done(i))
                    for k in range(4):
                        kk = 4 + k
                        c = 48 * (u // TL) + 24 * m + kk
                        last = nc.vector.tensor_scalar(hTk[:, kk, 128 * u:128 * u + 128], bank(i % 4)[:, 128 * k:128 * k + 128],
                                                       Ac[:, l, u // TL, m, kk:kk + 1], modc[:, l, c:c + 1], ALU.mult, ALU.add)
                    last.then_inc(evac_v, 1)

        def plan_lin(n, blocks, own="av"):
            g = "".join(b[3] * len(b[2]) if len(b) > 3 else "." * len(b[2]) for b in blocks)
            return Plan(n, "".join(own[i % 2] if o == "." else o for i, o in enumerate(g)))

        def sp_lin(sp, n, rel, w, blocks):
            p = plan_lin(n, blocks)
            i = 0
            for c0, c1, ts, *_ in blocks:
                c = n["chunk"]
                load_chunk(sp, n, lambda s: s[:, 0:w.shape[0] // P * (c1 - c0)].rearrange("p (k n) -> p k n", n=c1 - c0),
                           w[:, c0:c1].rearrange("(k p) n -> p k n", p=P), rel)
                i += len(ts)
                rel[c % 2] = p.done(i - 1)

        def pe_lin(pe, n, blocks, lhs):
            p = plan_lin(n, blocks)
            i = 0
            nk = lhs(None, None)
            for c0, c1, ts, *_ in blocks:
                s = take_chunk(pe, n)
                w = c1 - c0
                for t in ts:
                    if i >= 8:
                        pe.wait_ge(EV[p.own[i - 8]], p.val[i - 8])
                    for k in range(nk):
                        last = nc.tensor.matmul(bank(i % 8, w), lhs(k, t), s[:, k * w:k * w + w], start=(k == 0), stop=(k == nk - 1))
                    last.then_inc(mm_done, 1)
                    i += 1

        def each_lin(eng, n, blocks, who, put):
            p = plan_lin(n, blocks)
            i = 0
            for c0, c1, ts, *_ in blocks:
                for t in ts:
                    if p.own[i] == who:
                        eng.wait_ge(mm_done, p.done(i))
                        put(c0, c1, t, bank(i % 8, c1 - c0)).then_inc(EV[who], 1)
                    i += 1

        def h_lhs(k, t):
            return KT if k is None else hTk[:, k, 128 * t:128 * t + 128]

        ALLT, LAT = tuple(range(TA)), tuple(range(TL))
        BL1 = [(0, 512, LAT), (512, 1024, ALLT), (1024, 1536, ALLT), (1536, 2048, ALLT), (2048, 2560, ALLT),
               (2560, 3072, LAT), (3072, 3104, ALLT)]

        def act_put(c0, c1, t, b):
            return nc.scalar.activation(pjt[:, t, c0:c1], b, ACT.Copy)

        def dve_put(c0, c1, t, b):
            return nc.vector.tensor_copy(pjt[:, t, c0:c1], b)

        kT = [Z[:, 0:768], Z[:, 768:1536]]
        qT = [Z[:, 1536:2304], Z[:, 2304:3072]]
        EB = [[Z[:, 3072 + 1536 * u + 768 * m:3840 + 1536 * u + 768 * m] for m in range(2)] for u in range(2)]
        ET = [Z[:, 6144:6912], Z[:, 6912:7680]]
        TB = Z[:, 7680:9600]

        class Attn:

            def __init__(self, n, heads, units):
                self.heads, self.units = heads, units
                self.nm = 2 if units[0]["combine"] else 1
                self.preps = [(h, side, ts) for h, (_, _, qts, _) in enumerate(heads) for side in ("k", "q")
                              for ts in ((0, 1, 2, 3), (4, 5)) if side == "k" or set(ts) <= set(qts)]
                first = {}
                for i, u in enumerate(units):
                    first.setdefault(u["head"], i)
                self.at = {}
                seen = {}
                for j, (h, _, _) in enumerate(self.preps):
                    k = seen[h] = seen.get(h, -1) + 1
                    self.at.setdefault(-1 if h == 0 else first[h - 1] + k, []).append(j)
                c = lambda key, k=1: n.__setitem__(key, n.get(key, 0) + k) or n[key]
                self.s, self.e, self.mx, self.free, self.t, self.et, self.a, self.o, self.y = ([] for _ in range(9))
                for u in units:
                    for _ in range(self.nm):
                        self.s.append(c("s"))
                        self.mx.append(c("mx"))
                        self.e.append(c("e"))
                        self.free.append((s_free_v, c("sf")) if u["bias"] is not None else (e_ok, n["e"]))
                    full = len(u["keys"]) == 6
                    self.t.append((c("t"), c("t")) if full else (None, c("t")))
                    self.et.append((c("eta") if full else None, c("etv")))
                    self.a.append(c("acomb") if u["combine"] else None)
                    self.o.append(c("o"))
                    self.y.append(c("y"))
                self.pd, self.pe_ = [], []
                for j in range(len(self.preps)):
                    self.pd.append(c("pd"))
                    self.pe_.append((prep_a, c("pa")) if j % 2 == 0 else (prep_v, c("pv")))

        def pe_attn(pe, n, heads, units):
            A = Attn(n, heads, units)

            def prep(j):
                h, side, ts = A.preps[j]
                rows_, src, _, _ = heads[h]
                if j:
                    pe.wait_ge(*A.pe_[j - 1])
                for t in ts:
                    last = nc.tensor.transpose(bank(7)[0:rows_, 128 * (t - ts[0]):128 * (t - ts[0]) + 128], src(side, t), ident)
                last.then_inc(prep_done, 1)

            def scores(i):
                u = units[i]
                for j, (h, _, _) in enumerate(A.preps):
                    if h == u["head"]:
                        pe.wait_ge(*A.pe_[j])
                for m in range(A.nm):
                    g = A.nm * i + m
                    if g >= 2:
                        pe.wait_ge(*A.free[g - 2])
                    b = ps[:, 1024 * (g % 2):1024 * (g % 2) + 1024]
                    rs = slice(*u["rows"][m])
                    q = qT[u["head"] % 2][rs, 128 * u["qt"]:128 * u["qt"] + 128]
                    if len(u["keys"]) == 6:
                        nc.tensor.matmul(b[:, 0:512], q, kT[u["head"] % 2][rs, 0:512], start=True, stop=True)
                    nc.tensor.matmul(b[:, 512:768], q, kT[u["head"] % 2][rs, 512:768], start=True, stop=True).then_inc(s_done, 1)

            def transp(i):
                u = units[i]
                if u["combine"]:
                    pe.wait_ge(a_ok, A.a[i])
                else:
                    pe.wait_ge(e_ok, A.e[i])
                E = EB[i % 2][0]
                if len(u["keys"]) == 6:
                    prev = [x[0] for x in A.et[:i] if x[0] is not None]
                    if prev:
                        pe.wait_ge(et_a, prev[-1])
                    for t in range(4):
                        last = nc.tensor.transpose(bank(4)[:, 128 * t:128 * t + 128], E[:, 128 * t:128 * t + 128], ident)
                    last.then_inc(t_done, 1)
                if i:
                    pe.wait_ge(et_v, A.et[i - 1][1])
                for t in (4, 5):
                    last = nc.tensor.transpose(bank(5)[:, 128 * (t - 4):128 * (t - 4) + 128], E[:, 128 * t:128 * t + 128], ident)
                last.then_inc(t_done, 1)

            def values(i):
                u = units[i]
                if A.et[i][0] is not None:
                    pe.wait_ge(et_a, A.et[i][0])
                pe.wait_ge(et_v, A.et[i][1])
                if i:
                    pe.wait_ge(y_ok, A.y[i - 1])
                for t in u["keys"]:
                    last = nc.tensor.matmul(bank(6, u["dv"]), ET[i % 2][:, 128 * t:128 * t + 128], u["v"](t),
                                            start=(t == u["keys"][0]), stop=(t == u["keys"][-1]))
                last.then_inc(o_done, 1)

            for j in A.at.get(-1, []):
                prep(j)
            for i in range(len(units) + 2):
                if i < len(units):
                    scores(i)
                for j in A.at.get(i, []):
                    prep(j)
                if 0 <= i - 1 < len(units):
                    transp(i - 1)
                if i >= 2:
                    values(i - 2)

        def prep_out(eng, A, j, who):
            h, side, ts = A.preps[j]
            if A.pe_[j][0] is not (prep_a if who == "a" else prep_v):
                return
            rows_, _, _, gain = A.heads[h]
            eng.wait_ge(prep_done, A.pd[j])
            dst = (kT if side == "k" else qT)[h % 2][0:rows_, 128 * ts[0]:128 * ts[-1] + 128]
            src = bank(7, 128 * len(ts))[0:rows_, :]
            if who == "a":
                g = {} if gain is None else {"scale": gain(side)}
                nc.scalar.activation(dst, src, ACT.Copy, **g).then_inc(prep_a, 1)
            elif gain is None:
                nc.vector.tensor_copy(dst, src).then_inc(prep_v, 1)
            else:
                nc.vector.tensor_scalar(dst, src, gain(side), None, ALU.mult).then_inc(prep_v, 1)

        def stat(i, k):
            at = 100 + 8 * (i % 4) + k
            return st[:, at:at + 1]

        def act_attn(act, n, heads, units):
            A = Attn(n, heads, units)

            def exps(i):
                u = units[i]
                k0 = 128 * u["keys"][0]
                for m in range(A.nm):
                    g = A.nm * i + m
                    if i >= 2:
                        act.wait_ge(t_done, A.t[i - 2][1])
                    act.wait_ge(mx_ok, A.mx[g])
                    E = EB[i % 2][m][:, k0:768]
                    src = E if u["bias"] is not None else ps[:, 1024 * (g % 2) + k0:1024 * (g % 2) + 768]
                    act.activation(E, src, ACT.Exp, bias=stat(i, m), scale=1.0 if u["bias"] is not None else u["scale"],
                                   accum_out=stat(i, 2 + m)).then_inc(e_ok, 1)

            def et(i):
                if A.et[i][0] is None:
                    return
                act.wait_ge(t_done, A.t[i][0])
                if i >= 2:
                    act.wait_ge(o_done, A.o[i - 2])
                act.activation(ET[i % 2][:, 0:512], bank(4), ACT.Copy).then_inc(et_a, 1)

            for j in A.at.get(-1, []):
                prep_out(act, A, j, "a")
            for i in range(len(units) + 1):
                if i < len(units):
                    exps(i)
                for j in A.at.get(i, []):
                    prep_out(act, A, j, "a")
                if i >= 1:
                    et(i - 1)

        def dve_attn(dve, n, heads, units, lam=None, tables=None):
            A = Attn(n, heads, units)

            def maxima(i):
                u = units[i]
                k0 = 128 * u["keys"][0]
                for m in range(A.nm):
                    g = A.nm * i + m
                    dve.wait_ge(s_done, A.s[g])
                    src = ps[:, 1024 * (g % 2) + k0:1024 * (g % 2) + 768]
                    if u["bias"] is not None:
                        if i >= 2:
                            dve.wait_ge(t_done, A.t[i - 2][1])
                        E = EB[i % 2][m]
                        dve.wait_ge(tb_ok, tables + u["head"] + 1)
                        u["bias"](E, ps[:, 1024 * (g % 2):1024 * (g % 2) + 768]).then_inc(s_free_v, 1)
                        dve.drain()
                        src = E[:, k0:768]
                    nc.vector.reduce_max(stat(i, 6 + m), src, AX)
                    dve.drain()
                    nc.vector.tensor_scalar(stat(i, m), stat(i, 6 + m), -1.0 if u["bias"] is not None else -u["scale"],
                                            None, ALU.mult).then_inc(mx_ok, 1)

            def norms(i):
                u = units[i]
                dve.wait_ge(e_ok, A.e[A.nm * i + A.nm - 1])
                nc.vector.reciprocal(st[:, 100 + 8 * (i % 4) + 4:100 + 8 * (i % 4) + 4 + A.nm],
                                     st[:, 100 + 8 * (i % 4) + 2:100 + 8 * (i % 4) + 2 + A.nm])
                if u["combine"]:
                    dve.drain()
                    E0, E1 = EB[i % 2]
                    nc.vector.tensor_scalar(E1, E1, stat(i, 5), lam, ALU.mult, ALU.mult)
                    dve.drain()
                    nc.vector.scalar_tensor_tensor(E0, E0, stat(i, 4), E1, ALU.mult, ALU.subtract).then_inc(a_ok, 1)

            def et(i):
                dve.wait_ge(t_done, A.t[i][1])
                if i >= 2:
                    dve.wait_ge(o_done, A.o[i - 2])
                nc.vector.tensor_copy(ET[i % 2][:, 512:768], bank(5, 256)).then_inc(et_v, 1)

            def outs(i):
                u = units[i]
                dve.wait_ge(o_done, A.o[i])
                if u["combine"]:
                    nc.vector.tensor_copy(u["y"], bank(6, u["dv"])).then_inc(y_ok, 1)
                else:
                    nc.vector.tensor_scalar(u["y"], bank(6, u["dv"]), stat(i, 4), None, ALU.mult).then_inc(y_ok, 1)

            for j in A.at.get(-1, []):
                prep_out(dve, A, j, "v")
            for i in range(len(units) + 2):
                if i < len(units):
                    maxima(i)
                for j in A.at.get(i, []):
                    prep_out(dve, A, j, "v")
                if 0 <= i - 1 < len(units):
                    norms(i - 1)
                    et(i - 1)
                if i >= 2:
                    outs(i - 2)
                if tables is not None and i < len(units) and (i + 1 == len(units) or units[i + 1]["head"] != units[i]["head"]):
                    dve.drain().then_inc(tb_free, 1)

        def da_spec():
            def src(h):
                return lambda side, t: pjt[:, t, (DK if side == "k" else DQ) + 128 * h:(DK if side == "k" else DQ) + 128 * h + 128]
            heads = [(P, src(h), LAT, None) for h in range(4)]
            units = [dict(head=h, rows=((0, 64), (64, 128)), qt=t, keys=ALLT, bias=None, scale=64 ** -0.5, combine=True,
                          v=lambda kt, h=h: pjt[:, kt, DV + 128 * h:DV + 128 * h + 128], dv=128,
                          y=pjt[:, t, DQ + 128 * h:DQ + 128 * h + 128]) for h in range(4) for t in LAT]
            return heads, units

        def dve_rope(dve, t, v, g, f, cc, cs, A_, B_):
            cosb = C(cc + 4 * f * t, 4 * f).unsqueeze(1).broadcast_to([P, g, 4 * f])
            sin4 = C(cs + 4 * f * t, 4 * f).rearrange("p (a s f) -> p a s f", a=2, s=2)
            v5 = v.rearrange("p g (a s f) -> p g a s f", a=2, s=2)
            A3, B5 = A_.rearrange("p (g n) -> p g n", g=g), B_.rearrange("p (g a s f) -> p g a s f", g=g, a=2, s=2)
            nc.vector.tensor_tensor(A3, v, cosb, ALU.mult)
            for s in range(2):
                nc.vector.tensor_tensor(B5[:, :, :, s, :], v5[:, :, :, 1 - s, :],
                                        sin4[:, :, s, :].unsqueeze(1).broadcast_to([P, g, 2, f]), ALU.mult)
            dve.drain()
            nc.vector.tensor_tensor(v, A3, B_.rearrange("p (g n) -> p g n", g=g), ALU.add)

        lamt, lam = Z[:, 9600:9856], st[:, 180:181]
        subln, glag = Z[:, 9856:9984], Z[:, 9984:10112]
        w2a = Z[:, 10112:10624]

        def rms_heads(eng, who, n, tiles, view, H, dh, gain, mul=1.0):
            nt = len(tiles)
            ss = st[:, 200:200 + nt * H]
            vv = st[:, 260:260 + nt * H]
            sd = st[:, 320:320 + nt * H]
            rr = st[:, 380:380 + nt * H]
            sq = [Z[:, 0:H * dh], Z[:, 1024:1024 + H * dh]]
            if who == "v":
                for i, t in enumerate(tiles):
                    v = view(t)
                    s3 = sq[i % 2].rearrange("p (h d) -> p h d", h=H)
                    nc.vector.tensor_tensor(s3, v, v, ALU.mult)
                    eng.drain()
                    nc.vector.tensor_reduce(ss[:, H * i:H * i + H], s3, AX, ALU.add)
                eng.drain()
                nc.vector.tensor_scalar(vv, ss, 1.0 / dh, EPS, ALU.mult, ALU.add).then_inc(var, 1)
                n["std"] += 1
                eng.wait_ge(std, n["std"])
                nc.vector.reciprocal(rr, sd)
                eng.drain()
                if mul != 1.0:
                    nc.vector.tensor_scalar(rr, rr, mul, None, ALU.mult)
                    eng.drain()
                for i, t in enumerate(tiles):
                    v = view(t)
                    nc.vector.tensor_tensor(v, v, rr[:, H * i:H * i + H].unsqueeze(2).broadcast_to([P, H, dh]), ALU.mult)
                if gain is not None:
                    eng.drain()
                    for i, t in enumerate(tiles):
                        v = view(t)
                        nc.vector.tensor_tensor(v, v, gain.unsqueeze(1).broadcast_to([P, H, dh]), ALU.mult)
            else:
                n["var"] += 1
                eng.wait_ge(var, n["var"])
                eng.activation(sd, vv, ACT.Sqrt).then_inc(std, 1)

        def hv(c0, H, dh):
            return lambda t: pjt[:, t, c0:c0 + H * dh].rearrange("p (h d) -> p h d", h=H)

        def dve_da_before(dve):
            dve.wait_ge(prm, 16 * 7)
            for t in LAT:
                dve_rope(dve, t, hv(DQ, 16, 64)(t), 16, 16, C_R1C, C_R1S, Z[:, 2048 * (t % 2):2048 * (t % 2) + 1024],
                         Z[:, 2048 * (t % 2) + 1024:2048 * (t % 2) + 2048])
            l4 = lamt.rearrange("p (a b d) -> p a b d", a=2, b=2)
            pr = Z[:, 9000:9128].rearrange("p (a d) -> p a d", a=2)
            nc.vector.tensor_tensor(pr, l4[:, :, 0, :], l4[:, :, 1, :], ALU.mult)
            dve.drain()
            nc.vector.tensor_reduce(st[:, 182:184], pr, AX, ALU.add).then_inc(v2a, 1)

        def act_lambda(act, n):
            n["v2a"] += 1
            act.wait_ge(v2a, n["v2a"])
            act.activation(st[:, 184:186], st[:, 182:184], ACT.Exp).then_inc(a2v, 1)

        def dve_lambda(dve, n):
            n["a2v"] += 1
            dve.wait_ge(a2v, n["a2v"])
            nc.vector.scalar_tensor_tensor(lam, st[:, 184:185], 0.8 - 0.6 * math.exp(-0.0), st[:, 185:186], ALU.add, ALU.subtract)
            dve.drain()

        Gg = Z[:, 0:3072].rearrange("p (t n) -> p t n", t=TA)
        zc = Z[:, 3072:6144].rearrange("p (t n) -> p t n", t=TA)
        sp_ = Z[:, 6144:9216].rearrange("p (t n) -> p t n", t=TA)
        lrT = hT[0:32, 0:1536].rearrange("p (t n) -> p t n", t=TA)
        qdT = hT[:, 1536:3584].rearrange("p (t n) -> p t n", t=TL)
        kiT = hT[:, 3584:5632].rearrange("p (t n) -> p t n", t=TL)
        ex = [[Z[:, 3072 + 1536 * i + 512 * j:3584 + 1536 * i + 512 * j] for j in range(3)] for i in range(2)]
        qk = [Z[:, 6144 + 1024 * i:7168 + 1024 * i] for i in range(2)]
        DD = Z[:, 0:6144].rearrange("p (c d q n) -> p c d q n", c=12, d=2, q=2)
        SM = [[Z[:, 6144 + 1024 * i + 512 * d:6656 + 1024 * i + 512 * d] for d in range(2)] for i in range(2)]
        dec = st[:, 440:488]
        FWD = [8, 9, 10, 11] + list(range(8))
        BWD = [11, 10, 9, 8] + list(range(7, -1, -1))
        TRI = (C_TF, C_TB)
        AFTER = (C_TA, C_TZ)

        def plan_gate(n):
            return Plan(n, "a" * (2 * TA))

        def pe_gates(pe, n):
            p = plan_gate(n)
            n["v2p"] += 1
            pe.wait_ge(v2p, n["v2p"])
            for i in range(2 * TA):
                t = i % TA
                if i >= 4:
                    pe.wait_ge(evac_a, p.val[i - 4])
                if i < TA:
                    for d in range(2):
                        last = nc.tensor.transpose(bank(i % 4)[0:16, 128 * d:128 * d + 128], pjt[:, t, LRF + 16 * d:LRF + 16 * d + 16], ident)
                else:
                    pe.wait_ge(evac_a, p.val[t])
                    for d in range(2):
                        last = nc.tensor.matmul(bank(i % 4)[:, 256 * d:256 * d + 256], lrT[0:17, t, 128 * d:128 * d + 128],
                                                w2a[0:17, 256 * d:256 * d + 256], start=True, stop=True)
                last.then_inc(mm_done, 1)

        def act_gates(act, n):
            p = plan_gate(n)
            n["v2a"] += 1
            act.wait_ge(v2a, n["v2a"])
            for i in range(2 * TA):
                t = i % TA
                act.wait_ge(mm_done, p.done(i))
                if i < TA:
                    act.activation(lrT[0:16, t, :], bank(i % 4)[0:16, 0:256], ACT.Copy).then_inc(evac_a, 1)
                else:
                    act.activation(zc[:, t, :], bank(i % 4), ACT.Copy).then_inc(evac_a, 1)
            act.drain()
            act.activation(sp_, zc, ACT.Abs)
            act.drain()
            act.activation(sp_, sp_, ACT.Exp, scale=-1.0)
            act.drain()
            act.activation(sp_, sp_, ACT.Ln, bias=1.0).then_inc(a2v, 1)

        def dve_gates(dve, n):
            plan_gate(n)
            nc.vector.memset(hT[0:32, 0:1536], 1.0).then_inc(v2p, 1)
            nc.vector.memset(st[0:1, 599:600], 0.0).then_inc(v2a, 1)
            n["a2v"] += 1
            dve.wait_ge(a2v, n["a2v"])
            nc.vector.scalar_tensor_tensor(Gg, zc, 0.0, sp_, ALU.min, ALU.subtract)

        def plan_dec(n):
            return Plan(n, "aa" * TA + "va" * TL + "a")

        def pe_dec(pe, n):
            p = plan_dec(n)
            for t in range(TA):
                for j, tri in enumerate((TRI, AFTER)):
                    i = 2 * t + j
                    if t >= 2:
                        pe.wait_ge(evac_a, dec_s(p, t - 2, j))
                    for d in range(2):
                        last = nc.tensor.matmul(bank(i % 4)[:, 256 * d:256 * d + 256], C(tri[d]), Gg[:, t, 256 * d:256 * d + 256],
                                                start=True, stop=True)
                    last.then_inc(mm_done, 1)
                if 1 <= t <= TL:
                    turn_dec(pe, n, p, t - 1)
            for t in range(TA):
                for d in range(2):
                    for q in range(2):
                        k = 8 * t + 4 * d + 2 * q
                        last = nc.tensor.matmul(bank(6)[:, k:k + 2], Gg[:, t, 256 * d + 128 * q:256 * d + 128 * q + 128], C(C_CH, 2),
                                                start=True, stop=True)
            last.then_inc(mm_done, 1)

        def dec_order():
            o = []
            for t in range(TA):
                o += [("s", t, 0), ("s", t, 1)]
                if 1 <= t <= TL:
                    o += [("t", t - 1, 0), ("t", t - 1, 1)]
            return {k: i for i, k in enumerate(o)}

        DECO = dec_order()

        def turn_dec(pe, n, p, t):
            n["v2p"] += 1
            pe.wait_ge(v2p, n["v2p"])
            for j in range(2):
                if t >= 1:
                    pe.wait_ge(*((evac_v, p.val[2 * TA + 2 * (t - 1)]) if j == 0 else (evac_a, dec_a(p, t - 1))))
                for x in range(4):
                    last = nc.tensor.transpose(bank(4 + j)[:, 128 * x:128 * x + 128], qk[t % 2][:, 512 * j + 128 * x:512 * j + 128 * x + 128], ident)
                last.then_inc(mm_done, 1)

        def dec_a(p, t):
            k = DECO[("t", t, 1)]
            return p.val[0] - 1 + sum(1 for x, i in DECO.items() if i <= k and (x[0] == "s" or x[2] == 1))

        def dec_s(p, t, j):
            k = DECO[("s", t, j)]
            return p.val[0] - 1 + sum(1 for x, i in DECO.items() if i <= k and (x[0] == "s" or x[2] == 1))

        def act_dec(act, n):
            p = plan_dec(n)
            for (kind, t, j), i in DECO.items():
                act_need = kind == "s" or j == 1
                if not act_need:
                    continue
                act.wait_ge(mm_done, p.done(i))
                if kind == "t":
                    act.activation(kiT[:, t, :], bank(5), ACT.Copy).then_inc(evac_a, 1)
                elif j == 0:
                    if t >= 2:
                        act.wait_ge(ex_used, t - 1)
                    act.activation(ex[t % 2][0], bank((2 * t) % 4), ACT.Exp, scale=1 / 16)
                    act.activation(ex[t % 2][1], bank((2 * t) % 4), ACT.Exp, scale=-1 / 16).then_inc(evac_a, 1)
                else:
                    act.activation(ex[t % 2][2], bank((2 * t + 1) % 4), ACT.Exp, scale=1 / 16).then_inc(evac_a, 1)
            act.wait_ge(mm_done, p.done(len(DECO)))
            act.activation(dec, bank(6, 48), ACT.Exp, scale=1 / 16).then_inc(evac_a, 1)

        def dve_dec(dve, n):
            p = plan_dec(n)
            for t in range(TA):
                dve.wait_ge(evac_a, dec_s(p, t, 1))
                k2 = pjt[:, t, GK:GK + 256].unsqueeze(1).broadcast_to([P, 2, 256])
                q2 = pjt[:, t, GQ:GQ + 256].unsqueeze(1).broadcast_to([P, 2, 256])
                e3 = [e.rearrange("p (d n) -> p d n", d=2) for e in ex[t % 2]]
                if t < TL:
                    if t >= 2:
                        dve.wait_ge(mm_done, p.done(DECO[("t", t - 2, 1)]))
                    a = qk[t % 2].rearrange("p (j d n) -> p j d n", j=2, d=2)
                    nc.vector.scalar_tensor_tensor(a[:, 0], q2, 64 ** -0.5, e3[0], ALU.mult, ALU.mult)
                    nc.vector.tensor_tensor(a[:, 1], k2, e3[1], ALU.mult).then_inc(v2p, 1)
                nc.vector.tensor_tensor(pjt[:, t, DK:DK + 512].rearrange("p (d n) -> p d n", d=2), k2, e3[2], ALU.mult).then_inc(ex_used, 1)
                if 1 <= t <= TL:
                    dve.wait_ge(mm_done, p.done(DECO[("t", t - 1, 0)]))
                    nc.vector.tensor_copy(qdT[:, t - 1, :], bank(4)).then_inc(evac_v, 1)

        def plan_st(n):
            return Plan(n, "av" * 6)

        def pe_states(pe, n):
            p = plan_st(n)
            for ci in range(12):
                t, c = ci // 2, ci % 2
                if ci >= 8:
                    pe.wait_ge(EV[p.own[ci - 8]], p.val[ci - 8])
                rs = slice(64 * c, 64 * c + 64)
                for d in range(2):
                    for h in range(4):
                        last = nc.tensor.matmul(bank(ci % 8)[64 * (h % 2):64 * (h % 2) + 64, 256 * d + 128 * (h // 2):256 * d + 128 * (h // 2) + 128],
                                                pjt[rs, t, DK + 256 * d + 64 * h:DK + 256 * d + 64 * h + 64],
                                                pjt[rs, t, GV + 128 * h:GV + 128 * h + 128], start=True, stop=True)
                last.then_inc(mm_done, 1)

        def each_states(eng, n, who):
            p = plan_st(n)
            for ci in range(12):
                if p.own[ci] == who:
                    eng.wait_ge(mm_done, p.done(ci))
                    dst = Z[:, 512 * ci:512 * ci + 512]
                    if who == "a":
                        nc.scalar.activation(dst, bank(ci % 8), ACT.Copy).then_inc(evac_a, 1)
                    else:
                        nc.vector.tensor_copy(dst, bank(ci % 8)).then_inc(evac_v, 1)
            if who == "v":
                eng.wait_ge(evac_a, p.val[10])
                eng.drain()
                for s in range(1, 12):
                    for d, order in enumerate((FWD, BWD)):
                        a, b = order[s - 1], order[s]
                        for q in range(2):
                            k = 8 * (b // 2) + 4 * d + 2 * q + b % 2
                            nc.vector.scalar_tensor_tensor(DD[:, b, d, q, :], DD[:, a, d, q, :], dec[:, k:k + 1], DD[:, b, d, q, :],
                                                           ALU.mult, ALU.add)
                    eng.drain()

        def plan_o(n):
            return Plan(n, "vvvvaa" * TL)

        def pe_glao(pe, n):
            p = plan_o(n)
            for t in range(TL):
                for g in range(4):
                    d, par = g // 2, g % 2
                    rs = slice(64 * par, 64 * par + 64)
                    if t:
                        pe.wait_ge(evac_v, p.val[6 * (t - 1) + g])
                    for q in range(2):
                        x = 256 * d + 128 * q
                        last = nc.tensor.matmul(bank(g)[:, 128 * q:128 * q + 128], kiT[rs, t, x:x + 128], qdT[rs, t, x:x + 128],
                                                start=True, stop=True)
                    last.then_inc(mm_done, 1)
                for par in range(2):
                    rs = slice(64 * par, 64 * par + 64)
                    pe.wait_ge(evac_v, p.val[6 * t + 2 + par])
                    if t >= 2:
                        pe.wait_ge(evac_a, p.val[6 * (t - 2) + 4 + par])
                    for q in range(2):
                        h = 2 * q + par
                        o = bank(4 + 2 * (t % 2) + par)[:, 128 * q:128 * q + 128]
                        for d in range(2):
                            nc.tensor.matmul(o, SM[t % 2][d][:, 128 * h:128 * h + 128], pjt[:, t, GV + 128 * h:GV + 128 * h + 128],
                                             start=(d == 0), stop=False)
                        for d, order in enumerate((FWD, BWD)):
                            for c in range(2):
                                prev = order[order.index(2 * t + c) - 1]
                                x = 256 * d + 128 * q
                                last = nc.tensor.matmul(o[64 * c:64 * c + 64, :], qdT[rs, t, x + 64 * c:x + 64 * c + 64], DD[rs, prev, d, q, :],
                                                        start=False, stop=(d == 1))
                    last.then_inc(mm_done, 1)

        def dve_glao(dve, n):
            p = plan_o(n)
            for t in range(TL):
                if t >= 2:
                    dve.wait_ge(mm_done, p.done(6 * (t - 2) + 5))
                for g in range(4):
                    d, par = g // 2, g % 2
                    dve.wait_ge(mm_done, p.done(6 * t + g))
                    m = C(TRI[d]).unsqueeze(1).broadcast_to([P, 2, P])
                    nc.vector.tensor_tensor(SM[t % 2][d].rearrange("p (q a n) -> p a q n", q=2, a=2)[:, par],
                                            bank(g, 256).rearrange("p (q n) -> p q n", q=2), m, ALU.mult).then_inc(evac_v, 1)
            dve.wait_ge(evac_a, p.val[6 * (TL - 1) + 5])
            rms_heads(dve, "v", n, LAT, hv(DK, 4, 128), 4, 128, glag)
            dve.drain()
            n["a2v"] += 1
            dve.wait_ge(a2v, n["a2v"])
            for t in LAT:
                nc.vector.tensor_tensor(pjt[:, t, DK:DK + 512], pjt[:, t, DK:DK + 512], pjt[:, t, GR:GR + 512], ALU.mult)

        def act_glao(act, n):
            p = plan_o(n)
            for t in range(TL):
                for par in range(2):
                    act.wait_ge(mm_done, p.done(6 * t + 4 + par))
                    act.activation(pjt[:, t, DK:DK + 512].rearrange("p (q a n) -> p a q n", q=2, a=2)[:, par],
                                   bank(4 + 2 * (t % 2) + par, 256).rearrange("p (q n) -> p q n", q=2), ACT.Copy).then_inc(evac_a, 1)
            rms_heads(act, "a", n, LAT, hv(DK, 4, 128), 4, 128, glag)
            act.activation(pjt[:, 0:TL, GR:GR + 512], pjt[:, 0:TL, GR:GR + 512], ACT.Silu).then_inc(a2v, 1)

        def plan_turn(n, nk, tiles):
            return Plan(n, "av" * (nk * len(tiles) // 8) if (nk * len(tiles)) % 8 == 0 else "a" * (nk * len(tiles) // 4))

        def pe_turn(pe, n, nk, tiles, src):
            p = plan_turn(n, nk, tiles)
            i = 0
            for t in tiles:
                for k0 in range(0, nk, 4):
                    if i >= 8:
                        pe.wait_ge(EV[p.own[i - 8]], p.val[i - 8])
                    for k in range(4):
                        last = nc.tensor.transpose(bank(i % 8)[:, 128 * k:128 * k + 128], src(k0 + k, t), ident)
                    last.then_inc(mm_done, 1)
                    i += 1

        def each_turn(eng, n, who, nk, tiles, dst):
            p = plan_turn(n, nk, tiles)
            i = 0
            for t in tiles:
                for k0 in range(0, nk, 4):
                    if p.own[i] == who:
                        eng.wait_ge(mm_done, p.done(i))
                        b = bank(i % 8).rearrange("p (k n) -> p k n", k=4)
                        if who == "a":
                            nc.scalar.activation(dst(k0, t), b, ACT.Copy).then_inc(evac_a, 1)
                        else:
                            nc.vector.tensor_copy(dst(k0, t), b).then_inc(evac_v, 1)
                    i += 1

        def hT_dst(k0, t):
            return hTk[:, k0:k0 + 4, 128 * t:128 * t + 128]

        gtb = Z[:, 8192:10240].rearrange("p (w n) -> p w n", w=2)

        def load_gate(eng, l, s):
            for w in range(2):
                eng.dma_start(gtb[:, w, :], modd[l, w, D * s:D * s + D].partition_broadcast(P)).then_inc(gate_in, 16)

        def dve_resid(dve, n, blocks):
            p = plan_lin(n, blocks)
            i = 0
            tmp = [Z[:, 7168:7680], Z[:, 7680:8192]]
            n["gate"] = n.get("gate", 0) + 32
            dve.wait_ge(gate_in, n["gate"])
            for c0, c1, ts, *_ in blocks:
                for t in ts:
                    dve.wait_ge(mm_done, p.done(i))
                    nc.vector.tensor_tensor(tmp[i % 2], bank(i % 8), gtb[:, t // TL, c0:c1], ALU.mult).then_inc(evac_v, 1)
                    dve.drain()
                    nc.vector.tensor_tensor(xl[:, t, c0:c1], xl[:, t, c0:c1], tmp[i % 2], ALU.add)
                    i += 1

        XK = lambda t: Z[:, 1024 + 1024 * t:2048 + 1024 * t]
        rw = Z[:, 5200:5488].rearrange("p (k n) -> p k n", k=KT)
        rb = Z[:, 5488:5524]

        def rt(i, w=32):
            return Z[:, 5600 + 128 * i:5600 + 128 * i + TL * w].rearrange("p (t n) -> p t n", t=TL)

        LG = Z[:, 7400:7400 + 36 * TL].rearrange("p (t n) -> p t n", t=TL)
        sc = lambda i: Z[:, 7600 + TL * i:7600 + TL * i + TL]
        WT = [Z[:, 7700:7704], Z[:, 7704:7708]]
        IDX = Z[:, 7712:7720].bitcast(I32).rearrange("p (c t) -> p c t", c=2)
        TOK = Z[:, 7720:7724].bitcast(I32)
        ROWS = Z[:, 7724:7748].bitcast(I32)
        IDC = Z[:, 7748:7749].bitcast(I32)
        ZERO = Z[:, 7750:7774].bitcast(I32)
        EID = Z[0:1, 7780:7828].bitcast(I32)
        NIT = Z[0:1, 7828:7829].bitcast(I32)

        def pool_route_params(pool):
            pool.dma_start(rw[:, :, 0:NG], I["router_group_w"][0].rearrange("(k p) n -> p k n", p=P)).then_inc(rparams, 16)
            pool.dma_start(rw[:, :, NG:NG + NE], I["router_expert_w"][0].rearrange("(k p) n -> p k n", p=P)).then_inc(rparams, 16)
            pool.dma_start(rb[:, 0:NG], I["router_group_b"][0].partition_broadcast(P)).then_inc(rparams, 16)
            pool.dma_start(rb[:, NG:NG + NE], I["router_expert_b"][0].partition_broadcast(P)).then_inc(rparams, 16)
            pool.memset(ZERO, 0).then_inc(zero_ok, 1)
            pool.wait_ge(zero_ok, 2)
            pool.dma_start(rowtok.rearrange("(c p) a -> p (c a)", c=24), ZERO, allow_slow_non_contiguous=True).then_inc(rowz, 16)

        def plan_route(n):
            return Plan(n, "vvv")

        def pe_route(pe, n):
            p = plan_route(n)
            pe.wait_ge(rparams, 64)
            for t in range(TL):
                for k in range(KT):
                    last = nc.tensor.matmul(bank(0)[:, 36 * t:36 * t + 36], hTk[:, k, 128 * t:128 * t + 128], rw[:, k, :],
                                            start=(k == 0), stop=(k == KT - 1))
            last.then_inc(mm_done, 1)
            n["v2p"] += 1
            pe.wait_ge(v2p, n["v2p"])
            oh = rt(2)
            for t in range(TL):
                for u in range(t + 1):
                    last = nc.tensor.matmul(bank(1)[:, 32 * t:32 * t + 32], C(C_US) if u == t else C(C_ONE), oh[:, u, :],
                                            start=(u == 0), stop=(u == t))
            last.then_inc(mm_done, 1)
            for u in range(TL):
                last = nc.tensor.matmul(bank(2)[:, 0:32], C(C_ONE), oh[:, u, :], start=(u == 0), stop=(u == TL - 1))
            last.then_inc(mm_done, 1)

        def act_route(act, n):
            plan_route(n)
            for src, dst in ((LG[:, :, 0:NG], rt(6, NG)), (sc(5), sc(6))):
                n["v2a"] += 1
                act.wait_ge(v2a, n["v2a"])
                act.activation(dst, src, ACT.Exp).then_inc(a2v, 1)

        def dve_route(dve, n):
            p = plan_route(n)
            V = nc.vector
            D_ = dve.drain

            def bc(a, w):
                return a.unsqueeze(2).broadcast_to([P, TL, w])

            def first(dst, src, mx, w):
                V.tensor_reduce(mx, src, AX, ALU.max)
                D_()
                V.tensor_tensor(rt(7, w), src, bc(mx, w), ALU.is_equal)
                D_()
                V.tensor_tensor(rt(8, w), rt(7, w), C(C_I32 + 32 - w, w).unsqueeze(1).broadcast_to([P, TL, w]), ALU.mult)
                D_()
                V.tensor_reduce(sc(9), rt(8, w), AX, ALU.max)
                D_()
                V.tensor_tensor(dst, rt(8, w), bc(sc(9), w), ALU.is_equal)
                D_()

            V.tensor_copy(TOK, C(C_TK, TL))
            dve.wait_ge(rparams, 64)
            dve.wait_ge(mm_done, p.done(0))
            V.tensor_tensor(LG, bank(0)[:, 0:36 * TL].rearrange("p (t n) -> p t n", t=TL), rb.unsqueeze(1).broadcast_to([P, TL, 36]),
                            ALU.add).then_inc(evac_v, 1)
            D_()
            g, e = LG[:, :, 0:NG], LG[:, :, NG:NG + NE]
            ohg, em, oh1, oh2, oh = rt(9, NG), rt(3), rt(0), rt(1), rt(2)
            first(ohg, g, sc(0), NG)
            V.tensor_tensor(g, g, bc(sc(0), NG), ALU.subtract).then_inc(v2a, 1)
            n["a2v"] += 1
            dve.wait_ge(a2v, n["a2v"])
            V.tensor_reduce(sc(1), rt(6, NG), AX, ALU.add)
            D_()
            V.reciprocal(sc(2), sc(1))
            V.tensor_scalar(rt(10, NG), ohg, -1.0, -NEG, ALU.add, ALU.mult)
            v4 = lambda a: a.rearrange("p t (g x) -> p (t g) x", g=NG)
            b4 = lambda a: a.rearrange("p t g -> p (t g)").unsqueeze(2).broadcast_to([P, TL * NG, 8])
            for t in range(TL):
                V.tensor_tensor(em[:, t, :].rearrange("p (g x) -> p g x", g=NG), e[:, t, :].rearrange("p (g x) -> p g x", g=NG),
                                ohg[:, t, :].unsqueeze(2).broadcast_to([P, NG, 8]), ALU.mult)
            D_()
            V.tensor_tensor(v4(em), v4(em), b4(rt(10, NG)), ALU.add)
            D_()
            first(oh1, em, sc(3), 32)
            V.scalar_tensor_tensor(em, oh1, 2 * NEG, em, ALU.mult, ALU.add)
            D_()
            first(oh2, em, sc(4), 32)
            V.tensor_tensor(oh, oh1, oh2, ALU.add).then_inc(v2p, 1)
            V.tensor_tensor(sc(5), sc(4), sc(3), ALU.subtract).then_inc(v2a, 1)
            n["a2v"] += 1
            dve.wait_ge(a2v, n["a2v"])
            V.tensor_scalar(sc(7), sc(6), 1.0, None, ALU.add)
            D_()
            V.reciprocal(sc(8), sc(7))
            D_()
            V.tensor_tensor(WT[0], sc(8), sc(2), ALU.mult)
            D_()
            V.tensor_tensor(WT[1], WT[0], sc(6), ALU.mult)
            cnt, ov, oe, A_ = (Z[:, 7900 + 32 * i:7932 + 32 * i] for i in range(4))
            pos, gq, slot = rt(4), rt(5), rt(6)
            dve.wait_ge(mm_done, p.done(2))
            V.tensor_copy(pos, bank(1)[:, 0:128].rearrange("p (t n) -> p t n", t=TL)).then_inc(evac_v, 1)
            V.tensor_copy(cnt, bank(2)[:, 0:32]).then_inc(evac_v, 1)
            D_()
            V.tensor_scalar(ov, cnt, float(CAP), None, ALU.is_gt)
            for k in range(2, TL * P // CAP):
                D_()
                V.scalar_tensor_tensor(ov, cnt, float(CAP * k), ov, ALU.is_gt, ALU.add)
            D_()
            V.tensor_tensor_scan(oe, C(C_ONE, 32), ov, 0.0, ALU.mult, ALU.add)
            D_()
            V.tensor_tensor(A_, oe, ov, ALU.subtract)
            D_()
            V.tensor_scalar(A_, A_, float(NE - 1), float(CAP), ALU.add, ALU.mult)
            D_()
            V.tensor_tensor(A_, A_, C(C_E64, 32), ALU.subtract)
            V.tensor_scalar(gq, pos, float(CAP), None, ALU.is_ge)
            D_()
            V.tensor_tensor(gq, gq, A_.unsqueeze(1).broadcast_to([P, TL, 32]), ALU.mult)
            V.tensor_tensor(slot, pos, C(C_E64, 32).unsqueeze(1).broadcast_to([P, TL, 32]), ALU.add)
            D_()
            V.tensor_tensor(slot, slot, gq, ALU.add)
            D_()
            for c, o in enumerate((oh1, oh2)):
                V.tensor_tensor(rt(7 + c), slot, o, ALU.mult)
            D_()
            for c in range(2):
                V.tensor_reduce(sc(10 + c), rt(7 + c), AX, ALU.add)
            D_()
            for c in range(2):
                last = V.tensor_copy(IDX[:, c, :], sc(10 + c))
            last.then_inc(idx_ok, 1)
            ef = Z[0:1, 8100:8148]
            cm = Z[0:1, 8200:8712].rearrange("p (j e) -> p j e", j=16)
            V.tensor_scalar(ef[:, 0:32], C(C_E64, 32)[0:1], 1.0 / CAP, None, ALU.mult)
            V.tensor_tensor(cm, oe[0:1].unsqueeze(1).broadcast_to([1, 16, 32]), C(C_ROW, 16)[0:1].unsqueeze(2).broadcast_to([1, 16, 32]), ALU.is_le)
            V.tensor_scalar(Z[0:1, 8150:8158], C(C_ROW, 16)[0:1, 0:16:2], oe[0:1, 31:32], None, ALU.is_lt)
            D_()
            V.tensor_reduce(ef[:, 32:48], cm, AX, ALU.add)
            V.tensor_reduce(Z[0:1, 8160:8161], Z[0:1, 8150:8158], AX, ALU.add)
            D_()
            V.tensor_scalar(ef[:, 32:48], ef[:, 32:48], float(NE - 1), None, ALU.min)
            V.tensor_scalar(NIT, Z[0:1, 8160:8161], float(NE // 2), None, ALU.add)
            D_()
            V.tensor_copy(EID, ef)

        def pool_route(pool):
            pool.wait_ge(idx_ok, 1)
            pool.wait_ge(rowz, 16)
            for c in range(2):
                for t in range(TL):
                    pool.indirect_dma_start(rowtok, bass.IndirectOffsetOnAxis(ap=IDX[:, c, t:t + 1].bitcast(U32), axis=0),
                                            TOK[:, t:t + 1], None).then_inc(scat, 16)
            pool.wait_ge(scat, 16 * 2 * TL)
            pool.dma_start(ROWS, rowtok.rearrange("(c p) a -> p (c a)", c=24), allow_slow_non_contiguous=True).then_inc(rows_in, 16)
            pool.wait_ge(rows_in, 16)

        mslot = [ring[:, 0:HALF], ring[:, HALF:2 * HALF]] + [pj[:, HALF * i:HALF * i + HALF] for i in range(4)]
        xg = Z[:, 0:1024]
        xgT = Z[:, 1024:2048].rearrange("p (k n) -> p k n", k=KT)
        hg, hu, hd, yo = Z[:, 2048:2560], Z[:, 2560:3072], Z[:, 3072:3584], Z[:, 3584:4608]
        WE = [I["expert_w_gate"][0], I["expert_w_up"][0], I["expert_w_down"][0]]

        def trips(eng):
            return eng.value_load(NIT, min_val=NE // 2, max_val=NBLK // 2)

        def sp_moe(sp):
            with sp.Fori(0, trips(sp)) as i:
                e = [sp.value_load(EID[:, bass.ds(2 * i + x, 1)], min_val=0, max_val=NE - 1) for x in range(2)]
                for m in range(3):
                    sp.wait_ge(w_used[m], i + 1)
                    for x in range(2):
                        dst = mslot[2 * m + x].rearrange("p (k n) -> p k n", n=EH if m < 2 else D)
                        sp.dma_start(dst, WE[m][bass.ds(e[x], 1)].rearrange("a (k p) n -> p (a k) n", p=P)).then_inc(w_in_[2 * m + x], 16)

        def pool_moe(pool):
            with pool.Fori(0, trips(pool)) as i:
                pool.wait_ge(xt_done, 2 * i + 2)
                pool.tensor_copy(IDC, ROWS[:, bass.ds(i, 1)])
                pool.drain()
                pool.indirect_dma_start(xg, None, xnd, bass.IndirectOffsetOnAxis(ap=IDC.bitcast(U32), axis=0)).then_inc(xg_in, 16)

        def pe_moe(pe):
            nit = trips(pe)
            for s in w_used:
                pe.sem_inc(s, 1)
            pe.sem_inc(xt_done, 2)
            with pe.Fori(0, nit) as i:
                pe.wait_ge(xg_in, 16 * i + 16)
                for b in range(2):
                    for k in range(4):
                        last = nc.tensor.transpose(bank(b)[:, 128 * k:128 * k + 128], xg[:, 512 * b + 128 * k:512 * b + 128 * k + 128], ident)
                    last.then_inc(xt_done, 1)
                pe.wait_ge(xt_a, i + 1)
                pe.wait_ge(xt_v, i + 1)
                for m in range(2):
                    for x in range(2):
                        pe.wait_ge(w_in_[2 * m + x], 16 * i + 16)
                    for k in range(KT):
                        for x in range(2):
                            last = nc.tensor.matmul(bank(2 + m)[64 * x:64 * x + 64, :], xgT[:, k, 64 * x:64 * x + 64],
                                                    mslot[2 * m + x][:, 512 * k:512 * k + 512], start=(k == 0), stop=(k == KT - 1))
                    last.then_inc(w_used[m], 1)
                pe.wait_ge(hu_ok, i + 1)
                for k in range(4):
                    last = nc.tensor.transpose(bank(4)[:, 128 * k:128 * k + 128], hu[:, 128 * k:128 * k + 128], ident)
                last.then_inc(ht_done, 1)
                pe.wait_ge(ht_a, i + 1)
                for x in range(2):
                    pe.wait_ge(w_in_[4 + x], 16 * i + 16)
                for b in range(2):
                    for k in range(4):
                        for x in range(2):
                            last = nc.tensor.matmul(bank(5 + b)[64 * x:64 * x + 64, :], hd[:, 128 * k + 64 * x:128 * k + 64 * x + 64],
                                                    mslot[4 + x][:, 1024 * k + 512 * b:1024 * k + 512 * b + 512], start=(k == 0), stop=(k == 3))
                last.then_inc(w_used[2], 1)

        def act_moe(act):
            nit = trips(act)
            with act.Fori(0, nit) as i:
                act.wait_ge(xt_done, 2 * i + 3)
                for k in range(4):
                    last = act.activation(xgT[:, k, :], bank(0)[:, 128 * k:128 * k + 128], ACT.Identity,
                                          scale=Ac[:, 0, 0, 1, k:k + 1], bias=modc[:, 0, 24 + k:25 + k])
                last.then_inc(xt_a, 1)
                act.wait_ge(w_used[0], i + 2)
                act.activation(hg, bank(2), ACT.Silu).then_inc(silu_ok, 1)
                act.wait_ge(ht_done, i + 1)
                act.activation(hd, bank(4), ACT.Copy).then_inc(ht_a, 1)
                act.wait_ge(w_used[2], i + 2)
                act.wait_ge(y_out, 16 * i + 16)
                act.activation(yo[:, 0:512], bank(5), ACT.Copy).then_inc(y_a, 1)
                act.wait_ge(y_a, i + 1)
                act.wait_ge(y_v, i + 1)
                act.dma_start(ybuf[bass.ds(i * P, P), :], yo).then_inc(y_out, 16)
            act.wait_ge(y_out, 16 * nit + 16)
            act.sem_inc(y_stored, 1)

        def dve_moe(dve):
            with dve.Fori(0, trips(dve)) as i:
                dve.wait_ge(xt_done, 2 * i + 4)
                for k in range(4):
                    last = nc.vector.tensor_scalar(xgT[:, 4 + k, :], bank(1)[:, 128 * k:128 * k + 128], Ac[:, 0, 0, 1, 4 + k:5 + k],
                                                   modc[:, 0, 28 + k:29 + k], ALU.mult, ALU.add)
                last.then_inc(xt_v, 1)
                dve.wait_ge(silu_ok, i + 1)
                dve.wait_ge(w_used[1], i + 2)
                nc.vector.tensor_tensor(hu, hg, bank(3), ALU.mult).then_inc(hu_ok, 1)
                dve.wait_ge(w_used[2], i + 2)
                dve.wait_ge(y_out, 16 * i + 16)
                nc.vector.tensor_copy(yo[:, 512:1024], bank(6)).then_inc(y_v, 1)

        yg = [[Z[:, 1024 * (2 * i + c):1024 * (2 * i + c) + 1024] for c in range(2)] for i in range(2)]
        fng = Z[:, 4608:5632]

        def pool_comb(pool, n):
            for t in range(TL):
                if t >= 2:
                    pool.wait_ge(yg_free, t - 1)
                for c in range(2):
                    pool.indirect_dma_start(yg[t % 2][c], None, ybuf, bass.IndirectOffsetOnAxis(ap=IDX[:, c, t:t + 1].bitcast(U32), axis=0)
                                            ).then_inc(yg_in[t % 2], 16)

        def dve_comb(dve, n):
            n["gate"] += 32
            dve.wait_ge(gate_in, n["gate"])
            for t in range(TL):
                dve.wait_ge(yg_in[t % 2], 32 * (t // 2 + 1))
                y0, y1 = yg[t % 2]
                nc.vector.tensor_scalar(y0, y0, WT[0][:, t:t + 1], None, ALU.mult)
                dve.drain()
                nc.vector.scalar_tensor_tensor(y0, y1, WT[1][:, t:t + 1], y0, ALU.mult, ALU.add)
                dve.drain()
                nc.vector.tensor_tensor(y0, y0, gtb[:, 0, :], ALU.mult)
                dve.drain()
                nc.vector.tensor_tensor(xl[:, t, :], xl[:, t, :], y0, ALU.add).then_inc(yg_free, 1)

        def act_final(act, n):
            act.wait_ge(yg_free, TL)
            for t in range(TL):
                act.activation(junk, xl[:, t, :], ACT.Square, accum_out=st[:, t:t + 1])
                act.drain()
            act.activation(st[:, 16:20], st[:, 0:4], ACT.Copy).then_inc(sumsq, 1)
            n["var"] += 1
            act.wait_ge(var, n["var"])
            act.activation(st[:, 24:28], st[:, 8:12], ACT.Sqrt).then_inc(std, 1)

        def dve_final(dve, n):
            n["ss"] += 1
            dve.wait_ge(sumsq, n["ss"])
            nc.vector.tensor_scalar(st[:, 8:12], st[:, 16:20], 1.0 / D, EPS, ALU.mult, ALU.add).then_inc(var, 1)
            n["std"] += 1
            dve.wait_ge(std, n["std"])
            nc.vector.reciprocal(st[:, 32:36], st[:, 24:28])
            dve.drain()
            for t in range(TL):
                nc.vector.scalar_tensor_tensor(xl[:, t, :], xl[:, t, :], st[:, 32 + t:33 + t], fng, ALU.mult, ALU.mult)

        BL2 = [[(0, 512, ALLT), (512, 1024, ALLT), (1024, 1536, ALLT), (1536, 2048, ALLT), (2048, 2560, ALLT), (2560, 2976, ALLT)],
               [(0, 512, ALLT), (512, 1024, ALLT), (1024, 1536, ALLT), (1536, 2048, LAT), (2048, 2560, LAT), (2560, 2976, LAT)]]
        TQ = (ALLT, LAT)
        lng, lnb = Z[:, 8588:9100], Z[:, 9100:9612]
        cqg, ckg, qg, kg = Z[:, 9612:9868], Z[:, 9868:9996], Z[:, 9996:10092], Z[:, 10092:10188]
        wsr = Z[:, 10188:10700].rearrange("p (g q) -> p g q", g=4)
        wsT = Z[:, 8076:8588]
        rpt = Z[:, 7948:8076]
        tbt = [hT[:, 0:1792], hT[:, 1792:3584]]
        Qf = hT[:, 0:4608].rearrange("p (t n) -> p t n", t=TA)
        cqT = Z[:, 0:1536].rearrange("p (k n) -> p k n", k=2)
        ckT = Z[:, 1536:2304].rearrange("p (k n) -> p k n", k=1)
        rpbd = nc.dram_tensor("rpbd", (2, 120, 64 * P), F32, kind="Internal")

        def pool_params2(pool, l):
            for dst, name in ((lng, "gm_ln_g_2"), (lnb, "gm_ln_b_2"), (cqg, "mla_cq_gain_2"), (ckg, "mla_ckv_gain_2"),
                              (qg, "mla_q_gain_2"), (kg, "mla_k_gain_2")):
                pool.dma_start(dst, I[name][l].partition_broadcast(P)).then_inc(prm2, 16)
            pool.dma_start(wsr, I["gm_w_s_2"][l].rearrange("g p q -> p g q")).then_inc(prm2, 16)
            pool.memset(rpt, 0.0).then_inc(rp_ok, 1)
            pool.wait_ge(rp_ok, l + 1)
            pool.dma_start(rpt[0:120, 48:79], I["na_rpb_2"][l].rearrange("h r c -> (h r) c")).then_inc(rp_in, 16)
            pool.wait_ge(rp_in, 32 * l + 16)
            pool.dma_start(rpbd.ap()[l].rearrange("r (m n) -> r m n", n=P), rpt[0:120, :].unsqueeze(1).broadcast_to([120, 64, P])).then_inc(rp_in, 16)
            pool.wait_ge(rp_in, 32 * l + 32)

        def pool_bias(pool, l, pairs):
            for q in pairs:
                if q >= 2:
                    pool.wait_ge(tb_free, 4 * l + q - 1)
                t4 = tbt[q % 2].rearrange("p (h j c) -> p h j c", h=2, j=14)
                for h in range(2):
                    for half in range(2):
                        off = (l * 120 + (2 * q + h) * 15 + 1 - half) * 64 * P + 63
                        src = bass.AP(tensor=rpbd, offset=off, ap=[[P - 1, 64], [64 * P, 14], [1, 64]])
                        pool.dma_start(t4[64 * half:64 * half + 64, h], src).then_inc(tb_in[q % 2], 16)
                pool.wait_ge(tb_in[q % 2], 64 * (2 * l + q // 2 + 1))
                m = C(C_NM, 64).unsqueeze(1).broadcast_to([P, 28, 64])
                b = C(C_NB, 64).unsqueeze(1).broadcast_to([P, 28, 64])
                t3 = tbt[q % 2].rearrange("p (j c) -> p j c", c=64)
                pool.tensor_tensor(t3, t3, m, ALU.mult)
                pool.drain()
                pool.tensor_tensor(t3, t3, b, ALU.add).then_inc(tb_ok, 1)

        def act_shape(act, n, l):
            for t in TQ[l]:
                act.activation(pjt[:, t, GU:GU + 1024], pjt[:, t, GU:GU + 1024], ACT.Gelu).then_inc(gelu_ok, 1)
            rms_heads(act, "a", n, TQ[l], hv(NQ, 8, 64), 8, 64, None)
            rms_heads(act, "a", n, ALLT, hv(NK, 8, 64), 8, 64, None)
            rms_heads(act, "a", n, TQ[l], hv(CQ, 1, 256), 1, 256, cqg)
            rms_heads(act, "a", n, ALLT, hv(CKV, 1, 128), 1, 128, ckg)
            n["var"] += 1
            act.wait_ge(var, n["var"])
            act.activation(st[:, 320:320 + len(TQ[l])], st[:, 260:260 + len(TQ[l])], ACT.Sqrt).then_inc(std, 1)

        def dve_shape(dve, n, l):
            V = nc.vector
            nt = len(TQ[l])
            dve.wait_ge(prm2, 16 * 7 * (l + 1))
            rms_heads(dve, "v", n, TQ[l], hv(NQ, 8, 64), 8, 64, None)
            dve.drain()
            rms_heads(dve, "v", n, ALLT, hv(NK, 8, 64), 8, 64, None)
            dve.drain()
            rms_heads(dve, "v", n, TQ[l], hv(CQ, 1, 256), 1, 256, cqg)
            dve.drain()
            rms_heads(dve, "v", n, ALLT, hv(CKV, 1, 128), 1, 128, ckg)
            dve.drain()
            n["gelu"] = n.get("gelu", 0) + nt
            dve.wait_ge(gelu_ok, n["gelu"])
            vv = lambda t: pjt[:, t, GMV:GMV + 512]
            sq = [Z[:, 0:512], Z[:, 512:1024]]
            for t in TQ[l]:
                V.tensor_reduce(st[:, 500 + t:501 + t], vv(t), AX, ALU.add)
            dve.drain()
            V.tensor_scalar(st[:, 510:510 + nt], st[:, 500:500 + nt], 1.0 / 512, None, ALU.mult)
            dve.drain()
            for t in TQ[l]:
                V.tensor_scalar(vv(t), vv(t), st[:, 510 + t:511 + t], None, ALU.subtract)
            dve.drain()
            for t in TQ[l]:
                V.tensor_tensor(sq[t % 2], vv(t), vv(t), ALU.mult)
                dve.drain()
                V.tensor_reduce(st[:, 200 + t:201 + t], sq[t % 2], AX, ALU.add)
            dve.drain()
            V.tensor_scalar(st[:, 260:260 + nt], st[:, 200:200 + nt], 1.0 / 512, EPS, ALU.mult, ALU.add).then_inc(var, 1)
            n["std"] += 1
            dve.wait_ge(std, n["std"])
            V.reciprocal(st[:, 380:380 + nt], st[:, 320:320 + nt])
            dve.drain()
            for t in TQ[l]:
                V.scalar_tensor_tensor(vv(t), vv(t), st[:, 380 + t:381 + t], lng, ALU.mult, ALU.mult)
            dve.drain()
            for t in TQ[l]:
                V.tensor_tensor(vv(t), vv(t), lnb, ALU.add)

        def na_spec(l):
            def src(q):
                return lambda side, t: pjt[:, t, (NK if side == "k" else NQ) + 128 * q:(NK if side == "k" else NQ) + 128 * q + 128]

            def gain(side):
                r = (R_NAK if side == "k" else R_NAQ) + l
                return cols[:, r:r + 1]

            def biased(q, h, t):
                def f(E, b):
                    nc.vector.scalar_tensor_tensor(E[:, 0:512], b[:, 0:512], 64 ** -0.5,
                                                   tbt[q % 2][:, 896 * (h % 2) + 64 * (6 - 2 * t):896 * (h % 2) + 64 * (6 - 2 * t) + 512],
                                                   ALU.mult, ALU.add)
                    return nc.vector.tensor_scalar(E[:, 512:768], b[:, 512:768], 64 ** -0.5, None, ALU.mult)
                return f
            heads = [(P, src(q), TQ[l], gain) for q in range(4)]
            units = [dict(head=h // 2, rows=((64 * (h % 2), 64 * (h % 2) + 64),), qt=t, keys=ALLT if t < TL else (4, 5),
                          bias=biased(h // 2, h, t) if t < TL else None, scale=64 ** -0.5, combine=False,
                          v=lambda kt, h=h: pjt[:, kt, NV + 64 * h:NV + 64 * h + 64], dv=64,
                          y=pjt[:, t, NQ + 64 * h:NQ + 64 * h + 64]) for h in range(8) for t in TQ[l]]
            return heads, units

        def mla_spec(l):
            def src(h):
                return lambda side, t: pjt[:, t, GMV + 96 * h:GMV + 96 * h + 96] if side == "k" else Qf[:, t, 96 * h:96 * h + 96]
            heads = [(96, src(h), TQ[l], None) for h in range(8)]
            units = [dict(head=h, rows=((0, 96),), qt=t, keys=ALLT if t < TL else (4, 5), bias=None, scale=96 ** -0.5, combine=False,
                          v=lambda kt, h=h: pjt[:, kt, 128 * h + 64:128 * h + 128], dv=64,
                          y=Qf[:, t, 64 * h:64 * h + 64]) for h in range(8) for t in TQ[l]]
            return heads, units

        def plan_gm(n, l):
            return Plan(n, "a" + "v" * len(TQ[l]))

        def pe_gm(pe, n, l):
            p = plan_gm(n, l)
            pe.wait_ge(prm2, 16 * 7 * (l + 1))
            for g in range(4):
                last = nc.tensor.transpose(bank(7)[:, P * g:P * g + P], wsr[:, g, :], ident)
            last.then_inc(mm_done, 1)
            pe.wait_ge(evac_a, p.val[0])
            for i, t in enumerate(TQ[l]):
                for g in range(4):
                    last = nc.tensor.matmul(bank(i)[:, P * g:P * g + P], wsT[:, P * g:P * g + P], pjt[:, t, GMV + P * g:GMV + P * g + P],
                                            start=True, stop=True)
                last.then_inc(mm_done, 1)

        def act_gm(act, n, l):
            p = plan_gm(n, l)
            act.wait_ge(mm_done, p.done(0))
            act.activation(wsT, bank(7), ACT.Copy).then_inc(evac_a, 1)

        def dve_gm(dve, n, l):
            p = plan_gm(n, l)
            for i, t in enumerate(TQ[l]):
                dve.wait_ge(mm_done, p.done(1 + i))
                for g in range(4):
                    u = pjt[:, t, GU + P * g:GU + P * g + P]
                    last = nc.vector.scalar_tensor_tensor(u, bank(i)[:, P * g:P * g + P], cols[:, R_BS + 4 * l + g:R_BS + 4 * l + g + 1], u,
                                                          ALU.add, ALU.mult)
                last.then_inc(evac_v, 1)

        def plan_t(n, pairs):
            return Plan(n, ("av" * len(pairs))[:-(-len(pairs) // 4)])

        def pe_t(pe, n, pairs):
            p = plan_t(n, pairs)
            for i in range(len(p.own)):
                if i >= 8:
                    pe.wait_ge(EV[p.own[i - 8]], p.val[i - 8])
                for j, (src, _) in enumerate(pairs[4 * i:4 * i + 4]):
                    last = nc.tensor.transpose(bank(i % 8)[:, P * j:P * j + P], src, ident)
                last.then_inc(mm_done, 1)

        def each_t(eng, n, who, pairs):
            p = plan_t(n, pairs)
            for i in range(len(p.own)):
                if p.own[i] == who:
                    eng.wait_ge(mm_done, p.done(i))
                    for j, (_, dst) in enumerate(pairs[4 * i:4 * i + 4]):
                        b = bank(i % 8)[:, P * j:P * j + P]
                        last = nc.scalar.activation(dst, b, ACT.Copy) if who == "a" else nc.vector.tensor_copy(dst, b)
                    last.then_inc(EV[who], 1)

        def cqkv_pairs(l):
            return ([(pjt[:, t, CQ + P * k:CQ + P * k + P], cqT[:, k, P * t:P * t + P]) for t in TQ[l] for k in range(2)]
                    + [(pjt[:, t, CKV:CKV + P], ckT[:, 0, P * t:P * t + P]) for t in ALLT])

        def BUQ(l):
            return [(0, 512, TQ[l]), (512, 768, TQ[l])]

        BUKV = [(0, 512, ALLT), (512, 1024, ALLT)]
        q_lhs = lambda k, t: 2 if k is None else cqT[:, k, P * t:P * t + P]
        kv_lhs = lambda k, t: 1 if k is None else ckT[:, 0, P * t:P * t + P]
        act_q = lambda c0, c1, t, b: nc.scalar.activation(Qf[:, t, c0:c1], b, ACT.Copy)
        dve_q = lambda c0, c1, t, b: nc.vector.tensor_copy(Qf[:, t, c0:c1], b)

        kview = lambda t: pjt[:, t, GMV:GMV + 768].rearrange("p (h d) -> p h d", h=8)
        qview = lambda t: Qf[:, t, :].rearrange("p (h d) -> p h d", h=8)

        def dve_mla(dve, n, l):
            V = nc.vector
            for t in ALLT:
                V.tensor_copy(kview(t)[:, :, 0:64], pjt[:, t, 0:1024].rearrange("p (h d) -> p h d", h=8)[:, :, 0:64])
                V.tensor_copy(kview(t)[:, :, 64:96], pjt[:, t, KR:KR + 32].unsqueeze(1).broadcast_to([P, 8, 32]))
            dve.drain()
            rms_heads(dve, "v", n, TQ[l], qview, 8, 96, qg)
            dve.drain()
            rms_heads(dve, "v", n, ALLT, kview, 8, 96, kg)
            dve.drain()
            for t in LAT:
                for i, v in enumerate((qview, kview)):
                    x = 512 * ((2 * t + i) % 4)
                    dve_rope(dve, t, v(t)[:, :, 64:96], 8, 8, C_R2C, C_R2S, Z[:, x:x + 256], Z[:, x + 256:x + 512])

        def act_mla(act, n, l):
            rms_heads(act, "a", n, TQ[l], qview, 8, 96, qg)
            rms_heads(act, "a", n, ALLT, kview, 8, 96, kg)

        yT = [Z[:, 0:3072].rearrange("p (k n) -> p k n", k=4), Z[:, 3072:6144].rearrange("p (k n) -> p k n", k=4),
              pj[:, 0:3072].rearrange("p (k n) -> p k n", k=4)]
        acc = pj[:, 3072:3072 + TA * D].rearrange("p (t n) -> p t n", t=TA)

        def nagm_pairs(l):
            return [(pjt[:, t, c + P * k:c + P * k + P], yT[b][:, k, P * t:P * t + P])
                    for t in TQ[l] for b, c in ((0, NQ), (1, GU)) for k in range(4)]

        def mla_pairs(l):
            return [(Qf[:, t, P * k:P * k + P], yT[2][:, k, P * t:P * t + P]) for t in TQ[l] for k in range(4)]

        sg = [Z[:, 6144:6656], Z[:, 6656:7168]]
        mtmp = [Z[:, 7168:7680], Z[:, 7680:8192]]
        WO = ("na_w_o_2", "gm_w_o_2", "mla_w_o_2")

        def plan_merge(n, l):
            return Plan(n, "av" * (6 * len(TQ[l])))

        def sp_merge(sp, n, rel, l):
            p = plan_merge(n, l)
            nt = len(TQ[l])
            for j in range(6):
                nb, b = j // 3, j % 3
                for w, nk, c0, at in ((I["w_in_2"][l], KT, GATES + D * b + 512 * nb, 2 * nt * (j + 1) - 2),
                                      (I[WO[b]][l], 4, 512 * nb, 2 * nt * (j + 1) - 1)):
                    c = n["chunk"]
                    load_chunk(sp, n, lambda s, nk=nk: s[:, 0:512 * nk].rearrange("p (k n) -> p k n", n=512),
                               w[:, c0:c0 + 512].rearrange("(k p) n -> p k n", p=P), rel)
                    rel[c % 2] = p.done(at)

        def pe_merge(pe, n, l):
            p = plan_merge(n, l)
            i = 0
            for j in range(6):
                wg, wo = take_chunk(pe, n), take_chunk(pe, n)
                for t in TQ[l]:
                    for w, nk, lhs in ((wg, KT, h_lhs), (wo, 4, lambda k, t, b=j % 3: yT[b][:, k, P * t:P * t + P])):
                        if i >= 8:
                            pe.wait_ge(EV[p.own[i - 8]], p.val[i - 8])
                        for k in range(nk):
                            last = nc.tensor.matmul(bank(i % 8), lhs(k, t), w[:, 512 * k:512 * k + 512], start=(k == 0), stop=(k == nk - 1))
                        last.then_inc(mm_done, 1)
                        i += 1

        def act_merge(act, n, l):
            p = plan_merge(n, l)
            for u in range(6 * len(TQ[l])):
                act.wait_ge(mm_done, p.done(2 * u))
                if u >= 2:
                    act.wait_ge(evac_v, p.val[2 * u - 3])
                act.activation(sg[u % 2], bank((2 * u) % 8), ACT.Sigmoid).then_inc(evac_a, 1)

        def dve_merge(dve, n, l):
            p = plan_merge(n, l)
            nt = len(TQ[l])
            for u in range(6 * nt):
                j, t = u // nt, u % nt
                nb, b = j // 3, j % 3
                dve.wait_ge(evac_a, p.val[2 * u])
                dve.wait_ge(mm_done, p.done(2 * u + 1))
                a = acc[:, t, 512 * nb:512 * nb + 512]
                dst = a if b == 0 else mtmp[u % 2]
                nc.vector.tensor_tensor(dst, sg[u % 2], bank((2 * u + 1) % 8), ALU.mult).then_inc(evac_v, 1)
                if b:
                    dve.drain()
                    nc.vector.tensor_tensor(a, a, mtmp[u % 2], ALU.add)

        h1 = [pj[:, 6144 + 3072 * i:9216 + 3072 * i].rearrange("p (m n) -> p m n", m=4) for i in range(2)]
        yacc = pj[:, 0:6144].rearrange("p (t n) -> p t n", t=TA)
        rl = [Z[:, 0:512], Z[:, 512:1024]]

        def plan_ffn(n, l):
            s = 2 if len(TQ[l]) > TL else 1
            return Plan(n, ("a" * (4 * s) + "v" * (2 * len(TQ[l]))) * 8)

        def sp_ffn(sp, n, rel, l):
            p = plan_ffn(n, l)
            per = len(p.own) // 8
            for hb in range(8):
                for w, d, at in ((I["ffn_w1_2"][l][:, 512 * hb:512 * hb + 512], 512, per * hb + per - 2 * len(TQ[l]) - 1),
                                 (I["ffn_w2_2"][l][512 * hb:512 * hb + 512, :], D, per * (hb + 1) - 1)):
                    c = n["chunk"]
                    load_chunk(sp, n, lambda s, d=d: s.rearrange("p (k n) -> p k n", n=d), w.rearrange("(k p) n -> p k n", p=P), rel)
                    rel[c % 2] = p.done(at)

        def pe_ffn(pe, n, l):
            p = plan_ffn(n, l)
            i = 0
            for hb in range(8):
                w1 = take_chunk(pe, n)
                for m in range(4):
                    for c0, c1 in ((0, 512), (512, 768))[:2 if len(TQ[l]) > TL else 1]:
                        if i >= 8:
                            pe.wait_ge(EV[p.own[i - 8]], p.val[i - 8])
                        for k in range(KT):
                            last = nc.tensor.matmul(bank(i % 8, c1 - c0), w1[:, 512 * k + P * m:512 * k + P * m + P], hTk[:, k, c0:c1],
                                                    start=(k == 0), stop=(k == KT - 1))
                        last.then_inc(mm_done, 1)
                        i += 1
                w2 = take_chunk(pe, n)
                pe.wait_ge(evac_a, p.val[i - 1])
                for t in TQ[l]:
                    for b in range(2):
                        if i >= 8:
                            pe.wait_ge(EV[p.own[i - 8]], p.val[i - 8])
                        for k in range(4):
                            last = nc.tensor.matmul(bank(i % 8), h1[hb % 2][:, k, P * t:P * t + P], w2[:, D * k + 512 * b:D * k + 512 * b + 512],
                                                    start=(k == 0), stop=(k == 3))
                        last.then_inc(mm_done, 1)
                        i += 1

        def act_ffn(act, n, l):
            p = plan_ffn(n, l)
            per = len(p.own) // 8
            for hb in range(8):
                g = per * hb
                for m in range(4):
                    for c0, c1 in ((0, 512), (512, 768))[:2 if len(TQ[l]) > TL else 1]:
                        act.wait_ge(mm_done, p.done(g))
                        act.activation(rl[g % 2][:, 0:c1 - c0], bank(g % 8, c1 - c0), ACT.Relu)
                        act.drain()
                        act.activation(h1[hb % 2][:, m, c0:c1], rl[g % 2][:, 0:c1 - c0], ACT.Square).then_inc(evac_a, 1)
                        g += 1

        def dve_ffn(dve, n, l):
            p = plan_ffn(n, l)
            per = len(p.own) // 8
            for hb in range(8):
                g = per * (hb + 1) - 2 * len(TQ[l])
                for t in TQ[l]:
                    for b in range(2):
                        dve.wait_ge(mm_done, p.done(g))
                        y = yacc[:, t, 512 * b:512 * b + 512]
                        if hb == 0:
                            nc.vector.tensor_copy(y, bank(g % 8)).then_inc(evac_v, 1)
                        else:
                            nc.vector.tensor_tensor(y, y, bank(g % 8), ALU.add).then_inc(evac_v, 1)
                        g += 1
                dve.drain()
            n["gate"] += 32
            dve.wait_ge(gate_in, n["gate"])
            for t in TQ[l]:
                nc.vector.tensor_tensor(yacc[:, t, :], yacc[:, t, :], gtb[:, t // TL, :], ALU.mult)
            dve.drain()
            for t in TQ[l]:
                nc.vector.tensor_tensor(xl[:, t, :], xl[:, t, :], yacc[:, t, :], ALU.add)

        def WO2(l):
            return [(0, 512, TQ[l], "v"), (512, 1024, TQ[l], "v")]

        def acc_pairs(l):
            return [(acc[:, t, P * k:P * k + P], hTk[:, k, P * t:P * t + P]) for t in TQ[l] for k in range(KT)]

        STAGES2 = 17

        def sp_layer(sp, n, rel, l):
            f0 = n["fence"]
            plan_norm(n, TA)
            sp_lin(sp, n, rel, I["w_in_2"][l], BL2[l])
            sp.wait_ge(stage_done, f0 + 4 * 2)
            sp.dma_start(hTd, hT[:, :]).then_inc(spill, 16)
            plan_attn(n, *na_spec(l))
            plan_gm(n, l)
            plan_t(n, cqkv_pairs(l))
            sp_lin(sp, n, rel, I["mla_w_uq_2"][l], BUQ(l))
            sp_lin(sp, n, rel, I["mla_w_ukv_2"][l], BUKV)
            plan_attn(n, *mla_spec(l))
            plan_t(n, nagm_pairs(l))
            plan_t(n, mla_pairs(l))
            sp.wait_ge(stage_done, f0 + 4 * 12)
            sp.dma_start(hT[:, :], hTd).then_inc(unspill, 16)
            sp_merge(sp, n, rel, l)
            plan_t(n, acc_pairs(l))
            sp_lin(sp, n, rel, I["w_out_2"][l], WO2(l))
            plan_norm(n, len(TQ[l]))
            sp_ffn(sp, n, rel, l)
            n["fence"] = f0 + 4 * STAGES2

        def plan_attn(n, heads, units):
            Attn(n, heads, units)

        def pool_layer(pool, n, l):
            pool_params2(pool, l)
            fence(pool, n)
            fence(pool, n)
            pool.wait_ge(spill, 16 * (l + 1))
            pool_bias(pool, l, (0, 1))
            fence(pool, n)
            pool_bias(pool, l, (2, 3))
            for _ in range(10):
                fence(pool, n)
            load_gate(pool, l + 1, 2)
            fence(pool, n)
            fence(pool, n)
            load_gate(pool, l + 1, 5)
            fence(pool, n)
            fence(pool, n)

        def pe_layer(pe, n, l):
            pe_norm(pe, n, TA)
            fence(pe, n)
            pe_lin(pe, n, BL2[l], h_lhs)
            fence(pe, n)
            fence(pe, n)
            pe_attn(pe, n, *na_spec(l))
            fence(pe, n)
            pe_gm(pe, n, l)
            fence(pe, n)
            pe_t(pe, n, cqkv_pairs(l))
            fence(pe, n)
            pe_lin(pe, n, BUQ(l), q_lhs)
            fence(pe, n)
            pe_lin(pe, n, BUKV, kv_lhs)
            fence(pe, n)
            fence(pe, n)
            pe_attn(pe, n, *mla_spec(l))
            fence(pe, n)
            pe_t(pe, n, nagm_pairs(l))
            fence(pe, n)
            pe_t(pe, n, mla_pairs(l))
            fence(pe, n)
            pe.wait_ge(unspill, 16 * (l + 1))
            pe_merge(pe, n, l)
            fence(pe, n)
            pe_t(pe, n, acc_pairs(l))
            fence(pe, n)
            pe_lin(pe, n, WO2(l), h_lhs)
            fence(pe, n)
            pe_norm(pe, n, len(TQ[l]))
            fence(pe, n)
            pe_ffn(pe, n, l)
            fence(pe, n)

        def act_layer(act, n, l):
            act_norm(act, n, TA, l + 1, 0)
            fence(act, n)
            each_lin(act, n, BL2[l], "a", act_put)
            fence(act, n)
            act_shape(act, n, l)
            fence(act, n)
            act_attn(act, n, *na_spec(l))
            fence(act, n)
            act_gm(act, n, l)
            fence(act, n)
            each_t(act, n, "a", cqkv_pairs(l))
            fence(act, n)
            each_lin(act, n, BUQ(l), "a", act_q)
            fence(act, n)
            each_lin(act, n, BUKV, "a", act_put)
            fence(act, n)
            act_mla(act, n, l)
            fence(act, n)
            act_attn(act, n, *mla_spec(l))
            fence(act, n)
            each_t(act, n, "a", nagm_pairs(l))
            fence(act, n)
            each_t(act, n, "a", mla_pairs(l))
            fence(act, n)
            act_merge(act, n, l)
            fence(act, n)
            each_t(act, n, "a", acc_pairs(l))
            fence(act, n)
            plan_lin(n, WO2(l))
            fence(act, n)
            act_norm(act, n, len(TQ[l]), l + 1, 1)
            fence(act, n)
            act_ffn(act, n, l)
            fence(act, n)

        def dve_layer(dve, n, l):
            dve_norm(dve, n, TA, l + 1, 0)
            fence(dve, n)
            each_lin(dve, n, BL2[l], "v", dve_put)
            fence(dve, n)
            dve_shape(dve, n, l)
            fence(dve, n)
            dve_attn(dve, n, *na_spec(l), tables=4 * l)
            fence(dve, n)
            dve_gm(dve, n, l)
            fence(dve, n)
            each_t(dve, n, "v", cqkv_pairs(l))
            fence(dve, n)
            each_lin(dve, n, BUQ(l), "v", dve_q)
            fence(dve, n)
            each_lin(dve, n, BUKV, "v", dve_put)
            fence(dve, n)
            dve_mla(dve, n, l)
            fence(dve, n)
            dve_attn(dve, n, *mla_spec(l))
            fence(dve, n)
            each_t(dve, n, "v", nagm_pairs(l))
            fence(dve, n)
            each_t(dve, n, "v", mla_pairs(l))
            fence(dve, n)
            dve_merge(dve, n, l)
            fence(dve, n)
            each_t(dve, n, "v", acc_pairs(l))
            fence(dve, n)
            dve_resid(dve, n, WO2(l))
            fence(dve, n)
            dve_norm(dve, n, len(TQ[l]), l + 1, 1)
            fence(dve, n)
            dve_ffn(dve, n, l)
            fence(dve, n)

        block = ctx.enter_context(nc.Block())
        W_IN = I["w_in"][0]
        NF = 16 + 2 * STAGES2
        WO1 = [(0, 512, LAT, "v"), (512, 1024, LAT, "v")]

        @block.sync
        def _(sp):
            n, rel = tally(), [0, 0]
            sp.dma_start(xl[:, 0:TL, :], I["x"][0].rearrange("(t p) d -> p t d", p=P)).then_inc(x_in, 16)
            sp.dma_start(xl[:, TL:TA, :], I["ctx"][0].rearrange("(t p) d -> p t d", p=P)).then_inc(x_in, 16)
            sp_mods(sp, n, rel)
            plan_norm(n, TA)
            sp_lin(sp, n, rel, W_IN, BL1)
            for plan in (plan_gate, plan_dec, plan_st, plan_o):
                plan(n)
            plan_turn(n, KT, LAT)
            sp_lin(sp, n, rel, I["w_out"][0], WO1)
            for t in range(TL):
                sp.wait_ge(xn_ok, TA + t + 1)
                sp.dma_start(xnd[P * t:P * t + P, :], XK(t)).then_inc(xn_st, 16)
            plan_norm(n, TL)
            plan_route(n)
            sp.wait_ge(stage_done, 4 * 13)
            sp_moe(sp)
            n["fence"] = 4 * 16
            sp.wait_ge(stage_done, 4 * 16)
            sp.dma_start(xl[:, TL:TA, :], I["ctx_2"][0].rearrange("(t p) d -> p t d", p=P)).then_inc(x_in, 16)
            for l in range(2):
                sp_layer(sp, n, rel, l)
            F = 4 * NF
            sp.wait_ge(stage_done, F)
            sp.dma_start(out[0].rearrange("(t p) d -> p t d", p=P), xl[:, 0:TL, :]).then_inc(out_in, 16)
            sp.wait_ge(out_in, 16)

        @block.gpsimd
        def _(pool):
            n = tally()
            pool_params(pool)
            pool.dma_start(lamt, I["da_lambda"][0].rearrange("a d -> (a d)").partition_broadcast(P)).then_inc(prm, 16)
            pool.dma_start(subln, I["da_subln_g"][0].partition_broadcast(P)).then_inc(prm, 16)
            pool.dma_start(glag, I["gla_norm_g"][0].partition_broadcast(P)).then_inc(prm, 16)
            for m in range(2):
                pool.dma_start(w2a[16 * 0:16, 256 * m:256 * m + 256], I["gla_gate_w2"][0][m]).then_inc(prm, 16)
                pool.dma_start(w2a[16:17, 256 * m:256 * m + 256], I["gla_gate_b"][0][m:m + 1, :]).then_inc(prm, 16)
            for _ in range(3):
                fence(pool, n)
            pool.memset(hT[:, 0:D], 0.0).then_inc(zero_ok, 1)
            pool.wait_ge(zero_ok, 1)
            for r in range(NE * CAP, NBLK * CAP, P):
                pool.dma_start(ybuf[r:r + P, :], hT[:, 0:D]).then_inc(ybz, 16)
            pool.wait_ge(ybz, 16 * (NBLK - NE) * CAP // P)
            for _ in range(6):
                fence(pool, n)
            load_gate(pool, 0, 2)
            for _ in range(2):
                fence(pool, n)
            pool_route_params(pool)
            fence(pool, n)
            pool_route(pool)
            pool.wait_ge(xn_st, 64)
            fence(pool, n)
            pool_moe(pool)
            fence(pool, n)
            load_gate(pool, 0, 5)
            pool.dma_start(fng, I["final_norm_g"].partition_broadcast(P)).then_inc(fng_in, 16)
            pool_comb(pool, n)
            fence(pool, n)
            fence(pool, n)
            for l in range(2):
                pool_layer(pool, n, l)

        @block.tensor
        def _(pe):
            n = tally()
            pe_mods(pe, n)
            fence(pe, n)
            pe_norm(pe, n, TA)
            fence(pe, n)
            pe_lin(pe, n, BL1, h_lhs)
            fence(pe, n)
            fence(pe, n)
            pe_attn(pe, n, *da_spec())
            fence(pe, n)
            pe_gates(pe, n)
            fence(pe, n)
            pe_dec(pe, n)
            fence(pe, n)
            pe_states(pe, n)
            fence(pe, n)
            pe_glao(pe, n)
            fence(pe, n)
            pe_turn(pe, n, KT, LAT, lambda k, t: pjt[:, t, 128 * k:128 * k + 128])
            fence(pe, n)
            pe_lin(pe, n, WO1, h_lhs)
            fence(pe, n)
            pe_norm(pe, n, TL, keep=XK)
            fence(pe, n)
            pe_route(pe, n)
            fence(pe, n)
            pe_moe(pe)
            fence(pe, n)
            fence(pe, n)
            fence(pe, n)
            for l in range(2):
                pe_layer(pe, n, l)

        @block.scalar
        def _(act):
            n = tally()
            act_mods(act, n)
            fence(act, n)
            act.wait_ge(x_in, 32)
            act_norm(act, n, TA, 0, 0)
            fence(act, n)
            each_lin(act, n, BL1, "a", act_put)
            fence(act, n)
            act_lambda(act, n)
            fence(act, n)
            act_attn(act, n, *da_spec())
            rms_heads(act, "a", n, LAT, hv(DQ, 4, 128), 4, 128, subln)
            fence(act, n)
            act_gates(act, n)
            fence(act, n)
            act_dec(act, n)
            fence(act, n)
            each_states(act, n, "a")
            fence(act, n)
            act_glao(act, n)
            fence(act, n)
            each_turn(act, n, "a", KT, LAT, hT_dst)
            fence(act, n)
            plan_lin(n, WO1)
            fence(act, n)
            act_norm(act, n, TL, 0, 1)
            fence(act, n)
            act_route(act, n)
            act.sem_inc(y_out, 16)
            fence(act, n)
            act_moe(act)
            fence(act, n)
            fence(act, n)
            act_final(act, n)
            fence(act, n)
            act.wait_ge(x_in, 48)
            for l in range(2):
                act_layer(act, n, l)

        @block.vector
        def _(dve):
            n = tally()
            dve_mods(dve, n)
            fence(dve, n)
            dve.wait_ge(x_in, 32)
            dve_norm(dve, n, TA, 0, 0)
            fence(dve, n)
            each_lin(dve, n, BL1, "v", dve_put)
            fence(dve, n)
            dve_da_before(dve)
            dve_lambda(dve, n)
            fence(dve, n)
            dve_attn(dve, n, *da_spec(), lam=lam)
            rms_heads(dve, "v", n, LAT, hv(DQ, 4, 128), 4, 128, subln, mul=1.0 - (0.8 - 0.6))
            fence(dve, n)
            dve_gates(dve, n)
            fence(dve, n)
            dve_dec(dve, n)
            fence(dve, n)
            each_states(dve, n, "v")
            fence(dve, n)
            dve_glao(dve, n)
            fence(dve, n)
            each_turn(dve, n, "v", KT, LAT, hT_dst)
            fence(dve, n)
            dve_resid(dve, n, WO1)
            fence(dve, n)
            dve_norm(dve, n, TL, 0, 1, keep=XK)
            fence(dve, n)
            dve_route(dve, n)
            fence(dve, n)
            dve_moe(dve)
            fence(dve, n)
            dve_comb(dve, n)
            fence(dve, n)
            dve.wait_ge(fng_in, 16)
            dve_final(dve, n)
            fence(dve, n)
            dve.wait_ge(x_in, 48)
            for l in range(2):
                dve_layer(dve, n, l)


_INS = ["x", "c", "ctx", "c_ctx", "w_ada", "b_ada", "norm_mix_g", "norm_ffn_g", "w_in", "da_lambda", "da_subln_g",
        "gla_gate_w2", "gla_gate_b", "gla_norm_g", "w_out", "router_group_w", "router_group_b", "router_expert_w",
        "router_expert_b", "expert_w_gate", "expert_w_up", "expert_w_down", "final_norm_g", "c_2", "ctx_2",
        "c_ctx_2", "w_mod_2", "b_mod_2", "g_norm1_2", "g_norm2_2", "w_in_2", "na_q_gain_2", "na_k_gain_2", "na_rpb_2",
        "na_w_o_2", "gm_ln_g_2", "gm_ln_b_2", "gm_w_s_2", "gm_b_s_2", "gm_w_o_2", "mla_cq_gain_2", "mla_ckv_gain_2",
        "mla_w_uq_2", "mla_w_ukv_2", "mla_q_gain_2", "mla_k_gain_2", "mla_w_o_2", "w_out_2", "ffn_w1_2", "ffn_w2_2"]


def kernel(**inputs):
    import concourse.bacc as _bacc
    from concourse.bass_utils import run_bass_kernel_spmd as _run

    nc = _bacc.Bacc("TRN2", target_bir_lowering=False, num_devices=1)
    arrays, aps = {}, {}
    for name in _INS + ["cst"]:
        a = np.ascontiguousarray(constants() if name == "cst" else inputs[name])
        arrays[f"in_{name}_dram"] = a
        aps[name] = nc.dram_tensor(f"in_{name}_dram", a.shape, mybir.dt.from_np(a.dtype), kind="ExternalInput").ap()
    out = nc.dram_tensor("out_0_dram", (1, TL * P, D), F32, kind="ExternalOutput").ap()
    program(nc, aps, out)
    r = _run(nc, [arrays], core_ids=[0])
    return r.results[0]["out_0_dram"]
```

```python
import math
from contextlib import ExitStack

import numpy as np

import concourse.bass as bass
from concourse import mybir

F32 = mybir.dt.float32
I32 = mybir.dt.int32
U32 = mybir.dt.uint32
ALU = mybir.AluOpType
ACT = mybir.ActivationFunctionType
AX = mybir.AxisListType.X

P = 128
D = 1024
KT = D // P
TL, TC = 4, 2
TA = TL + TC
NTOK = TA * P
CHUNK = 64
EPS = 1e-6
NEG = -1e30
BANK = 512

DQ, DK, DV, GQ, GK, GV, GR, LRF, LRB, IN1 = 0, 512, 1024, 1536, 1792, 2048, 2560, 3072, 3088, 3104
NK, NV, CKV, KR, NQ, GU, GMV, CQ, GATES = 0, 512, 1024, 1152, 1184, 1696, 2208, 2720, 2976
PW = IN1
NE, NG, EH = 32, 4, 512
CAP = 64
NBLK = 48
HALF = 4096

C_ID, C_TF, C_TB, C_BLK, C_US, C_CH = 0, 128, 256, 384, 512, 640
C_R1C, C_R1S, C_R2C, C_R2S, C_NM, C_NB = 642, 898, 1154, 1282, 1410, 1474
C_I32, C_E64, C_ONE, C_ROW, C_TA, C_TZ, C_TK, C_N = 1538, 1570, 1602, 1730, 1746, 1874, 2002, 2006

R_C, R_G, R_NAQ, R_NAK, R_BS, R_N, R_MB, R_ALL = 0, 48, 96, 98, 100, 108, 108, 252


def constants():
    c = np.zeros((P, C_N), np.float32)
    i = np.arange(P)
    same = i[:, None] // CHUNK == i[None, :] // CHUNK
    c[:, C_ID:C_ID + P] = np.eye(P)
    c[:, C_TF:C_TF + P] = same & (i[:, None] <= i[None, :])
    c[:, C_TB:C_TB + P] = same & (i[:, None] >= i[None, :])
    c[:, C_TK:C_TK + TL] = i[:, None] + P * np.arange(TL)
    c[:, C_TA:C_TA + P] = same & (i[:, None] > i[None, :])
    c[:, C_TZ:C_TZ + P] = same & (i[:, None] < i[None, :])
    c[:, C_BLK:C_BLK + P] = same
    c[:, C_US:C_US + P] = i[:, None] < i[None, :]
    c[:, C_CH:C_CH + 2] = i[:, None] // CHUNK == np.arange(2)
    tok = np.arange(TL * P)
    pos = np.stack([tok // 64, tok % 64], 1).astype(np.float32)
    for n, (cc, cs) in ((16, (C_R1C, C_R1S)), (8, (C_R2C, C_R2S))):
        inv = np.power(np.float32(10000.0), -np.arange(n, dtype=np.float32) / np.float32(n)).astype(np.float32)
        ang = pos[:, :, None] * inv
        cos = np.repeat(np.cos(ang)[:, :, None, :], 2, 2)
        sin = np.sin(ang)[:, :, None, :] * np.array([-1.0, 1.0], np.float32)[:, None]
        for at, t in ((cc, cos), (cs, sin)):
            c[:, at:at + TL * 4 * n] = t.reshape(TL, P, 4 * n).transpose(1, 0, 2).reshape(P, -1)
    col = i % 64
    c0 = np.clip(col - 8, 0, 48)
    kc = np.arange(64)
    inw = (kc[None] >= c0[:, None]) & (kc[None] < c0[:, None] + 16)
    c[:, C_NM:C_NM + 64] = inw
    c[:, C_NB:C_NB + 64] = np.where(inw, 0.0, NEG)
    c[:, C_I32:C_I32 + 32] = np.arange(32, 0, -1)
    c[:, C_E64:C_E64 + 32] = np.arange(32) * CAP
    c[:, C_ONE:C_ONE + P] = 1.0
    c[:, C_ROW:C_ROW + 16] = np.arange(16)
    return c


class Plan:

    def __init__(self, n, owners):
        self.mm0, self.own, self.val = n["mm"], owners, []
        for o in owners:
            if o != "-":
                n[o] += 1
            self.val.append(n.get(o, 0))
        n["mm"] += len(owners)

    def done(self, i):
        return self.mm0 + i + 1


def program(nc, I, out):
    ctx = ExitStack()
    with ctx:
        def sb(name, shape, dt=F32):
            return ctx.enter_context(nc.sbuf_tensor(name, shape, dt))

        def sem(name):
            return ctx.enter_context(nc.semaphore(name))

        ring = sb("ring", [P, 2 * HALF])
        xl = sb("xl", [P, TA, D])
        hT = sb("hT", [P, KT * NTOK])
        pj = sb("pj", [P, TA * PW])
        cst = sb("consts", [P, C_N])
        small = sb("small", [P, 1296])
        Z = sb("Z", [P, 10700])
        ps = ctx.enter_context(nc.psum_tensor("ps", [P, 8 * BANK], F32))

        hTk = hT[:, :].rearrange("p (k n) -> p k n", k=KT)
        pjt = pj[:, :].rearrange("p (t n) -> p t n", t=TA)

        def bank(b, n=BANK):
            return ps[:, b * BANK:b * BANK + n]

        def C(at, n=P):
            return cst[:, at:at + n]

        ident = C(C_ID)

        cols = small[:, 0:R_ALL]
        modc = small[:, 252:540].rearrange("p (l n) -> p l n", l=3)
        Ac = small[:, 540:636].rearrange("p (l w n k) -> p l w n k", l=3, w=2, n=2)
        st = small[:, 640:1240]

        modp = nc.dram_tensor("modp", (3, 2, 6 * D), F32, kind="Internal").ap()
        modd = nc.dram_tensor("modd", (3, 2, 6 * D), F32, kind="Internal").ap()
        hTd = nc.dram_tensor("hTd", (P, KT * NTOK), F32, kind="Internal").ap()
        xnd = nc.dram_tensor("xnd", (TL * P, D), F32, kind="Internal").ap()
        rowtok = nc.dram_tensor("rowtok", (NBLK * CAP, 1), I32, kind="Internal").ap()
        ybuf = nc.dram_tensor("ybuf", (NBLK * CAP, D), F32, kind="Internal").ap()

        stage_done = sem("stage_done")
        mm_done, evac_a, evac_v = sem("mm_done"), sem("evac_a"), sem("evac_v")
        EV = {"a": evac_a, "v": evac_v}
        slot_in = [sem("slot0_in"), sem("slot1_in")]
        params_in, cols_in, mod_st = sem("params_in"), sem("cols_in"), sem("mod_st")
        modr_in, mod_in = [sem(f"modr{l}_in") for l in range(3)], [sem(f"mod_slot{i}_in") for i in range(6)]
        mring_in = [sem(f"merge_slot{i}_in") for i in range(5)]
        mod_done, mod_out, modT_done, modc_ok = sem("mod_done"), sem("mod_out"), sem("modT_done"), sem("modc_ok")
        modb_ok, modd_in, cols_done, cols_ok = sem("modb_ok"), sem("modd_in"), sem("cols_done"), sem("cols_ok")
        ctx_in, x_in = sem("ctx_in"), sem("x_in")
        silu_c = sem("silu_c")
        sumsq, var, std, xn_ok = sem("sumsq"), sem("var"), sem("std"), sem("xn_ok")
        s_done, s_free_a, s_free_v = sem("s_done"), sem("s_free_a"), sem("s_free_v")
        mx_ok, e_ok, a_ok, t_done = sem("mx_ok"), sem("e_ok"), sem("a_ok"), sem("t_done")
        et_a, et_v, o_done, y_ok = sem("et_a"), sem("et_v"), sem("o_done"), sem("y_ok")
        prep_done, prep_a, prep_v = sem("prep_done"), sem("prep_a"), sem("prep_v")
        v2a, a2v, v2p, prm = sem("v2a"), sem("a2v"), sem("v2p"), sem("prm")
        out_in, gate_in = sem("out_in"), sem("gate_in")
        rparams, zero_ok, rowz, idx_ok = sem("rparams"), sem("zero_ok"), sem("rowz"), sem("idx_ok")
        scat, rows_in, xg_in, xn_st = sem("scat"), sem("rows_in"), sem("xg_in"), sem("xn_st")
        w_used = [sem(f"w_used{m}") for m in range(3)]
        w_in_ = [sem(f"w_in{m}") for m in range(6)]
        xt_done, xt_a, xt_v, silu_ok = sem("xt_done"), sem("xt_a"), sem("xt_v"), sem("silu_ok")
        hu_ok, ht_done, ht_a = sem("hu_ok"), sem("ht_done"), sem("ht_a")
        y_a, y_v, y_out, yg_free = sem("y_a"), sem("y_v"), sem("y_out"), sem("yg_free")
        prm2, rp_ok, rp_in, tb_free, tb_ok = sem("prm2"), sem("rp_ok"), sem("rp_in"), sem("tb_free"), sem("tb_ok")
        tb_in = [sem("tb_in0"), sem("tb_in1")]
        spill, unspill = sem("spill"), sem("unspill")
        y_stored = sem("y_stored")
        ex_used, ybz = sem("ex_used"), sem("ybz")
        yg_in, fng_in = [sem("yg_in0"), sem("yg_in1")], sem("fng_in")

        def tally():
            return {k: 0 for k in ("mm", "a", "v", "fence", "chunk", "ss", "var", "std", "xn", "at", "a2v", "v2a", "v2p", "prm")}

        def fence(eng, n):
            eng.drain().then_inc(stage_done, 1)
            n["fence"] += 4
            eng.wait_ge(stage_done, n["fence"])

        def load_chunk(sp, n, dst, src, rel):
            c = n["chunk"]
            if rel[c % 2]:
                sp.wait_ge(mm_done, rel[c % 2])
            o = (c % 2) * HALF
            sp.dma_start(dst(ring[:, o:o + HALF]), src).then_inc(slot_in[c % 2], 16)
            n["chunk"] += 1

        def take_chunk(pe, n):
            c = n["chunk"]
            pe.wait_ge(slot_in[c % 2], 16 * (c // 2 + 1))
            n["chunk"] += 1
            o = (c % 2) * HALF
            return ring[:, o:o + HALF]

        WM = [I["w_ada"][0], I["w_mod_2"][0], I["w_mod_2"][1]]
        BM = [I["b_ada"][0], I["b_mod_2"][0], I["b_mod_2"][1]]
        sT = small[:, 1240:1288]
        rows = Z[:, 0:P]
        brows = Z[:, P:4 * P]
        mstage = [Z[:, 8192:8704], Z[:, 8704:9216]]
        modr = Z[:, 9216:9600]
        MSTEPS = 12

        def mod_slot(c):
            if c < MSTEPS:
                return pj[:, HALF * (c % 4):HALF * (c % 4) + HALF], mod_in[c % 4], 16 * (c // 4 + 1)
            c -= MSTEPS
            return Z[:, HALF * (c % 2):HALF * (c % 2) + HALF], mod_in[4 + c % 2], 16 * (c // 2 + 1)

        def load_mod(eng, c):
            depth = 4 if c < MSTEPS else 2
            if c % MSTEPS >= depth or c >= 2 * MSTEPS:
                eng.wait_ge(mod_done, c - depth + 1)
            l, r, q = c // MSTEPS, c // 4 % 3, c % 4
            slot, ready, _ = mod_slot(c)
            eng.dma_start(slot.rearrange("p (k n) -> p k n", k=2),
                          WM[l][256 * q:256 * q + 256, 2048 * r:2048 * r + 2048].rearrange("(k p) n -> p k n", p=P)).then_inc(ready, 16)

        def pe_mod(pe, c):
            g, q = c // 4, c % 4
            slot, ready, value = mod_slot(c)
            if q == 0 and g >= 2:
                pe.wait_ge(mod_out, g - 1)
            pe.wait_ge(ready, value)
            for kk in range(2):
                k = 2 * q + kk
                for j in range(4):
                    last = nc.tensor.matmul(ps[32 * j:32 * j + 2, (6 + g % 2) * BANK:(7 + g % 2) * BANK],
                                            sT[:, 16 * (c // MSTEPS) + k:16 * (c // MSTEPS) + k + 9:8],
                                            slot[:, 2048 * kk + 512 * j:2048 * kk + 512 * j + 512],
                                            start=(k == 0), stop=(k == KT - 1))
            last.then_inc(mod_done, 1)

        def dve_mod(dve, g):
            dve.wait_ge(mod_done, 4 * g + 4)
            if g >= 2:
                dve.wait_ge(mod_st, 64 * (g - 1))
            for j in range(4):
                last = nc.vector.tensor_copy(mstage[g % 2][32 * j:32 * j + 2, :], ps[32 * j:32 * j + 2, (6 + g % 2) * BANK:(7 + g % 2) * BANK])
            last.then_inc(mod_out, 1)

        def act_mod(act, g):
            l, r = g // 3, g % 3
            act.wait_ge(mod_out, g + 1)
            for j in range(4):
                act.dma_start(modp[l][:, 2048 * r + 512 * j:2048 * r + 512 * j + 512], mstage[g % 2][32 * j:32 * j + 2, :]).then_inc(mod_st, 16)
            if g in (0, 1, 3, 4, 6, 7):
                act.wait_ge(mod_st, 64 * (g + 1))
            if r == 2:
                act.wait_ge(mod_st, 64 * (g + 1))
                act.dma_start(modr[0:96, P * l:P * l + P], modp[l].rearrange("w (s q) -> (w s) q", q=P)).then_inc(modr_in[l], 16)

        def pe_mod_turn(pe, layers):
            for l in layers:
                pe.wait_ge(modr_in[l], 16)
                nc.tensor.transpose(bank(l, 96), modr[0:96, P * l:P * l + P], ident[0:96, 0:96]).then_inc(modT_done, 1)
            for l in layers:
                pe.wait_ge(modc_ok, l + 1)
                nc.tensor.transpose(bank(3 + l, P)[0:96, :], modc[:, l, :], ident).then_inc(modT_done, 1)

        def dve_mod_turn(dve, layers):
            for i, l in enumerate(layers):
                dve.wait_ge(modT_done, 2 * layers[0] + i + 1)
                b = cols[:, R_MB + 48 * l:R_MB + 48 * l + 48].unsqueeze(1).broadcast_to([P, 2, 48])
                nc.vector.tensor_tensor(modc[:, l, :].rearrange("p (w n) -> p w n", w=2), bank(l, 96).rearrange("p (w n) -> p w n", w=2),
                                        b, ALU.add).then_inc(modc_ok, 1)
                dve.drain()
                for w in range(2):
                    for m in range(2):
                        s = modc[:, l, 48 * w + 8 * (1 + 3 * m):48 * w + 8 * (1 + 3 * m) + 8]
                        g = cols[:, R_G + 16 * l + 8 * m:R_G + 16 * l + 8 * m + 8]
                        nc.vector.scalar_tensor_tensor(Ac[:, l, w, m, :], s, 1.0, g, ALU.add, ALU.mult)

        def act_mod_turn(act, layers):
            for i, l in enumerate(layers):
                act.wait_ge(modT_done, 2 * layers[0] + len(layers) + i + 1)
                act.activation(modr[0:96, P * l:P * l + P], bank(3 + l, P)[0:96, :], ACT.Copy).then_inc(modb_ok, 1)
                act.wait_ge(modb_ok, l + 1)
                act.dma_start(modd[l].rearrange("w (s q) -> (w s) q", q=P), modr[0:96, P * l:P * l + P]).then_inc(modd_in, 16)
            act.wait_ge(modd_in, 16 * (layers[-1] + 1))

        def sp_first(sp):
            sp.dma_start(cst[:, :], I["cst"]).then_inc(params_in, 16)
            for c in range(MSTEPS):
                load_mod(sp, c)

        def pe_first(pe):
            pe.wait_ge(params_in, 16)
            pe.wait_ge(cols_in, 16 * N_COLS)
            nc.tensor.transpose(bank(0, R_N), rows[0:R_N, :], ident[0:R_N, 0:R_N])
            for l in range(3):
                last = nc.tensor.transpose(bank(0)[:, R_MB + 48 * l:R_MB + 48 * l + 48], brows[0:48, P * l:P * l + P], ident[0:48, 0:48])
            last.then_inc(cols_done, 1)
            pe.wait_ge(silu_c, 1)
            for c in range(MSTEPS):
                pe_mod(pe, c)
            pe_mod_turn(pe, (0,))

        def act_first(act):
            act.wait_ge(cols_done, 1)
            act.activation(cols, bank(0, R_ALL), ACT.Copy).then_inc(cols_ok, 1)
            act.wait_ge(cols_ok, 1)
            act.activation(sT, cols[:, 0:48], ACT.Silu).then_inc(silu_c, 1)
            for g in range(3):
                act_mod(act, g)
            act_mod_turn(act, (0,))

        def dve_first(dve):
            for g in range(3):
                dve_mod(dve, g)
            dve.wait_ge(cols_ok, 1)
            dve_mod_turn(dve, (0,))

        N_COLS = 6 + 6 + 4 + 2 + 3

        def load_rows(eng):
            def row(at, src, k):
                eng.dma_start(rows[at:at + k, :], src).then_inc(cols_in, 16)

            flat = lambda a: a.rearrange("(k p) -> k p", p=P)
            row(0, flat(I["c"][0]), 8)
            row(8, flat(I["c_ctx"]), 8)
            row(16, flat(I["c_2"][0]), 8)
            row(24, flat(I["c_ctx_2"]), 8)
            row(32, flat(I["c_2"][0]), 8)
            row(40, flat(I["c_ctx_2"]), 8)
            row(48, flat(I["norm_mix_g"][0]), 8)
            row(56, flat(I["norm_ffn_g"][0]), 8)
            for l in range(2):
                row(64 + 16 * l, flat(I["g_norm1_2"][l]), 8)
                row(72 + 16 * l, flat(I["g_norm2_2"][l]), 8)
            for m in range(2):
                eng.dma_start(rows[R_NAQ:R_NAQ + 2, 64 * m:64 * m + 64], I["na_q_gain_2"]).then_inc(cols_in, 16)
                eng.dma_start(rows[R_NAK:R_NAK + 2, 64 * m:64 * m + 64], I["na_k_gain_2"]).then_inc(cols_in, 16)
            for l in range(2):
                row(R_BS + 4 * l, I["gm_b_s_2"][l], 4)
            for l in range(3):
                eng.dma_start(brows[0:48, P * l:P * l + P], flat(BM[l])).then_inc(cols_in, 16)

        junk = Z[:, 0:D]
        xn = [Z[:, D:2 * D], Z[:, 2 * D:3 * D]]

        def plan_norm(n, nt):
            return Plan(n, "av" * nt)

        def pe_norm(pe, n, nt, keep=None):
            p = plan_norm(n, nt)
            for t in range(nt):
                pe.wait_ge(xn_ok, n["xn"] + t + 1)
                src = xn[t % 2] if keep is None else keep(t)
                for h in range(2):
                    i = 2 * t + h
                    if i >= 4:
                        pe.wait_ge(EV[p.own[i - 4]], p.val[i - 4])
                    for k in range(4):
                        last = nc.tensor.transpose(bank(i % 4)[:, 128 * k:128 * k + 128],
                                                   src[:, 512 * h + 128 * k:512 * h + 128 * k + 128], ident)
                    last.then_inc(mm_done, 1)
            n["xn"] += nt

        def act_norm(act, n, nt, l, m):
            p = plan_norm(n, nt)
            n["xn"] += nt
            for t in range(nt):
                last = act.activation(junk, xl[:, t, :], ACT.Square, accum_out=st[:, t:t + 1])
                act.drain()
            last = act.activation(st[:, 16:16 + nt], st[:, 0:nt], ACT.Copy)
            last.then_inc(sumsq, 1)
            n["var"] += 1
            act.wait_ge(var, n["var"])
            act.activation(st[:, 24:24 + nt], st[:, 8:8 + nt], ACT.Sqrt).then_inc(std, 1)
            for t in range(nt):
                i = 2 * t
                act.wait_ge(mm_done, p.done(i))
                for k in range(4):
                    last = act.activation(hTk[:, k, 128 * t:128 * t + 128], bank(i % 4)[:, 128 * k:128 * k + 128], ACT.Identity,
                                          scale=Ac[:, l, t // TL, m, k:k + 1],
                                          bias=modc[:, l, 48 * (t // TL) + 24 * m + k:48 * (t // TL) + 24 * m + k + 1])
                last.then_inc(evac_a, 1)

        def dve_norm(dve, n, nt, l, m, keep=None):
            p = plan_norm(n, nt)
            n["ss"] += 1
            dve.wait_ge(sumsq, n["ss"])
            nc.vector.tensor_scalar(st[:, 8:8 + nt], st[:, 16:16 + nt], 1.0 / D, EPS, ALU.mult, ALU.add).then_inc(var, 1)
            n["std"] += 1
            dve.wait_ge(std, n["std"])
            nc.vector.reciprocal(st[:, 32:32 + nt], st[:, 24:24 + nt])
            dve.drain()
            for t in range(nt + 1):
                if t < nt:
                    if t >= 2 and keep is None:
                        dve.wait_ge(mm_done, p.done(2 * t - 3))
                    dst = xn[t % 2] if keep is None else keep(t)
                    nc.vector.tensor_scalar(dst, xl[:, t, :], st[:, 32 + t:33 + t], None, ALU.mult).then_inc(xn_ok, 1)
                if t >= 1:
                    u = t - 1
                    i = 2 * u + 1
                    dve.wait_ge(mm_done, p.done(i))
                    for k in range(4):
                        kk = 4 + k
                        c = 48 * (u // TL) + 24 * m + kk
                        last = nc.vector.tensor_scalar(hTk[:, kk, 128 * u:128 * u + 128], bank(i % 4)[:, 128 * k:128 * k + 128],
                                                       Ac[:, l, u // TL, m, kk:kk + 1], modc[:, l, c:c + 1], ALU.mult, ALU.add)
                    last.then_inc(evac_v, 1)

        def lin_banks(blocks):
            return 6 if blocks is BL1 else 8

        def plan_lin(n, blocks, own="av"):
            g = "".join(b[3] * len(b[2]) if len(b) > 3 else "." * len(b[2]) for b in blocks)
            return Plan(n, "".join(own[i % 2] if o == "." else o for i, o in enumerate(g)))

        def sp_lin(sp, n, rel, w, blocks):
            p = plan_lin(n, blocks)
            i = 0
            for c0, c1, ts, *_ in blocks:
                c = n["chunk"]
                load_chunk(sp, n, lambda s: s[:, 0:w.shape[0] // P * (c1 - c0)].rearrange("p (k n) -> p k n", n=c1 - c0),
                           w[:, c0:c1].rearrange("(k p) n -> p k n", p=P), rel)
                i += len(ts)
                rel[c % 2] = p.done(i - 1)

        def pe_lin(pe, n, blocks, lhs):
            p, nb = plan_lin(n, blocks), lin_banks(blocks)
            i = 0
            nk = lhs(None, None)
            for c0, c1, ts, *_ in blocks:
                s = take_chunk(pe, n)
                w = c1 - c0
                for t in ts:
                    if i >= nb:
                        pe.wait_ge(EV[p.own[i - nb]], p.val[i - nb])
                    for k in range(nk):
                        last = nc.tensor.matmul(bank(i % nb, w), lhs(k, t), s[:, k * w:k * w + w], start=(k == 0), stop=(k == nk - 1))
                    last.then_inc(mm_done, 1)
                    i += 1
                    if nb == 6 and i <= 2 * MSTEPS:
                        pe_mod(pe, MSTEPS + i - 1)

        def each_lin(eng, n, blocks, who, put):
            p, nb = plan_lin(n, blocks), lin_banks(blocks)
            i = 0
            for c0, c1, ts, *_ in blocks:
                for t in ts:
                    if p.own[i] == who:
                        eng.wait_ge(mm_done, p.done(i))
                        put(c0, c1, t, bank(i % nb, c1 - c0)).then_inc(EV[who], 1)
                    i += 1
                    if nb == 6 and i % 4 == 0 and i <= 2 * MSTEPS:
                        (act_mod if who == "a" else dve_mod)(eng, 3 + i // 4 - 1)

        def h_lhs(k, t):
            return KT if k is None else hTk[:, k, 128 * t:128 * t + 128]

        ALLT, LAT = tuple(range(TA)), tuple(range(TL))
        BL1 = [(0, 512, LAT), (512, 1024, ALLT), (1024, 1536, ALLT), (1536, 2048, ALLT), (2048, 2560, ALLT),
               (2560, 3072, LAT), (3072, 3104, ALLT)]

        def act_put(c0, c1, t, b):
            return nc.scalar.activation(pjt[:, t, c0:c1], b, ACT.Copy)

        def dve_put(c0, c1, t, b):
            return nc.vector.tensor_copy(pjt[:, t, c0:c1], b)

        kT = [Z[:, 0:768], Z[:, 768:1536]]
        qT = [Z[:, 1536:2304], Z[:, 2304:3072]]
        qz = [[Z[:, 1536:2304], Z[:, 2304:3072]], [hT[:, 4608:5376], hT[:, 5376:6144]]]
        EB = [[Z[:, 3072 + 1536 * u + 768 * m:3840 + 1536 * u + 768 * m] for m in range(2)] for u in range(2)]
        ET = [Z[:, 6144:6912], Z[:, 6912:7680]]
        TB = Z[:, 7680:9600]

        class Attn:

            def __init__(self, n, heads, units):
                self.heads, self.units = heads, units
                self.nm = 2 if units[0]["combine"] else 1
                self.split = units[0]["rows"][0] == (0, 64)
                self.preps = [(h, side, ts) for h, (_, _, qts, _) in enumerate(heads) for side in ("k", "q")
                              for ts in ((0, 1, 2, 3), (4, 5)) if side == "k" or set(ts) <= set(qts)]
                first = {}
                for i, u in enumerate(units):
                    first.setdefault(u["head"], i)
                self.at = {}
                seen = {}
                for j, (h, _, _) in enumerate(self.preps):
                    k = seen[h] = seen.get(h, -1) + 1
                    self.at.setdefault(-1 if h == 0 else first[h - 1] + k, []).append(j)
                c = lambda key, k=1: n.__setitem__(key, n.get(key, 0) + k) or n[key]
                self.s, self.e, self.mx, self.free, self.t, self.et, self.a, self.o, self.y = ([] for _ in range(9))
                for u in units:
                    for _ in range(self.nm):
                        self.s.append(c("s"))
                        self.mx.append(c("mx"))
                        self.e.append(c("e"))
                        self.free.append((s_free_v, c("sf")) if u["bias"] is not None else (e_ok, n["e"]))
                    full = len(u["keys"]) == 6
                    self.t.append((c("t"), c("t")) if full else (None, c("t")))
                    self.et.append((c("eta") if full else None, c("etv")))
                    self.a.append(c("acomb") if u["combine"] else None)
                    self.o.append(c("o"))
                    self.y.append(c("y"))
                self.pd, self.pe_ = [], []
                for j in range(len(self.preps)):
                    self.pd.append(c("pd"))
                    self.pe_.append((prep_a, c("pa")) if j % 2 == 0 else (prep_v, c("pv")))

        def pe_attn(pe, n, heads, units):
            A = Attn(n, heads, units)

            def prep(j):
                h, side, ts = A.preps[j]
                rows_, src, _, _ = heads[h]
                if j:
                    pe.wait_ge(*A.pe_[j - 1])
                for t in ts:
                    last = nc.tensor.transpose(bank(7)[0:rows_, 128 * (t - ts[0]):128 * (t - ts[0]) + 128], src(side, t), ident)
                last.then_inc(prep_done, 1)

            def scores(i):
                u = units[i]
                for j, (h, _, _) in enumerate(A.preps):
                    if h == u["head"]:
                        pe.wait_ge(*A.pe_[j])
                for m in range(A.nm):
                    g = A.nm * i + m
                    if g >= 2:
                        pe.wait_ge(*A.free[g - 2])
                    b = ps[:, 1024 * (g % 2):1024 * (g % 2) + 1024]
                    rs = slice(*u["rows"][m])
                    q = qT[u["head"] % 2]
                    if A.split:
                        q = qz[u["head"] % 2][rs.start // 64]
                        rs = slice(0, P)
                    q = q[rs, 128 * u["qt"]:128 * u["qt"] + 128]
                    if len(u["keys"]) == 6:
                        nc.tensor.matmul(b[:, 0:512], q, kT[u["head"] % 2][rs, 0:512], start=True, stop=True)
                    nc.tensor.matmul(b[:, 512:768], q, kT[u["head"] % 2][rs, 512:768], start=True, stop=True).then_inc(s_done, 1)

            def transp(i):
                u = units[i]
                if u["combine"]:
                    pe.wait_ge(a_ok, A.a[i])
                else:
                    pe.wait_ge(e_ok, A.e[i])
                E = EB[i % 2][0]
                if len(u["keys"]) == 6:
                    prev = [x[0] for x in A.et[:i] if x[0] is not None]
                    if prev:
                        pe.wait_ge(et_a, prev[-1])
                    for t in range(4):
                        last = nc.tensor.transpose(bank(4)[:, 128 * t:128 * t + 128], E[:, 128 * t:128 * t + 128], ident)
                    last.then_inc(t_done, 1)
                if i:
                    pe.wait_ge(et_v, A.et[i - 1][1])
                for t in (4, 5):
                    last = nc.tensor.transpose(bank(5)[:, 128 * (t - 4):128 * (t - 4) + 128], E[:, 128 * t:128 * t + 128], ident)
                last.then_inc(t_done, 1)

            def values(i):
                u = units[i]
                if A.et[i][0] is not None:
                    pe.wait_ge(et_a, A.et[i][0])
                pe.wait_ge(et_v, A.et[i][1])
                if i:
                    pe.wait_ge(y_ok, A.y[i - 1])
                for t in u["keys"]:
                    last = nc.tensor.matmul(bank(6, u["dv"]), ET[i % 2][:, 128 * t:128 * t + 128], u["v"](t),
                                            start=(t == u["keys"][0]), stop=(t == u["keys"][-1]))
                last.then_inc(o_done, 1)

            for j in A.at.get(-1, []):
                prep(j)
            for i in range(len(units) + 2):
                if i < len(units):
                    scores(i)
                for j in A.at.get(i, []):
                    prep(j)
                if 0 <= i - 1 < len(units):
                    transp(i - 1)
                if i >= 2:
                    values(i - 2)

        def prep_out(eng, A, j, who):
            h, side, ts = A.preps[j]
            if A.pe_[j][0] is not (prep_a if who == "a" else prep_v):
                return
            rows_, _, _, gain = A.heads[h]
            eng.wait_ge(prep_done, A.pd[j])
            dst = (kT if side == "k" else qT)[h % 2][0:rows_, 128 * ts[0]:128 * ts[-1] + 128]
            src = bank(7, 128 * len(ts))[0:rows_, :]
            parts = [(slice(0, rows_), dst)]
            if A.split and side == "q":
                parts = [(slice(64 * x, 64 * x + 64), qz[h % 2][x][64 * x:64 * x + 64, 128 * ts[0]:128 * ts[-1] + 128]) for x in range(2)]
            for rs, dst in parts:
                if who == "a":
                    last = nc.scalar.activation(dst, src[rs], ACT.Copy, **({} if gain is None else {"scale": gain(side)[rs]}))
                elif gain is None:
                    last = nc.vector.tensor_copy(dst, src[rs])
                else:
                    last = nc.vector.tensor_scalar(dst, src[rs], gain(side)[rs], None, ALU.mult)
            last.then_inc(prep_a if who == "a" else prep_v, 1)

        def stat(i, k):
            at = 100 + 8 * (i % 4) + k
            return st[:, at:at + 1]

        def act_attn(act, n, heads, units):
            A = Attn(n, heads, units)

            def exps(i):
                u = units[i]
                k0 = 128 * u["keys"][0]
                for m in range(A.nm):
                    g = A.nm * i + m
                    if i >= 2:
                        act.wait_ge(t_done, A.t[i - 2][1])
                    act.wait_ge(mx_ok, A.mx[g])
                    E = EB[i % 2][m][:, k0:768]
                    src = E if u["bias"] is not None else ps[:, 1024 * (g % 2) + k0:1024 * (g % 2) + 768]
                    act.activation(E, src, ACT.Exp, bias=stat(i, m), scale=1.0 if u["bias"] is not None else u["scale"],
                                   accum_out=stat(i, 2 + m)).then_inc(e_ok, 1)

            def et(i):
                if A.et[i][0] is None:
                    return
                act.wait_ge(t_done, A.t[i][0])
                if i >= 2:
                    act.wait_ge(o_done, A.o[i - 2])
                act.activation(ET[i % 2][:, 0:512], bank(4), ACT.Copy).then_inc(et_a, 1)

            for j in A.at.get(-1, []):
                prep_out(act, A, j, "a")
            for i in range(len(units) + 1):
                if i < len(units):
                    exps(i)
                for j in A.at.get(i, []):
                    prep_out(act, A, j, "a")
                if i >= 1:
                    et(i - 1)

        def dve_attn(dve, n, heads, units, lam=None, tables=None):
            A = Attn(n, heads, units)

            def maxima(i):
                u = units[i]
                k0 = 128 * u["keys"][0]
                for m in range(A.nm):
                    g = A.nm * i + m
                    dve.wait_ge(s_done, A.s[g])
                    src = ps[:, 1024 * (g % 2) + k0:1024 * (g % 2) + 768]
                    if u["bias"] is not None:
                        if i >= 2:
                            dve.wait_ge(t_done, A.t[i - 2][1])
                        E = EB[i % 2][m]
                        dve.wait_ge(tb_ok, tables + u["head"] + 1)
                        u["bias"](E, ps[:, 1024 * (g % 2):1024 * (g % 2) + 768]).then_inc(s_free_v, 1)
                        dve.drain()
                        src = E[:, k0:768]
                    nc.vector.reduce_max(stat(i, 6 + m), src, AX)
                    dve.drain()
                    nc.vector.tensor_scalar(stat(i, m), stat(i, 6 + m), -1.0 if u["bias"] is not None else -u["scale"],
                                            None, ALU.mult).then_inc(mx_ok, 1)

            def norms(i):
                u = units[i]
                dve.wait_ge(e_ok, A.e[A.nm * i + A.nm - 1])
                nc.vector.reciprocal(st[:, 100 + 8 * (i % 4) + 4:100 + 8 * (i % 4) + 4 + A.nm],
                                     st[:, 100 + 8 * (i % 4) + 2:100 + 8 * (i % 4) + 2 + A.nm])
                if u["combine"]:
                    dve.drain()
                    E0, E1 = EB[i % 2]
                    nc.vector.tensor_scalar(E1, E1, stat(i, 5), lam, ALU.mult, ALU.mult)
                    dve.drain()
                    nc.vector.scalar_tensor_tensor(E0, E0, stat(i, 4), E1, ALU.mult, ALU.subtract).then_inc(a_ok, 1)

            def et(i):
                dve.wait_ge(t_done, A.t[i][1])
                if i >= 2:
                    dve.wait_ge(o_done, A.o[i - 2])
                nc.vector.tensor_copy(ET[i % 2][:, 512:768], bank(5, 256)).then_inc(et_v, 1)

            def outs(i):
                u = units[i]
                dve.wait_ge(o_done, A.o[i])
                if u["combine"]:
                    nc.vector.tensor_copy(u["y"], bank(6, u["dv"])).then_inc(y_ok, 1)
                else:
                    nc.vector.tensor_scalar(u["y"], bank(6, u["dv"]), stat(i, 4), None, ALU.mult).then_inc(y_ok, 1)

            if A.split:
                for b in range(2):
                    for x in range(2):
                        nc.vector.memset(qz[b][x][64 - 64 * x:128 - 64 * x, :], 0.0)
            for j in A.at.get(-1, []):
                prep_out(dve, A, j, "v")
            for i in range(len(units) + 2):
                if i < len(units):
                    maxima(i)
                for j in A.at.get(i, []):
                    prep_out(dve, A, j, "v")
                if 0 <= i - 1 < len(units):
                    norms(i - 1)
                    et(i - 1)
                if i >= 2:
                    outs(i - 2)
                if tables is not None and i < len(units) and (i + 1 == len(units) or units[i + 1]["head"] != units[i]["head"]):
                    dve.drain().then_inc(tb_free, 1)

        def da_spec():
            def src(h):
                return lambda side, t: pjt[:, t, (DK if side == "k" else DQ) + 128 * h:(DK if side == "k" else DQ) + 128 * h + 128]
            heads = [(P, src(h), LAT, None) for h in range(4)]
            units = [dict(head=h, rows=((0, 64), (64, 128)), qt=t, keys=ALLT, bias=None, scale=64 ** -0.5, combine=True,
                          v=lambda kt, h=h: pjt[:, kt, DV + 128 * h:DV + 128 * h + 128], dv=128,
                          y=pjt[:, t, DQ + 128 * h:DQ + 128 * h + 128]) for h in range(4) for t in LAT]
            return heads, units

        def dve_rope(dve, t, v, g, f, cc, cs, A_, B_):
            cosb = C(cc + 4 * f * t, 4 * f).unsqueeze(1).broadcast_to([P, g, 4 * f])
            sin4 = C(cs + 4 * f * t, 4 * f).rearrange("p (a s f) -> p a s f", a=2, s=2)
            v5 = v.rearrange("p g (a s f) -> p g a s f", a=2, s=2)
            A3, B5 = A_.rearrange("p (g n) -> p g n", g=g), B_.rearrange("p (g a s f) -> p g a s f", g=g, a=2, s=2)
            nc.vector.tensor_tensor(A3, v, cosb, ALU.mult)
            for s in range(2):
                nc.vector.tensor_tensor(B5[:, :, :, s, :], v5[:, :, :, 1 - s, :],
                                        sin4[:, :, s, :].unsqueeze(1).broadcast_to([P, g, 2, f]), ALU.mult)
            dve.drain()
            nc.vector.tensor_tensor(v, A3, B_.rearrange("p (g n) -> p g n", g=g), ALU.add)

        lamt, lam = Z[:, 9600:9856], st[:, 180:181]
        subln, glag = Z[:, 9856:9984], Z[:, 9984:10112]
        w2a = Z[:, 10112:10624]

        def rms_heads(eng, who, n, tiles, view, H, dh, gain, mul=1.0):
            nt = len(tiles)
            ss = st[:, 200:200 + nt * H]
            vv = st[:, 260:260 + nt * H]
            sd = st[:, 320:320 + nt * H]
            rr = st[:, 380:380 + nt * H]
            sq = [Z[:, 0:H * dh], Z[:, 1024:1024 + H * dh]]
            if who == "v":
                for i, t in enumerate(tiles):
                    v = view(t)
                    s3 = sq[i % 2].rearrange("p (h d) -> p h d", h=H)
                    nc.vector.tensor_tensor(s3, v, v, ALU.mult)
                    eng.drain()
                    nc.vector.tensor_reduce(ss[:, H * i:H * i + H], s3, AX, ALU.add)
                eng.drain()
                nc.vector.tensor_scalar(vv, ss, 1.0 / dh, EPS, ALU.mult, ALU.add).then_inc(var, 1)
                n["std"] += 1
                eng.wait_ge(std, n["std"])
                nc.vector.reciprocal(rr, sd)
                eng.drain()
                if mul != 1.0:
                    nc.vector.tensor_scalar(rr, rr, mul, None, ALU.mult)
                    eng.drain()
                for i, t in enumerate(tiles):
                    v = view(t)
                    nc.vector.tensor_tensor(v, v, rr[:, H * i:H * i + H].unsqueeze(2).broadcast_to([P, H, dh]), ALU.mult)
                if gain is not None:
                    eng.drain()
                    for i, t in enumerate(tiles):
                        v = view(t)
                        nc.vector.tensor_tensor(v, v, gain.unsqueeze(1).broadcast_to([P, H, dh]), ALU.mult)
            else:
                n["var"] += 1
                eng.wait_ge(var, n["var"])
                eng.activation(sd, vv, ACT.Sqrt).then_inc(std, 1)

        def hv(c0, H, dh):
            return lambda t: pjt[:, t, c0:c0 + H * dh].rearrange("p (h d) -> p h d", h=H)

        def dve_da_before(dve):
            dve.wait_ge(prm, 16 * 7)
            for t in LAT:
                dve_rope(dve, t, hv(DQ, 16, 64)(t), 16, 16, C_R1C, C_R1S, Z[:, 2048 * (t % 2):2048 * (t % 2) + 1024],
                         Z[:, 2048 * (t % 2) + 1024:2048 * (t % 2) + 2048])
            l4 = lamt.rearrange("p (a b d) -> p a b d", a=2, b=2)
            pr = Z[:, 9000:9128].rearrange("p (a d) -> p a d", a=2)
            nc.vector.tensor_tensor(pr, l4[:, :, 0, :], l4[:, :, 1, :], ALU.mult)
            dve.drain()
            nc.vector.tensor_reduce(st[:, 182:184], pr, AX, ALU.add).then_inc(v2a, 1)

        def act_lambda(act, n):
            n["v2a"] += 1
            act.wait_ge(v2a, n["v2a"])
            act.activation(st[:, 184:186], st[:, 182:184], ACT.Exp).then_inc(a2v, 1)

        def dve_lambda(dve, n):
            n["a2v"] += 1
            dve.wait_ge(a2v, n["a2v"])
            nc.vector.scalar_tensor_tensor(lam, st[:, 184:185], 0.8 - 0.6 * math.exp(-0.0), st[:, 185:186], ALU.add, ALU.subtract)
            dve.drain()

        Gg = Z[:, 0:3072].rearrange("p (t n) -> p t n", t=TA)
        zc = Z[:, 3072:6144].rearrange("p (t n) -> p t n", t=TA)
        sp_ = Z[:, 6144:9216].rearrange("p (t n) -> p t n", t=TA)
        lrT = hT[0:32, 0:1536].rearrange("p (t n) -> p t n", t=TA)
        qdT = hT[:, 1536:3584].rearrange("p (t n) -> p t n", t=TL)
        kiT = hT[:, 3584:5632].rearrange("p (t n) -> p t n", t=TL)
        ex = [[Z[:, 3072 + 1536 * i + 512 * j:3584 + 1536 * i + 512 * j] for j in range(3)] for i in range(2)]
        qk = [Z[:, 6144 + 1024 * i:7168 + 1024 * i] for i in range(2)]
        DD = Z[:, 0:6144].rearrange("p (c d q n) -> p c d q n", c=12, d=2, q=2)
        SM = [[Z[:, 6144 + 1024 * i + 512 * d:6656 + 1024 * i + 512 * d] for d in range(2)] for i in range(2)]
        dec = st[:, 440:488]
        FWD = [8, 9, 10, 11] + list(range(8))
        BWD = [11, 10, 9, 8] + list(range(7, -1, -1))
        TRI = (C_TF, C_TB)
        AFTER = (C_TA, C_TZ)

        def plan_gate(n):
            return Plan(n, "a" * (2 * TA))

        def pe_gates(pe, n):
            p = plan_gate(n)
            n["v2p"] += 1
            pe.wait_ge(v2p, n["v2p"])
            for i in range(2 * TA):
                t = i % TA
                if i >= 4:
                    pe.wait_ge(evac_a, p.val[i - 4])
                if i < TA:
                    for d in range(2):
                        last = nc.tensor.transpose(bank(i % 4)[0:16, 128 * d:128 * d + 128], pjt[:, t, LRF + 16 * d:LRF + 16 * d + 16], ident)
                else:
                    pe.wait_ge(evac_a, p.val[t])
                    for d in range(2):
                        last = nc.tensor.matmul(bank(i % 4)[:, 256 * d:256 * d + 256], lrT[0:17, t, 128 * d:128 * d + 128],
                                                w2a[0:17, 256 * d:256 * d + 256], start=True, stop=True)
                last.then_inc(mm_done, 1)

        def act_gates(act, n):
            p = plan_gate(n)
            n["v2a"] += 1
            act.wait_ge(v2a, n["v2a"])
            for i in range(2 * TA):
                t = i % TA
                act.wait_ge(mm_done, p.done(i))
                if i < TA:
                    act.activation(lrT[0:16, t, :], bank(i % 4)[0:16, 0:256], ACT.Copy).then_inc(evac_a, 1)
                else:
                    act.activation(zc[:, t, :], bank(i % 4), ACT.Copy).then_inc(evac_a, 1)
            act.drain()
            act.activation(sp_, zc, ACT.Abs)
            act.drain()
            act.activation(sp_, sp_, ACT.Exp, scale=-1.0)
            act.drain()
            act.activation(sp_, sp_, ACT.Ln, bias=1.0).then_inc(a2v, 1)

        def dve_gates(dve, n):
            plan_gate(n)
            nc.vector.memset(hT[0:32, 0:1536], 1.0).then_inc(v2p, 1)
            nc.vector.memset(st[0:1, 599:600], 0.0).then_inc(v2a, 1)
            n["a2v"] += 1
            dve.wait_ge(a2v, n["a2v"])
            nc.vector.scalar_tensor_tensor(Gg, zc, 0.0, sp_, ALU.min, ALU.subtract)

        def plan_dec(n):
            return Plan(n, "aa" * TA + "va" * TL + "a")

        def pe_dec(pe, n):
            p = plan_dec(n)
            for t in range(TA):
                for j, tri in enumerate((TRI, AFTER)):
                    i = 2 * t + j
                    if t >= 2:
                        pe.wait_ge(evac_a, dec_s(p, t - 2, j))
                    for d in range(2):
                        last = nc.tensor.matmul(bank(i % 4)[:, 256 * d:256 * d + 256], C(tri[d]), Gg[:, t, 256 * d:256 * d + 256],
                                                start=True, stop=True)
                    last.then_inc(mm_done, 1)
                if 1 <= t <= TL:
                    turn_dec(pe, n, p, t - 1)
            for t in range(TA):
                for d in range(2):
                    for q in range(2):
                        k = 8 * t + 4 * d + 2 * q
                        last = nc.tensor.matmul(bank(6)[:, k:k + 2], Gg[:, t, 256 * d + 128 * q:256 * d + 128 * q + 128], C(C_CH, 2),
                                                start=True, stop=True)
            last.then_inc(mm_done, 1)

        def dec_order():
            o = []
            for t in range(TA):
                o += [("s", t, 0), ("s", t, 1)]
                if 1 <= t <= TL:
                    o += [("t", t - 1, 0), ("t", t - 1, 1)]
            return {k: i for i, k in enumerate(o)}

        DECO = dec_order()

        def turn_dec(pe, n, p, t):
            n["v2p"] += 1
            pe.wait_ge(v2p, n["v2p"])
            for j in range(2):
                if t >= 1:
                    pe.wait_ge(*((evac_v, p.val[2 * TA + 2 * (t - 1)]) if j == 0 else (evac_a, dec_a(p, t - 1))))
                for x in range(4):
                    last = nc.tensor.transpose(bank(4 + j)[:, 128 * x:128 * x + 128], qk[t % 2][:, 512 * j + 128 * x:512 * j + 128 * x + 128], ident)
                last.then_inc(mm_done, 1)

        def dec_a(p, t):
            k = DECO[("t", t, 1)]
            return p.val[0] - 1 + sum(1 for x, i in DECO.items() if i <= k and (x[0] == "s" or x[2] == 1))

        def dec_s(p, t, j):
            k = DECO[("s", t, j)]
            return p.val[0] - 1 + sum(1 for x, i in DECO.items() if i <= k and (x[0] == "s" or x[2] == 1))

        def act_dec(act, n):
            p = plan_dec(n)
            for (kind, t, j), i in DECO.items():
                act_need = kind == "s" or j == 1
                if not act_need:
                    continue
                act.wait_ge(mm_done, p.done(i))
                if kind == "t":
                    act.activation(kiT[:, t, :], bank(5), ACT.Copy).then_inc(evac_a, 1)
                elif j == 0:
                    if t >= 2:
                        act.wait_ge(ex_used, t - 1)
                    act.activation(ex[t % 2][0], bank((2 * t) % 4), ACT.Exp, scale=1 / 16)
                    act.activation(ex[t % 2][1], bank((2 * t) % 4), ACT.Exp, scale=-1 / 16).then_inc(evac_a, 1)
                else:
                    act.activation(ex[t % 2][2], bank((2 * t + 1) % 4), ACT.Exp, scale=1 / 16).then_inc(evac_a, 1)
            act.wait_ge(mm_done, p.done(len(DECO)))
            act.activation(dec, bank(6, 48), ACT.Exp, scale=1 / 16).then_inc(evac_a, 1)

        def dve_dec(dve, n):
            p = plan_dec(n)
            for t in range(TA):
                dve.wait_ge(evac_a, dec_s(p, t, 1))
                k2 = pjt[:, t, GK:GK + 256].unsqueeze(1).broadcast_to([P, 2, 256])
                q2 = pjt[:, t, GQ:GQ + 256].unsqueeze(1).broadcast_to([P, 2, 256])
                e3 = [e.rearrange("p (d n) -> p d n", d=2) for e in ex[t % 2]]
                if t < TL:
                    if t >= 2:
                        dve.wait_ge(mm_done, p.done(DECO[("t", t - 2, 1)]))
                    a = qk[t % 2].rearrange("p (j d n) -> p j d n", j=2, d=2)
                    nc.vector.scalar_tensor_tensor(a[:, 0], q2, 64 ** -0.5, e3[0], ALU.mult, ALU.mult)
                    nc.vector.tensor_tensor(a[:, 1], k2, e3[1], ALU.mult).then_inc(v2p, 1)
                nc.vector.tensor_tensor(pjt[:, t, DK:DK + 512].rearrange("p (d n) -> p d n", d=2), k2, e3[2], ALU.mult).then_inc(ex_used, 1)
                if 1 <= t <= TL:
                    dve.wait_ge(mm_done, p.done(DECO[("t", t - 1, 0)]))
                    nc.vector.tensor_copy(qdT[:, t - 1, :], bank(4)).then_inc(evac_v, 1)

        def plan_st(n):
            return Plan(n, "av" * 6)

        def pe_states(pe, n):
            p = plan_st(n)
            for ci in range(12):
                t, c = ci // 2, ci % 2
                if ci >= 8:
                    pe.wait_ge(EV[p.own[ci - 8]], p.val[ci - 8])
                rs = slice(64 * c, 64 * c + 64)
                for d in range(2):
                    for h in range(4):
                        last = nc.tensor.matmul(bank(ci % 8)[64 * (h % 2):64 * (h % 2) + 64, 256 * d + 128 * (h // 2):256 * d + 128 * (h // 2) + 128],
                                                pjt[rs, t, DK + 256 * d + 64 * h:DK + 256 * d + 64 * h + 64],
                                                pjt[rs, t, GV + 128 * h:GV + 128 * h + 128], start=True, stop=True)
                last.then_inc(mm_done, 1)

        def each_states(eng, n, who):
            p = plan_st(n)
            for ci in range(12):
                if p.own[ci] == who:
                    eng.wait_ge(mm_done, p.done(ci))
                    dst = Z[:, 512 * ci:512 * ci + 512]
                    if who == "a":
                        nc.scalar.activation(dst, bank(ci % 8), ACT.Copy).then_inc(evac_a, 1)
                    else:
                        nc.vector.tensor_copy(dst, bank(ci % 8)).then_inc(evac_v, 1)
            if who == "v":
                eng.wait_ge(evac_a, p.val[10])
                eng.drain()
                for s in range(1, 12):
                    for d, order in enumerate((FWD, BWD)):
                        a, b = order[s - 1], order[s]
                        for q in range(2):
                            k = 8 * (b // 2) + 4 * d + 2 * q + b % 2
                            nc.vector.scalar_tensor_tensor(DD[:, b, d, q, :], DD[:, a, d, q, :], dec[:, k:k + 1], DD[:, b, d, q, :],
                                                           ALU.mult, ALU.add)
                    eng.drain()

        def plan_o(n):
            return Plan(n, "vvvvaa" * TL)

        def pe_glao(pe, n):
            p = plan_o(n)
            for t in range(TL):
                for g in range(4):
                    d, par = g // 2, g % 2
                    rs = slice(64 * par, 64 * par + 64)
                    if t:
                        pe.wait_ge(evac_v, p.val[6 * (t - 1) + g])
                    for q in range(2):
                        x = 256 * d + 128 * q
                        last = nc.tensor.matmul(bank(g)[:, 128 * q:128 * q + 128], kiT[rs, t, x:x + 128], qdT[rs, t, x:x + 128],
                                                start=True, stop=True)
                    last.then_inc(mm_done, 1)
                for par in range(2):
                    rs = slice(64 * par, 64 * par + 64)
                    pe.wait_ge(evac_v, p.val[6 * t + 2 + par])
                    if t >= 2:
                        pe.wait_ge(evac_a, p.val[6 * (t - 2) + 4 + par])
                    for q in range(2):
                        h = 2 * q + par
                        o = bank(4 + 2 * (t % 2) + par)[:, 128 * q:128 * q + 128]
                        for d in range(2):
                            nc.tensor.matmul(o, SM[t % 2][d][:, 128 * h:128 * h + 128], pjt[:, t, GV + 128 * h:GV + 128 * h + 128],
                                             start=(d == 0), stop=False)
                        for d, order in enumerate((FWD, BWD)):
                            for c in range(2):
                                prev = order[order.index(2 * t + c) - 1]
                                x = 256 * d + 128 * q
                                last = nc.tensor.matmul(o[64 * c:64 * c + 64, :], qdT[rs, t, x + 64 * c:x + 64 * c + 64], DD[rs, prev, d, q, :],
                                                        start=False, stop=(d == 1))
                    last.then_inc(mm_done, 1)

        def dve_glao(dve, n):
            p = plan_o(n)
            for t in range(TL):
                if t >= 2:
                    dve.wait_ge(mm_done, p.done(6 * (t - 2) + 5))
                for g in range(4):
                    d, par = g // 2, g % 2
                    dve.wait_ge(mm_done, p.done(6 * t + g))
                    m = C(TRI[d]).unsqueeze(1).broadcast_to([P, 2, P])
                    nc.vector.tensor_tensor(SM[t % 2][d].rearrange("p (q a n) -> p a q n", q=2, a=2)[:, par],
                                            bank(g, 256).rearrange("p (q n) -> p q n", q=2), m, ALU.mult).then_inc(evac_v, 1)
            dve.wait_ge(evac_a, p.val[6 * (TL - 1) + 5])
            rms_heads(dve, "v", n, LAT, hv(DK, 4, 128), 4, 128, glag)
            dve.drain()
            n["a2v"] += 1
            dve.wait_ge(a2v, n["a2v"])
            for t in LAT:
                nc.vector.tensor_tensor(pjt[:, t, DK:DK + 512], pjt[:, t, DK:DK + 512], pjt[:, t, GR:GR + 512], ALU.mult)

        def act_glao(act, n):
            p = plan_o(n)
            for t in range(TL):
                for par in range(2):
                    act.wait_ge(mm_done, p.done(6 * t + 4 + par))
                    act.activation(pjt[:, t, DK:DK + 512].rearrange("p (q a n) -> p a q n", q=2, a=2)[:, par],
                                   bank(4 + 2 * (t % 2) + par, 256).rearrange("p (q n) -> p q n", q=2), ACT.Copy).then_inc(evac_a, 1)
            rms_heads(act, "a", n, LAT, hv(DK, 4, 128), 4, 128, glag)
            act.activation(pjt[:, 0:TL, GR:GR + 512], pjt[:, 0:TL, GR:GR + 512], ACT.Silu).then_inc(a2v, 1)

        def plan_turn(n, nk, tiles):
            return Plan(n, "av" * (nk * len(tiles) // 8) if (nk * len(tiles)) % 8 == 0 else "a" * (nk * len(tiles) // 4))

        def pe_turn(pe, n, nk, tiles, src):
            p = plan_turn(n, nk, tiles)
            i = 0
            for t in tiles:
                for k0 in range(0, nk, 4):
                    if i >= 8:
                        pe.wait_ge(EV[p.own[i - 8]], p.val[i - 8])
                    for k in range(4):
                        last = nc.tensor.transpose(bank(i % 8)[:, 128 * k:128 * k + 128], src(k0 + k, t), ident)
                    last.then_inc(mm_done, 1)
                    i += 1

        def each_turn(eng, n, who, nk, tiles, dst):
            p = plan_turn(n, nk, tiles)
            i = 0
            for t in tiles:
                for k0 in range(0, nk, 4):
                    if p.own[i] == who:
                        eng.wait_ge(mm_done, p.done(i))
                        b = bank(i % 8).rearrange("p (k n) -> p k n", k=4)
                        if who == "a":
                            nc.scalar.activation(dst(k0, t), b, ACT.Copy).then_inc(evac_a, 1)
                        else:
                            nc.vector.tensor_copy(dst(k0, t), b).then_inc(evac_v, 1)
                    i += 1

        def hT_dst(k0, t):
            return hTk[:, k0:k0 + 4, 128 * t:128 * t + 128]

        gtb = Z[:, 8192:10240].rearrange("p (w n) -> p w n", w=2)

        def load_gate(eng, l, s):
            for w in range(2):
                eng.dma_start(gtb[:, w, :], modd[l, w, D * s:D * s + D].partition_broadcast(P)).then_inc(gate_in, 16)

        def dve_resid(dve, n, blocks):
            p = plan_lin(n, blocks)
            i = 0
            tmp = [Z[:, 7168:7680], Z[:, 7680:8192]]
            n["gate"] = n.get("gate", 0) + 32
            dve.wait_ge(gate_in, n["gate"])
            for c0, c1, ts, *_ in blocks:
                for t in ts:
                    dve.wait_ge(mm_done, p.done(i))
                    nc.vector.tensor_tensor(tmp[i % 2], bank(i % 8), gtb[:, t // TL, c0:c1], ALU.mult).then_inc(evac_v, 1)
                    dve.drain()
                    nc.vector.tensor_tensor(xl[:, t, c0:c1], xl[:, t, c0:c1], tmp[i % 2], ALU.add)
                    i += 1

        XK = lambda t: Z[:, 1024 + 1024 * t:2048 + 1024 * t]
        rw = Z[:, 5200:5488].rearrange("p (k n) -> p k n", k=KT)
        rb = Z[:, 5488:5524]

        def rt(i, w=32):
            return Z[:, 5600 + 128 * i:5600 + 128 * i + TL * w].rearrange("p (t n) -> p t n", t=TL)

        LG = Z[:, 7400:7400 + 36 * TL].rearrange("p (t n) -> p t n", t=TL)
        sc = lambda i: Z[:, 7600 + TL * i:7600 + TL * i + TL]
        WT = [Z[:, 7700:7704], Z[:, 7704:7708]]
        IDX = Z[:, 7712:7720].bitcast(I32).rearrange("p (c t) -> p c t", c=2)
        TOK = Z[:, 7720:7724].bitcast(I32)
        ROWS = Z[:, 7724:7748].bitcast(I32)
        IDC = Z[:, 7748:7749].bitcast(I32)
        ZERO = Z[:, 7750:7774].bitcast(I32)
        EID = Z[0:1, 7780:7828].bitcast(I32)
        NIT = Z[0:1, 7828:7829].bitcast(I32)

        def pool_route_params(pool):
            pool.dma_start(rw[:, :, 0:NG], I["router_group_w"][0].rearrange("(k p) n -> p k n", p=P)).then_inc(rparams, 16)
            pool.dma_start(rw[:, :, NG:NG + NE], I["router_expert_w"][0].rearrange("(k p) n -> p k n", p=P)).then_inc(rparams, 16)
            pool.dma_start(rb[:, 0:NG], I["router_group_b"][0].partition_broadcast(P)).then_inc(rparams, 16)
            pool.dma_start(rb[:, NG:NG + NE], I["router_expert_b"][0].partition_broadcast(P)).then_inc(rparams, 16)
            pool.memset(ZERO, 0).then_inc(zero_ok, 1)
            pool.wait_ge(zero_ok, 2)
            pool.dma_start(rowtok.rearrange("(c p) a -> p (c a)", c=24), ZERO, allow_slow_non_contiguous=True).then_inc(rowz, 16)

        def plan_route(n):
            return Plan(n, "vvv")

        def pe_route(pe, n):
            p = plan_route(n)
            pe.wait_ge(rparams, 64)
            for t in range(TL):
                for k in range(KT):
                    last = nc.tensor.matmul(bank(0)[:, 36 * t:36 * t + 36], hTk[:, k, 128 * t:128 * t + 128], rw[:, k, :],
                                            start=(k == 0), stop=(k == KT - 1))
            last.then_inc(mm_done, 1)
            n["v2p"] += 1
            pe.wait_ge(v2p, n["v2p"])
            oh = rt(2)
            for t in range(TL):
                for u in range(t + 1):
                    last = nc.tensor.matmul(bank(1)[:, 32 * t:32 * t + 32], C(C_US) if u == t else C(C_ONE), oh[:, u, :],
                                            start=(u == 0), stop=(u == t))
            last.then_inc(mm_done, 1)
            for u in range(TL):
                last = nc.tensor.matmul(bank(2)[:, 0:32], C(C_ONE), oh[:, u, :], start=(u == 0), stop=(u == TL - 1))
            last.then_inc(mm_done, 1)

        def act_route(act, n):
            plan_route(n)
            for src, dst in ((LG[:, :, 0:NG], rt(6, NG)), (sc(5), sc(6))):
                n["v2a"] += 1
                act.wait_ge(v2a, n["v2a"])
                act.activation(dst, src, ACT.Exp).then_inc(a2v, 1)

        def dve_route(dve, n):
            p = plan_route(n)
            V = nc.vector
            D_ = dve.drain

            def bc(a, w):
                return a.unsqueeze(2).broadcast_to([P, TL, w])

            def first(dst, src, mx, w):
                V.tensor_reduce(mx, src, AX, ALU.max)
                D_()
                V.tensor_tensor(rt(7, w), src, bc(mx, w), ALU.is_equal)
                D_()
                V.tensor_tensor(rt(8, w), rt(7, w), C(C_I32 + 32 - w, w).unsqueeze(1).broadcast_to([P, TL, w]), ALU.mult)
                D_()
                V.tensor_reduce(sc(9), rt(8, w), AX, ALU.max)
                D_()
                V.tensor_tensor(dst, rt(8, w), bc(sc(9), w), ALU.is_equal)
                D_()

            V.tensor_copy(TOK, C(C_TK, TL))
            dve.wait_ge(rparams, 64)
            dve.wait_ge(mm_done, p.done(0))
            V.tensor_tensor(LG, bank(0)[:, 0:36 * TL].rearrange("p (t n) -> p t n", t=TL), rb.unsqueeze(1).broadcast_to([P, TL, 36]),
                            ALU.add).then_inc(evac_v, 1)
            D_()
            g, e = LG[:, :, 0:NG], LG[:, :, NG:NG + NE]
            ohg, em, oh1, oh2, oh = rt(9, NG), rt(3), rt(0), rt(1), rt(2)
            first(ohg, g, sc(0), NG)
            V.tensor_tensor(g, g, bc(sc(0), NG), ALU.subtract).then_inc(v2a, 1)
            n["a2v"] += 1
            dve.wait_ge(a2v, n["a2v"])
            V.tensor_reduce(sc(1), rt(6, NG), AX, ALU.add)
            D_()
            V.reciprocal(sc(2), sc(1))
            V.tensor_scalar(rt(10, NG), ohg, -1.0, -NEG, ALU.add, ALU.mult)
            v4 = lambda a: a.rearrange("p t (g x) -> p (t g) x", g=NG)
            b4 = lambda a: a.rearrange("p t g -> p (t g)").unsqueeze(2).broadcast_to([P, TL * NG, 8])
            for t in range(TL):
                V.tensor_tensor(em[:, t, :].rearrange("p (g x) -> p g x", g=NG), e[:, t, :].rearrange("p (g x) -> p g x", g=NG),
                                ohg[:, t, :].unsqueeze(2).broadcast_to([P, NG, 8]), ALU.mult)
            D_()
            V.tensor_tensor(v4(em), v4(em), b4(rt(10, NG)), ALU.add)
            D_()
            first(oh1, em, sc(3), 32)
            V.scalar_tensor_tensor(em, oh1, 2 * NEG, em, ALU.mult, ALU.add)
            D_()
            first(oh2, em, sc(4), 32)
            V.tensor_tensor(oh, oh1, oh2, ALU.add).then_inc(v2p, 1)
            V.tensor_tensor(sc(5), sc(4), sc(3), ALU.subtract).then_inc(v2a, 1)
            n["a2v"] += 1
            dve.wait_ge(a2v, n["a2v"])
            V.tensor_scalar(sc(7), sc(6), 1.0, None, ALU.add)
            D_()
            V.reciprocal(sc(8), sc(7))
            D_()
            V.tensor_tensor(WT[0], sc(8), sc(2), ALU.mult)
            D_()
            V.tensor_tensor(WT[1], WT[0], sc(6), ALU.mult)
            cnt, ov, oe, A_ = (Z[:, 7900 + 32 * i:7932 + 32 * i] for i in range(4))
            pos, gq, slot = rt(4), rt(5), rt(6)
            dve.wait_ge(mm_done, p.done(2))
            V.tensor_copy(pos, bank(1)[:, 0:128].rearrange("p (t n) -> p t n", t=TL)).then_inc(evac_v, 1)
            V.tensor_copy(cnt, bank(2)[:, 0:32]).then_inc(evac_v, 1)
            D_()
            V.tensor_scalar(ov, cnt, float(CAP), None, ALU.is_gt)
            for k in range(2, TL * P // CAP):
                D_()
                V.scalar_tensor_tensor(ov, cnt, float(CAP * k), ov, ALU.is_gt, ALU.add)
            D_()
            V.tensor_tensor_scan(oe, C(C_ONE, 32), ov, 0.0, ALU.mult, ALU.add)
            D_()
            V.tensor_tensor(A_, oe, ov, ALU.subtract)
            D_()
            V.tensor_scalar(A_, A_, float(NE - 1), float(CAP), ALU.add, ALU.mult)
            D_()
            V.tensor_tensor(A_, A_, C(C_E64, 32), ALU.subtract)
            V.tensor_scalar(gq, pos, float(CAP), None, ALU.is_ge)
            D_()
            V.tensor_tensor(gq, gq, A_.unsqueeze(1).broadcast_to([P, TL, 32]), ALU.mult)
            V.tensor_tensor(slot, pos, C(C_E64, 32).unsqueeze(1).broadcast_to([P, TL, 32]), ALU.add)
            D_()
            V.tensor_tensor(slot, slot, gq, ALU.add)
            D_()
            for c, o in enumerate((oh1, oh2)):
                V.tensor_tensor(rt(7 + c), slot, o, ALU.mult)
            D_()
            for c in range(2):
                V.tensor_reduce(sc(10 + c), rt(7 + c), AX, ALU.add)
            D_()
            for c in range(2):
                last = V.tensor_copy(IDX[:, c, :], sc(10 + c))
            last.then_inc(idx_ok, 1)
            ef = Z[0:1, 8100:8148]
            cm = Z[0:1, 8200:8712].rearrange("p (j e) -> p j e", j=16)
            V.tensor_scalar(ef[:, 0:32], C(C_E64, 32)[0:1], 1.0 / CAP, None, ALU.mult)
            V.tensor_tensor(cm, oe[0:1].unsqueeze(1).broadcast_to([1, 16, 32]), C(C_ROW, 16)[0:1].unsqueeze(2).broadcast_to([1, 16, 32]), ALU.is_le)
            V.tensor_scalar(Z[0:1, 8150:8158], C(C_ROW, 16)[0:1, 0:16:2], oe[0:1, 31:32], None, ALU.is_lt)
            D_()
            V.tensor_reduce(ef[:, 32:48], cm, AX, ALU.add)
            V.tensor_reduce(Z[0:1, 8160:8161], Z[0:1, 8150:8158], AX, ALU.add)
            D_()
            V.tensor_scalar(ef[:, 32:48], ef[:, 32:48], float(NE - 1), None, ALU.min)
            V.tensor_scalar(NIT, Z[0:1, 8160:8161], float(NE // 2), None, ALU.add)
            D_()
            V.tensor_copy(EID, ef)

        def pool_route(pool):
            pool.wait_ge(idx_ok, 1)
            pool.wait_ge(rowz, 16)
            for c in range(2):
                for t in range(TL):
                    pool.indirect_dma_start(rowtok, bass.IndirectOffsetOnAxis(ap=IDX[:, c, t:t + 1].bitcast(U32), axis=0),
                                            TOK[:, t:t + 1], None).then_inc(scat, 16)
            pool.wait_ge(scat, 16 * 2 * TL)
            pool.dma_start(ROWS, rowtok.rearrange("(c p) a -> p (c a)", c=24), allow_slow_non_contiguous=True).then_inc(rows_in, 16)
            pool.wait_ge(rows_in, 16)

        mslot = [ring[:, 0:HALF], ring[:, HALF:2 * HALF]] + [pj[:, HALF * i:HALF * i + HALF] for i in range(4)]
        xg = Z[:, 0:1024]
        xgT = Z[:, 1024:2048].rearrange("p (k n) -> p k n", k=KT)
        hg, hu, hd, yo = Z[:, 2048:2560], Z[:, 2560:3072], Z[:, 3072:3584], Z[:, 3584:4608]
        WE = [I["expert_w_gate"][0], I["expert_w_up"][0], I["expert_w_down"][0]]

        def trips(eng):
            return eng.value_load(NIT, min_val=NE // 2, max_val=NBLK // 2)

        def load_expert(sp, m, x, e):
            dst = mslot[2 * m + x].rearrange("p (k n) -> p k n", n=EH if m < 2 else D)
            sp.dma_start(dst, WE[m][e].rearrange("a (k p) n -> p (a k) n", p=P)).then_inc(w_in_[2 * m + x], 16)

        def sp_moe(sp):
            with sp.Fori(1, trips(sp)) as i:
                e = [sp.value_load(EID[:, bass.ds(2 * i + x, 1)], min_val=0, max_val=NE - 1) for x in range(2)]
                for m in range(3):
                    sp.wait_ge(w_used[m], i + 1)
                    for x in range(2):
                        load_expert(sp, m, x, bass.ds(e[x], 1))

        def pool_moe(pool):
            with pool.Fori(0, trips(pool)) as i:
                pool.wait_ge(xt_done, 2 * i + 2)
                pool.tensor_copy(IDC, ROWS[:, bass.ds(i, 1)])
                pool.drain()
                pool.indirect_dma_start(xg, None, xnd, bass.IndirectOffsetOnAxis(ap=IDC.bitcast(U32), axis=0)).then_inc(xg_in, 16)

        def pe_moe(pe):
            nit = trips(pe)
            for s in w_used:
                pe.sem_inc(s, 1)
            pe.sem_inc(xt_done, 2)
            with pe.Fori(0, nit) as i:
                pe.wait_ge(xg_in, 16 * i + 16)
                for b in range(2):
                    for k in range(4):
                        last = nc.tensor.transpose(bank(b)[:, 128 * k:128 * k + 128], xg[:, 512 * b + 128 * k:512 * b + 128 * k + 128], ident)
                    last.then_inc(xt_done, 1)
                pe.wait_ge(xt_a, i + 1)
                pe.wait_ge(xt_v, i + 1)
                for m in range(2):
                    for x in range(2):
                        pe.wait_ge(w_in_[2 * m + x], 16 * i + 16)
                    for k in range(KT):
                        for x in range(2):
                            last = nc.tensor.matmul(bank(2 + m)[64 * x:64 * x + 64, :], xgT[:, k, 64 * x:64 * x + 64],
                                                    mslot[2 * m + x][:, 512 * k:512 * k + 512], start=(k == 0), stop=(k == KT - 1))
                    last.then_inc(w_used[m], 1)
                pe.wait_ge(hu_ok, i + 1)
                for k in range(4):
                    last = nc.tensor.transpose(bank(4)[:, 128 * k:128 * k + 128], hu[:, 128 * k:128 * k + 128], ident)
                last.then_inc(ht_done, 1)
                pe.wait_ge(ht_a, i + 1)
                for x in range(2):
                    pe.wait_ge(w_in_[4 + x], 16 * i + 16)
                for b in range(2):
                    for k in range(4):
                        for x in range(2):
                            last = nc.tensor.matmul(bank(5 + b)[64 * x:64 * x + 64, :], hd[:, 128 * k + 64 * x:128 * k + 64 * x + 64],
                                                    mslot[4 + x][:, 1024 * k + 512 * b:1024 * k + 512 * b + 512], start=(k == 0), stop=(k == 3))
                last.then_inc(w_used[2], 1)

        def act_moe(act):
            nit = trips(act)
            with act.Fori(0, nit) as i:
                act.wait_ge(xt_done, 2 * i + 3)
                for k in range(4):
                    last = act.activation(xgT[:, k, :], bank(0)[:, 128 * k:128 * k + 128], ACT.Identity,
                                          scale=Ac[:, 0, 0, 1, k:k + 1], bias=modc[:, 0, 24 + k:25 + k])
                last.then_inc(xt_a, 1)
                act.wait_ge(w_used[0], i + 2)
                act.activation(hg, bank(2), ACT.Silu).then_inc(silu_ok, 1)
                act.wait_ge(ht_done, i + 1)
                act.activation(hd, bank(4), ACT.Copy).then_inc(ht_a, 1)
                act.wait_ge(w_used[2], i + 2)
                act.wait_ge(y_out, 16 * i + 16)
                act.activation(yo[:, 0:512], bank(5), ACT.Copy).then_inc(y_a, 1)
                act.wait_ge(y_a, i + 1)
                act.wait_ge(y_v, i + 1)
                act.dma_start(ybuf[bass.ds(i * P, P), :], yo).then_inc(y_out, 16)
            act.wait_ge(y_out, 16 * nit + 16)
            act.sem_inc(y_stored, 1)

        def dve_moe(dve):
            with dve.Fori(0, trips(dve)) as i:
                dve.wait_ge(xt_done, 2 * i + 4)
                for k in range(4):
                    last = nc.vector.tensor_scalar(xgT[:, 4 + k, :], bank(1)[:, 128 * k:128 * k + 128], Ac[:, 0, 0, 1, 4 + k:5 + k],
                                                   modc[:, 0, 28 + k:29 + k], ALU.mult, ALU.add)
                last.then_inc(xt_v, 1)
                dve.wait_ge(silu_ok, i + 1)
                dve.wait_ge(w_used[1], i + 2)
                nc.vector.tensor_tensor(hu, hg, bank(3), ALU.mult).then_inc(hu_ok, 1)
                dve.wait_ge(w_used[2], i + 2)
                dve.wait_ge(y_out, 16 * i + 16)
                nc.vector.tensor_copy(yo[:, 512:1024], bank(6)).then_inc(y_v, 1)

        yg = [[Z[:, 1024 * (2 * i + c):1024 * (2 * i + c) + 1024] for c in range(2)] for i in range(2)]
        fng = Z[:, 4608:5632]

        def pool_comb(pool, n):
            for t in range(TL):
                if t >= 2:
                    pool.wait_ge(yg_free, t - 1)
                for c in range(2):
                    pool.indirect_dma_start(yg[t % 2][c], None, ybuf, bass.IndirectOffsetOnAxis(ap=IDX[:, c, t:t + 1].bitcast(U32), axis=0)
                                            ).then_inc(yg_in[t % 2], 16)

        def dve_comb(dve, n):
            n["gate"] += 32
            dve.wait_ge(gate_in, n["gate"])
            for t in range(TL):
                dve.wait_ge(yg_in[t % 2], 32 * (t // 2 + 1))
                y0, y1 = yg[t % 2]
                nc.vector.tensor_scalar(y0, y0, WT[0][:, t:t + 1], None, ALU.mult)
                dve.drain()
                nc.vector.scalar_tensor_tensor(y0, y1, WT[1][:, t:t + 1], y0, ALU.mult, ALU.add)
                dve.drain()
                nc.vector.tensor_tensor(y0, y0, gtb[:, 0, :], ALU.mult)
                dve.drain()
                nc.vector.tensor_tensor(xl[:, t, :], xl[:, t, :], y0, ALU.add).then_inc(yg_free, 1)

        def act_final(act, n):
            act.wait_ge(yg_free, TL)
            for t in range(TL):
                act.activation(junk, xl[:, t, :], ACT.Square, accum_out=st[:, t:t + 1])
                act.drain()
            act.activation(st[:, 16:20], st[:, 0:4], ACT.Copy).then_inc(sumsq, 1)
            n["var"] += 1
            act.wait_ge(var, n["var"])
            act.activation(st[:, 24:28], st[:, 8:12], ACT.Sqrt).then_inc(std, 1)

        def dve_final(dve, n):
            n["ss"] += 1
            dve.wait_ge(sumsq, n["ss"])
            nc.vector.tensor_scalar(st[:, 8:12], st[:, 16:20], 1.0 / D, EPS, ALU.mult, ALU.add).then_inc(var, 1)
            n["std"] += 1
            dve.wait_ge(std, n["std"])
            nc.vector.reciprocal(st[:, 32:36], st[:, 24:28])
            dve.drain()
            for t in range(TL):
                nc.vector.scalar_tensor_tensor(xl[:, t, :], xl[:, t, :], st[:, 32 + t:33 + t], fng, ALU.mult, ALU.mult)

        TQ = (ALLT, LAT)
        BL2 = [[(NK, NV, ALLT, "a"), (NQ, GU, TQ[l], "a"), (GMV, CQ, TQ[l], "a"), (CQ, GATES, TQ[l], "a"), (CKV, NQ, ALLT, "a"),
                (GU, GMV, TQ[l], "a"), (NV, CKV, ALLT, "a")] for l in range(2)]
        lng, lnb = Z[:, 8588:9100], Z[:, 9100:9612]
        cqg, ckg, qg, kg = Z[:, 9612:9868], Z[:, 9868:9996], Z[:, 9996:10092], Z[:, 10092:10188]
        wsr = Z[:, 10188:10700].rearrange("p (g q) -> p g q", g=4)
        wsT = Z[:, 8076:8588]
        rpt = Z[:, 7948:8076]
        tbt = [hT[:, 0:1792], hT[:, 1792:3584]]
        Qf = hT[:, 0:4608].rearrange("p (t n) -> p t n", t=TA)
        cqT = Z[:, 0:1536].rearrange("p (k n) -> p k n", k=2)
        ckT = Z[:, 1536:2304].rearrange("p (k n) -> p k n", k=1)
        rpbd = nc.dram_tensor("rpbd", (2, 120, 64 * P), F32, kind="Internal")

        def pool_params2(pool, l):
            for dst, name in ((lng, "gm_ln_g_2"), (lnb, "gm_ln_b_2"), (cqg, "mla_cq_gain_2"), (ckg, "mla_ckv_gain_2"),
                              (qg, "mla_q_gain_2"), (kg, "mla_k_gain_2")):
                pool.dma_start(dst, I[name][l].partition_broadcast(P)).then_inc(prm2, 16)
            pool.dma_start(wsr, I["gm_w_s_2"][l].rearrange("g p q -> p g q")).then_inc(prm2, 16)
            pool.memset(rpt, 0.0).then_inc(rp_ok, 1)
            pool.wait_ge(rp_ok, l + 1)
            pool.dma_start(rpt[0:120, 48:79], I["na_rpb_2"][l].rearrange("h r c -> (h r) c")).then_inc(rp_in, 16)
            pool.wait_ge(rp_in, 32 * l + 16)
            pool.dma_start(rpbd.ap()[l].rearrange("r (m n) -> r m n", n=P), rpt[0:120, :].unsqueeze(1).broadcast_to([120, 64, P])).then_inc(rp_in, 16)
            pool.wait_ge(rp_in, 32 * l + 32)

        def pool_bias(pool, l, pairs):
            for q in pairs:
                if q >= 2:
                    pool.wait_ge(tb_free, 4 * l + q - 1)
                t4 = tbt[q % 2].rearrange("p (h j c) -> p h j c", h=2, j=14)
                for h in range(2):
                    for half in range(2):
                        off = (l * 120 + (2 * q + h) * 15 + 1 - half) * 64 * P + 63
                        src = bass.AP(tensor=rpbd, offset=off, ap=[[P - 1, 64], [64 * P, 14], [1, 64]])
                        pool.dma_start(t4[64 * half:64 * half + 64, h], src).then_inc(tb_in[q % 2], 16)
                pool.wait_ge(tb_in[q % 2], 64 * (2 * l + q // 2 + 1))
                m = C(C_NM, 64).unsqueeze(1).broadcast_to([P, 28, 64])
                b = C(C_NB, 64).unsqueeze(1).broadcast_to([P, 28, 64])
                t3 = tbt[q % 2].rearrange("p (j c) -> p j c", c=64)
                pool.tensor_tensor(t3, t3, m, ALU.mult)
                pool.drain()
                pool.tensor_tensor(t3, t3, b, ALU.add).then_inc(tb_ok, 1)

        def act_project(act, n, l):
            p = plan_lin(n, BL2[l])
            i = 0
            for j, (c0, c1, ts, _) in enumerate(BL2[l]):
                for m, t in enumerate(ts):
                    if j == 5 and m == 2:
                        rms_heads(act, "a", n, ALLT, hv(CKV, 1, 128), 1, 128, ckg)
                    act.wait_ge(mm_done, p.done(i))
                    f = ACT.Gelu if c0 in (GU, GMV) else ACT.Copy
                    act.activation(pjt[:, t, c0:c1], bank(i % 8, c1 - c0), f).then_inc(evac_a, 1)
                    i += 1
                if j == 1:
                    rms_heads(act, "a", n, ALLT, hv(NK, 8, 64), 8, 64, None)
                elif j == 2:
                    rms_heads(act, "a", n, TQ[l], hv(NQ, 8, 64), 8, 64, None)
                elif j == 3:
                    n["var"] += 1
                    act.wait_ge(var, n["var"])
                    act.activation(st[:, 320:320 + len(TQ[l])], st[:, 260:260 + len(TQ[l])], ACT.Sqrt).then_inc(std, 1)
                elif j == 4:
                    rms_heads(act, "a", n, TQ[l], hv(CQ, 1, 256), 1, 256, cqg)

        def dve_project(dve, n, l):
            V = nc.vector
            p = plan_lin(n, BL2[l])
            ends, i = [], 0
            for b in BL2[l]:
                i += len(b[2])
                ends.append(p.val[i - 1])
            nt = len(TQ[l])
            dve.wait_ge(prm2, 16 * 7 * (l + 1))
            dve.wait_ge(evac_a, ends[0])
            rms_heads(dve, "v", n, ALLT, hv(NK, 8, 64), 8, 64, None)
            dve.drain()
            dve.wait_ge(evac_a, ends[1])
            rms_heads(dve, "v", n, TQ[l], hv(NQ, 8, 64), 8, 64, None)
            dve.drain()
            dve.wait_ge(evac_a, ends[2])
            vv = lambda t: pjt[:, t, GMV:GMV + 512]
            sq = [Z[:, 0:512], Z[:, 512:1024]]
            for t in TQ[l]:
                V.tensor_reduce(st[:, 500 + t:501 + t], vv(t), AX, ALU.add)
            dve.drain()
            V.tensor_scalar(st[:, 510:510 + nt], st[:, 500:500 + nt], 1.0 / 512, None, ALU.mult)
            dve.drain()
            for t in TQ[l]:
                V.tensor_scalar(vv(t), vv(t), st[:, 510 + t:511 + t], None, ALU.subtract)
            dve.drain()
            for t in TQ[l]:
                V.tensor_tensor(sq[t % 2], vv(t), vv(t), ALU.mult)
                dve.drain()
                V.tensor_reduce(st[:, 200 + t:201 + t], sq[t % 2], AX, ALU.add)
            dve.drain()
            V.tensor_scalar(st[:, 260:260 + nt], st[:, 200:200 + nt], 1.0 / 512, EPS, ALU.mult, ALU.add).then_inc(var, 1)
            n["std"] += 1
            dve.wait_ge(std, n["std"])
            V.reciprocal(st[:, 380:380 + nt], st[:, 320:320 + nt])
            dve.drain()
            for t in TQ[l]:
                V.scalar_tensor_tensor(vv(t), vv(t), st[:, 380 + t:381 + t], lng, ALU.mult, ALU.mult)
            dve.drain()
            for t in TQ[l]:
                V.tensor_tensor(vv(t), vv(t), lnb, ALU.add)
            dve.drain()
            dve.wait_ge(evac_a, ends[3])
            rms_heads(dve, "v", n, TQ[l], hv(CQ, 1, 256), 1, 256, cqg)
            dve.drain()
            dve.wait_ge(evac_a, ends[4])
            rms_heads(dve, "v", n, ALLT, hv(CKV, 1, 128), 1, 128, ckg)

        def na_spec(l):
            def src(q):
                return lambda side, t: pjt[:, t, (NK if side == "k" else NQ) + 128 * q:(NK if side == "k" else NQ) + 128 * q + 128]

            def gain(side):
                r = (R_NAK if side == "k" else R_NAQ) + l
                return cols[:, r:r + 1]

            def biased(q, h, t):
                def f(E, b):
                    nc.vector.scalar_tensor_tensor(E[:, 0:512], b[:, 0:512], 64 ** -0.5,
                                                   tbt[q % 2][:, 896 * (h % 2) + 64 * (6 - 2 * t):896 * (h % 2) + 64 * (6 - 2 * t) + 512],
                                                   ALU.mult, ALU.add)
                    return nc.vector.tensor_scalar(E[:, 512:768], b[:, 512:768], 64 ** -0.5, None, ALU.mult)
                return f
            heads = [(P, src(q), TQ[l], gain) for q in range(4)]
            units = [dict(head=h // 2, rows=((64 * (h % 2), 64 * (h % 2) + 64),), qt=t, keys=ALLT if t < TL else (4, 5),
                          bias=biased(h // 2, h, t) if t < TL else None, scale=64 ** -0.5, combine=False,
                          v=lambda kt, h=h: pjt[:, kt, NV + 64 * h:NV + 64 * h + 64], dv=64,
                          y=pjt[:, t, NQ + 64 * h:NQ + 64 * h + 64]) for h in range(8) for t in TQ[l]]
            return heads, units

        def mla_spec(l):
            def src(h):
                return lambda side, t: pjt[:, t, GMV + 96 * h:GMV + 96 * h + 96] if side == "k" else Qf[:, t, 96 * h:96 * h + 96]
            heads = [(96, src(h), TQ[l], None) for h in range(8)]
            units = [dict(head=h, rows=((0, 96),), qt=t, keys=ALLT if t < TL else (4, 5), bias=None, scale=96 ** -0.5, combine=False,
                          v=lambda kt, h=h: pjt[:, kt, 128 * h + 64:128 * h + 128], dv=64,
                          y=Qf[:, t, 64 * h:64 * h + 64]) for h in range(8) for t in TQ[l]]
            return heads, units

        def plan_gm(n, l):
            return Plan(n, "a" + "v" * len(TQ[l]))

        def pe_gm(pe, n, l):
            p = plan_gm(n, l)
            pe.wait_ge(prm2, 16 * 7 * (l + 1))
            for g in range(4):
                last = nc.tensor.transpose(bank(7)[:, P * g:P * g + P], wsr[:, g, :], ident)
            last.then_inc(mm_done, 1)
            pe.wait_ge(evac_a, p.val[0])
            for i, t in enumerate(TQ[l]):
                for g in range(4):
                    last = nc.tensor.matmul(bank(i)[:, P * g:P * g + P], wsT[:, P * g:P * g + P], pjt[:, t, GMV + P * g:GMV + P * g + P],
                                            start=True, stop=True)
                last.then_inc(mm_done, 1)

        def act_gm(act, n, l):
            p = plan_gm(n, l)
            act.wait_ge(mm_done, p.done(0))
            act.activation(wsT, bank(7), ACT.Copy).then_inc(evac_a, 1)

        def dve_gm(dve, n, l):
            p = plan_gm(n, l)
            for i, t in enumerate(TQ[l]):
                dve.wait_ge(mm_done, p.done(1 + i))
                for g in range(4):
                    u = pjt[:, t, GU + P * g:GU + P * g + P]
                    last = nc.vector.scalar_tensor_tensor(u, bank(i)[:, P * g:P * g + P], cols[:, R_BS + 4 * l + g:R_BS + 4 * l + g + 1], u,
                                                          ALU.add, ALU.mult)
                last.then_inc(evac_v, 1)

        def plan_t(n, pairs):
            return Plan(n, ("av" * len(pairs))[:-(-len(pairs) // 4)])

        def pe_t(pe, n, pairs):
            p = plan_t(n, pairs)
            for i in range(len(p.own)):
                if i >= 8:
                    pe.wait_ge(EV[p.own[i - 8]], p.val[i - 8])
                for j, (src, _) in enumerate(pairs[4 * i:4 * i + 4]):
                    last = nc.tensor.transpose(bank(i % 8)[:, P * j:P * j + P], src, ident)
                last.then_inc(mm_done, 1)

        def each_t(eng, n, who, pairs):
            p = plan_t(n, pairs)
            for i in range(len(p.own)):
                if p.own[i] == who:
                    eng.wait_ge(mm_done, p.done(i))
                    for j, (_, dst) in enumerate(pairs[4 * i:4 * i + 4]):
                        b = bank(i % 8)[:, P * j:P * j + P]
                        last = nc.scalar.activation(dst, b, ACT.Copy) if who == "a" else nc.vector.tensor_copy(dst, b)
                    last.then_inc(EV[who], 1)

        def cqkv_pairs(l):
            return ([(pjt[:, t, CQ + P * k:CQ + P * k + P], cqT[:, k, P * t:P * t + P]) for t in TQ[l] for k in range(2)]
                    + [(pjt[:, t, CKV:CKV + P], ckT[:, 0, P * t:P * t + P]) for t in ALLT])

        def BUQ(l):
            return [(0, 512, TQ[l]), (512, 768, TQ[l])]

        BUKV = [(0, 512, ALLT), (512, 1024, ALLT)]
        q_lhs = lambda k, t: 2 if k is None else cqT[:, k, P * t:P * t + P]
        kv_lhs = lambda k, t: 1 if k is None else ckT[:, 0, P * t:P * t + P]
        act_q = lambda c0, c1, t, b: nc.scalar.activation(Qf[:, t, c0:c1], b, ACT.Copy)
        dve_q = lambda c0, c1, t, b: nc.vector.tensor_copy(Qf[:, t, c0:c1], b)

        kview = lambda t: pjt[:, t, GMV:GMV + 768].rearrange("p (h d) -> p h d", h=8)
        qview = lambda t: Qf[:, t, :].rearrange("p (h d) -> p h d", h=8)

        def dve_mla(dve, n, l):
            V = nc.vector
            for t in ALLT:
                V.tensor_copy(kview(t)[:, :, 0:64], pjt[:, t, 0:1024].rearrange("p (h d) -> p h d", h=8)[:, :, 0:64])
                V.tensor_copy(kview(t)[:, :, 64:96], pjt[:, t, KR:KR + 32].unsqueeze(1).broadcast_to([P, 8, 32]))
            dve.drain()
            rms_heads(dve, "v", n, TQ[l], qview, 8, 96, qg)
            dve.drain()
            rms_heads(dve, "v", n, ALLT, kview, 8, 96, kg)
            dve.drain()
            for t in LAT:
                for i, v in enumerate((qview, kview)):
                    x = 512 * ((2 * t + i) % 4)
                    dve_rope(dve, t, v(t)[:, :, 64:96], 8, 8, C_R2C, C_R2S, Z[:, x:x + 256], Z[:, x + 256:x + 512])

        def act_mla(act, n, l):
            rms_heads(act, "a", n, TQ[l], qview, 8, 96, qg)
            rms_heads(act, "a", n, ALLT, kview, 8, 96, kg)

        yT = [Z[:, 0:3072].rearrange("p (k n) -> p k n", k=4), Z[:, 3072:6144].rearrange("p (k n) -> p k n", k=4),
              pj[:, 0:3072].rearrange("p (k n) -> p k n", k=4)]
        acc = pj[:, 3072:3072 + TA * D].rearrange("p (t n) -> p t n", t=TA)

        def nagm_pairs(l):
            return [(pjt[:, t, c + P * k:c + P * k + P], yT[b][:, k, P * t:P * t + P])
                    for t in TQ[l] for b, c in ((0, NQ), (1, GU)) for k in range(4)]

        def mla_pairs(l):
            return [(Qf[:, t, P * k:P * k + P], yT[2][:, k, P * t:P * t + P]) for t in TQ[l] for k in range(4)]

        sg = [Z[:, 6144:6656], Z[:, 6656:7168]]
        mtmp = [Z[:, 7168:7680], Z[:, 7680:8192]]
        WO = ("na_w_o_2", "gm_w_o_2", "mla_w_o_2")

        def plan_merge(n, l):
            return Plan(n, "av" * (6 * len(TQ[l])))

        mring = [ring[:, 2048 * i:2048 * i + 2048] for i in range(4)] + [Z[:, 8192:10240]]

        def sp_merge(sp, n, rel, l):
            p = plan_merge(n, l)
            nt = len(TQ[l])
            for x in range(18):
                j, y = x // 3, x % 3
                nb, b = j // 3, j % 3
                if x >= 5:
                    sp.wait_ge(mm_done, p.done(2 * nt * ((x - 5) // 3 + 1) - (1 if (x - 5) % 3 == 2 else 2)))
                elif x < 4 and rel[x // 2]:
                    sp.wait_ge(mm_done, rel[x // 2])
                if y < 2:
                    w = I["w_in_2"][l][512 * y:512 * y + 512, GATES + D * b + 512 * nb:GATES + D * b + 512 * nb + 512]
                else:
                    w = I[WO[b]][l][:, 512 * nb:512 * nb + 512]
                sp.dma_start(mring[x % 5].rearrange("p (k n) -> p k n", n=512), w.rearrange("(k p) n -> p k n", p=P)).then_inc(mring_in[x % 5], 16)
            rel[0] = rel[1] = p.done(12 * nt - 1)

        def pe_merge(pe, n, l):
            p = plan_merge(n, l)
            i = 0
            for j in range(6):
                w = [mring[(3 * j + y) % 5] for y in range(3)]
                for y in range(3):
                    x = 3 * j + y
                    pe.wait_ge(mring_in[x % 5], 16 * ((4 if x % 5 < 3 else 3) * l + x // 5 + 1))
                for t in TQ[l]:
                    for g in range(2):
                        if i >= 8:
                            pe.wait_ge(EV[p.own[i - 8]], p.val[i - 8])
                        for k in range((8, 4)[g]):
                            lhs, r = (h_lhs(k, t), w[k // 4]) if g == 0 else (yT[j % 3][:, k, P * t:P * t + P], w[2])
                            last = nc.tensor.matmul(bank(i % 8), lhs, r[:, 512 * (k % 4):512 * (k % 4) + 512], start=(k == 0), stop=(k == (7, 3)[g]))
                        last.then_inc(mm_done, 1)
                        i += 1

        def act_merge(act, n, l):
            p = plan_merge(n, l)
            for u in range(6 * len(TQ[l])):
                act.wait_ge(mm_done, p.done(2 * u))
                if u >= 2:
                    act.wait_ge(evac_v, p.val[2 * u - 3])
                act.activation(sg[u % 2], bank((2 * u) % 8), ACT.Sigmoid).then_inc(evac_a, 1)

        def dve_merge(dve, n, l):
            p = plan_merge(n, l)
            nt = len(TQ[l])
            for u in range(6 * nt):
                j, t = u // nt, u % nt
                nb, b = j // 3, j % 3
                dve.wait_ge(evac_a, p.val[2 * u])
                dve.wait_ge(mm_done, p.done(2 * u + 1))
                a = acc[:, t, 512 * nb:512 * nb + 512]
                dst = a if b == 0 else mtmp[u % 2]
                nc.vector.tensor_tensor(dst, sg[u % 2], bank((2 * u + 1) % 8), ALU.mult).then_inc(evac_v, 1)
                if b:
                    dve.drain()
                    nc.vector.tensor_tensor(a, a, mtmp[u % 2], ALU.add)

        h1 = [pj[:, 6144 + 3072 * i:9216 + 3072 * i].rearrange("p (m n) -> p m n", m=4) for i in range(2)]
        yacc = pj[:, 0:6144].rearrange("p (t n) -> p t n", t=TA)
        rl = [Z[:, 0:512], Z[:, 512:1024]]

        def plan_ffn(n, l):
            s = 2 if len(TQ[l]) > TL else 1
            h, y = "a" * (4 * s), "v" * (2 * len(TQ[l]))
            return Plan(n, h + (h + y) * 7 + y)

        def ffn_order(l):
            nh, ny = 4 * (2 if len(TQ[l]) > TL else 1), 2 * len(TQ[l])
            steps = [("h", 0)] + [s for hb in range(1, 8) for s in (("h", hb), ("y", hb - 1))] + [("y", 7)]
            at, out = 0, []
            for kind, hb in steps:
                out.append((kind, hb, at))
                at += nh if kind == "h" else ny
            return out, nh, ny

        def sp_ffn(sp, n, rel, l):
            p = plan_ffn(n, l)
            order, nh, ny = ffn_order(l)
            for kind, hb, at in order:
                w, d = (I["ffn_w1_2"][l][:, 512 * hb:512 * hb + 512], 512) if kind == "h" else (I["ffn_w2_2"][l][512 * hb:512 * hb + 512, :], D)
                c = n["chunk"]
                load_chunk(sp, n, lambda s, d=d: s.rearrange("p (k n) -> p k n", n=d), w.rearrange("(k p) n -> p k n", p=P), rel)
                rel[c % 2] = p.done(at + (nh if kind == "h" else ny) - 1)

        def pe_ffn(pe, n, l):
            p = plan_ffn(n, l)
            order, nh, ny = ffn_order(l)
            last_h = {hb: p.val[at + nh - 1] for kind, hb, at in order if kind == "h"}
            for kind, hb, i in order:
                w = take_chunk(pe, n)
                if kind == "h":
                    for m in range(4):
                        for c0, c1 in ((0, 512), (512, 768))[:nh // 4]:
                            if i >= 8:
                                pe.wait_ge(EV[p.own[i - 8]], p.val[i - 8])
                            for k in range(KT):
                                last = nc.tensor.matmul(bank(i % 8, c1 - c0), w[:, 512 * k + P * m:512 * k + P * m + P], hTk[:, k, c0:c1],
                                                        start=(k == 0), stop=(k == KT - 1))
                            last.then_inc(mm_done, 1)
                            i += 1
                else:
                    pe.wait_ge(evac_a, last_h[hb])
                    for t in TQ[l]:
                        for b in range(2):
                            pe.wait_ge(EV[p.own[i - 8]], p.val[i - 8])
                            for k in range(4):
                                last = nc.tensor.matmul(bank(i % 8), h1[hb % 2][:, k, P * t:P * t + P], w[:, D * k + 512 * b:D * k + 512 * b + 512],
                                                        start=(k == 0), stop=(k == 3))
                            last.then_inc(mm_done, 1)
                            i += 1

        def act_ffn(act, n, l):
            p = plan_ffn(n, l)
            order, nh, ny = ffn_order(l)
            for kind, hb, g in order:
                if kind == "y":
                    continue
                if hb >= 2:
                    act.wait_ge(mm_done, p.done(g - 1))
                for m in range(4):
                    for c0, c1 in ((0, 512), (512, 768))[:nh // 4]:
                        act.wait_ge(mm_done, p.done(g))
                        act.activation(rl[g % 2][:, 0:c1 - c0], bank(g % 8, c1 - c0), ACT.Relu)
                        act.drain()
                        act.activation(h1[hb % 2][:, m, c0:c1], rl[g % 2][:, 0:c1 - c0], ACT.Square).then_inc(evac_a, 1)
                        g += 1

        def dve_ffn(dve, n, l):
            p = plan_ffn(n, l)
            order, nh, ny = ffn_order(l)
            for kind, hb, g in order:
                if kind == "h":
                    continue
                for t in TQ[l]:
                    for b in range(2):
                        dve.wait_ge(mm_done, p.done(g))
                        y = yacc[:, t, 512 * b:512 * b + 512]
                        if hb == 0:
                            nc.vector.tensor_copy(y, bank(g % 8)).then_inc(evac_v, 1)
                        else:
                            nc.vector.tensor_tensor(y, y, bank(g % 8), ALU.add).then_inc(evac_v, 1)
                        g += 1
                dve.drain()
            n["gate"] += 32
            dve.wait_ge(gate_in, n["gate"])
            for t in TQ[l]:
                nc.vector.tensor_tensor(yacc[:, t, :], yacc[:, t, :], gtb[:, t // TL, :], ALU.mult)
            dve.drain()
            for t in TQ[l]:
                nc.vector.tensor_tensor(xl[:, t, :], xl[:, t, :], yacc[:, t, :], ALU.add)

        def WO2(l):
            return [(0, 512, TQ[l], "v"), (512, 1024, TQ[l], "v")]

        def acc_pairs(l):
            return [(acc[:, t, P * k:P * k + P], hTk[:, k, P * t:P * t + P]) for t in TQ[l] for k in range(KT)]

        STAGES2 = 16

        def sp_layer(sp, n, rel, l):
            f0 = n["fence"]
            plan_norm(n, TA)
            sp_lin(sp, n, rel, I["w_in_2"][l], BL2[l])
            plan_attn(n, *na_spec(l))
            plan_gm(n, l)
            plan_t(n, cqkv_pairs(l))
            sp_lin(sp, n, rel, I["mla_w_uq_2"][l], BUQ(l))
            sp_lin(sp, n, rel, I["mla_w_ukv_2"][l], BUKV)
            plan_attn(n, *mla_spec(l))
            plan_t(n, nagm_pairs(l))
            plan_t(n, mla_pairs(l))
            sp.wait_ge(stage_done, f0 + 4 * 9)
            sp.dma_start(hT[:, 4608:6144], hTd[:, 4608:6144]).then_inc(unspill, 16)
            sp.wait_ge(stage_done, f0 + 4 * 11)
            sp.dma_start(hT[:, 0:4608], hTd[:, 0:4608]).then_inc(unspill, 16)
            sp_merge(sp, n, rel, l)
            plan_t(n, acc_pairs(l))
            sp_lin(sp, n, rel, I["w_out_2"][l], WO2(l))
            plan_norm(n, len(TQ[l]))
            sp_ffn(sp, n, rel, l)
            n["fence"] = f0 + 4 * STAGES2

        def plan_attn(n, heads, units):
            Attn(n, heads, units)

        def pool_layer(pool, n, l):
            pool_params2(pool, l)
            fence(pool, n)
            fence(pool, n)
            pool.wait_ge(spill, 16 * (l + 1))
            pool_bias(pool, l, (0, 1))
            pool_bias(pool, l, (2, 3))
            for _ in range(10):
                fence(pool, n)
            load_gate(pool, l + 1, 2)
            fence(pool, n)
            fence(pool, n)
            load_gate(pool, l + 1, 5)
            fence(pool, n)
            fence(pool, n)

        def pe_layer(pe, n, l):
            pe_norm(pe, n, TA)
            fence(pe, n)
            pe_lin(pe, n, BL2[l], h_lhs)
            fence(pe, n)
            pe_attn(pe, n, *na_spec(l))
            fence(pe, n)
            pe_gm(pe, n, l)
            fence(pe, n)
            pe_t(pe, n, cqkv_pairs(l))
            fence(pe, n)
            pe_lin(pe, n, BUQ(l), q_lhs)
            fence(pe, n)
            pe_lin(pe, n, BUKV, kv_lhs)
            fence(pe, n)
            fence(pe, n)
            pe_attn(pe, n, *mla_spec(l))
            fence(pe, n)
            pe_t(pe, n, nagm_pairs(l))
            fence(pe, n)
            pe_t(pe, n, mla_pairs(l))
            fence(pe, n)
            pe.wait_ge(unspill, 32 * (l + 1))
            pe_merge(pe, n, l)
            fence(pe, n)
            pe_t(pe, n, acc_pairs(l))
            fence(pe, n)
            pe_lin(pe, n, WO2(l), h_lhs)
            fence(pe, n)
            pe_norm(pe, n, len(TQ[l]))
            fence(pe, n)
            pe_ffn(pe, n, l)
            fence(pe, n)

        def act_layer(act, n, l):
            act_norm(act, n, TA, l + 1, 0)
            fence(act, n)
            act.dma_start(hTd, hT[:, :]).then_inc(spill, 16)
            act_project(act, n, l)
            act.wait_ge(spill, 16 * (l + 1))
            fence(act, n)
            act_attn(act, n, *na_spec(l))
            fence(act, n)
            act_gm(act, n, l)
            fence(act, n)
            each_t(act, n, "a", cqkv_pairs(l))
            fence(act, n)
            each_lin(act, n, BUQ(l), "a", act_q)
            fence(act, n)
            each_lin(act, n, BUKV, "a", act_put)
            fence(act, n)
            act_mla(act, n, l)
            fence(act, n)
            act_attn(act, n, *mla_spec(l))
            fence(act, n)
            each_t(act, n, "a", nagm_pairs(l))
            fence(act, n)
            each_t(act, n, "a", mla_pairs(l))
            fence(act, n)
            act_merge(act, n, l)
            fence(act, n)
            each_t(act, n, "a", acc_pairs(l))
            fence(act, n)
            plan_lin(n, WO2(l))
            fence(act, n)
            act_norm(act, n, len(TQ[l]), l + 1, 1)
            fence(act, n)
            act_ffn(act, n, l)
            fence(act, n)

        def dve_layer(dve, n, l):
            dve_norm(dve, n, TA, l + 1, 0)
            fence(dve, n)
            dve_project(dve, n, l)
            fence(dve, n)
            dve_attn(dve, n, *na_spec(l), tables=4 * l)
            fence(dve, n)
            dve_gm(dve, n, l)
            fence(dve, n)
            each_t(dve, n, "v", cqkv_pairs(l))
            fence(dve, n)
            each_lin(dve, n, BUQ(l), "v", dve_q)
            fence(dve, n)
            each_lin(dve, n, BUKV, "v", dve_put)
            fence(dve, n)
            dve_mla(dve, n, l)
            fence(dve, n)
            dve_attn(dve, n, *mla_spec(l))
            fence(dve, n)
            each_t(dve, n, "v", nagm_pairs(l))
            fence(dve, n)
            each_t(dve, n, "v", mla_pairs(l))
            fence(dve, n)
            dve_merge(dve, n, l)
            fence(dve, n)
            each_t(dve, n, "v", acc_pairs(l))
            fence(dve, n)
            dve_resid(dve, n, WO2(l))
            fence(dve, n)
            dve_norm(dve, n, len(TQ[l]), l + 1, 1)
            fence(dve, n)
            dve_ffn(dve, n, l)
            fence(dve, n)

        block = ctx.enter_context(nc.Block())
        W_IN = I["w_in"][0]
        NF = 16 + 2 * STAGES2
        WO1 = [(0, 512, LAT, "v"), (512, 1024, LAT, "v")]

        @block.sync
        def _(sp):
            n, rel = tally(), [0, 0]
            sp_first(sp)
            sp.dma_start(xl[:, 0:TL, :], I["x"][0].rearrange("(t p) d -> p t d", p=P)).then_inc(x_in, 16)
            sp.dma_start(xl[:, TL:TA, :], I["ctx"][0].rearrange("(t p) d -> p t d", p=P)).then_inc(x_in, 16)
            plan_norm(n, TA)
            sp_lin(sp, n, rel, W_IN, BL1)
            for plan in (plan_gate, plan_dec, plan_st, plan_o):
                plan(n)
            plan_turn(n, KT, LAT)
            sp_lin(sp, n, rel, I["w_out"][0], WO1)
            sp.wait_ge(stage_done, 4 * 10)
            for m in (1, 2):
                for x in range(2):
                    load_expert(sp, m, x, slice(x, x + 1))
            sp.wait_ge(stage_done, 4 * 11)
            for x in range(2):
                load_expert(sp, 0, x, slice(x, x + 1))
            for t in range(TL):
                sp.wait_ge(xn_ok, TA + t + 1)
                sp.dma_start(xnd[P * t:P * t + P, :], XK(t)).then_inc(xn_st, 16)
            plan_norm(n, TL)
            plan_route(n)
            sp.wait_ge(stage_done, 4 * 13)
            sp_moe(sp)
            n["fence"] = 4 * 16
            sp.wait_ge(stage_done, 4 * 16)
            sp.dma_start(xl[:, TL:TA, :], I["ctx_2"][0].rearrange("(t p) d -> p t d", p=P)).then_inc(x_in, 16)
            for l in range(2):
                sp_layer(sp, n, rel, l)
            F = 4 * NF
            sp.wait_ge(stage_done, F)
            sp.dma_start(out[0].rearrange("(t p) d -> p t d", p=P), xl[:, 0:TL, :]).then_inc(out_in, 16)
            sp.wait_ge(out_in, 16)

        @block.gpsimd
        def _(pool):
            n = tally()
            pool.dma_start(lamt, I["da_lambda"][0].rearrange("a d -> (a d)").partition_broadcast(P)).then_inc(prm, 16)
            pool.dma_start(subln, I["da_subln_g"][0].partition_broadcast(P)).then_inc(prm, 16)
            pool.dma_start(glag, I["gla_norm_g"][0].partition_broadcast(P)).then_inc(prm, 16)
            for m in range(2):
                pool.dma_start(w2a[16 * 0:16, 256 * m:256 * m + 256], I["gla_gate_w2"][0][m]).then_inc(prm, 16)
                pool.dma_start(w2a[16:17, 256 * m:256 * m + 256], I["gla_gate_b"][0][m:m + 1, :]).then_inc(prm, 16)
            fence(pool, n)
            fence(pool, n)
            for c in range(MSTEPS, 3 * MSTEPS):
                load_mod(pool, c)
            fence(pool, n)
            pool.memset(hT[:, 0:D], 0.0).then_inc(zero_ok, 1)
            pool.wait_ge(zero_ok, 1)
            for r in range(NE * CAP, NBLK * CAP, P):
                pool.dma_start(ybuf[r:r + P, :], hT[:, 0:D]).then_inc(ybz, 16)
            pool.wait_ge(ybz, 16 * (NBLK - NE) * CAP // P)
            for _ in range(6):
                fence(pool, n)
            load_gate(pool, 0, 2)
            for _ in range(2):
                fence(pool, n)
            pool_route_params(pool)
            fence(pool, n)
            pool_route(pool)
            pool.wait_ge(xn_st, 64)
            fence(pool, n)
            pool_moe(pool)
            fence(pool, n)
            load_gate(pool, 0, 5)
            pool.dma_start(fng, I["final_norm_g"].partition_broadcast(P)).then_inc(fng_in, 16)
            pool_comb(pool, n)
            fence(pool, n)
            fence(pool, n)
            for l in range(2):
                pool_layer(pool, n, l)

        @block.tensor
        def _(pe):
            n = tally()
            pe_first(pe)
            fence(pe, n)
            pe_norm(pe, n, TA)
            fence(pe, n)
            pe_lin(pe, n, BL1, h_lhs)
            fence(pe, n)
            pe_mod_turn(pe, (1, 2))
            fence(pe, n)
            pe_attn(pe, n, *da_spec())
            fence(pe, n)
            pe_gates(pe, n)
            fence(pe, n)
            pe_dec(pe, n)
            fence(pe, n)
            pe_states(pe, n)
            fence(pe, n)
            pe_glao(pe, n)
            fence(pe, n)
            pe_turn(pe, n, KT, LAT, lambda k, t: pjt[:, t, 128 * k:128 * k + 128])
            fence(pe, n)
            pe_lin(pe, n, WO1, h_lhs)
            fence(pe, n)
            pe_norm(pe, n, TL, keep=XK)
            fence(pe, n)
            pe_route(pe, n)
            fence(pe, n)
            pe_moe(pe)
            fence(pe, n)
            fence(pe, n)
            fence(pe, n)
            for l in range(2):
                pe_layer(pe, n, l)

        @block.scalar
        def _(act):
            n = tally()
            load_rows(act)
            act_first(act)
            fence(act, n)
            act.wait_ge(x_in, 32)
            act_norm(act, n, TA, 0, 0)
            fence(act, n)
            each_lin(act, n, BL1, "a", act_put)
            fence(act, n)
            act_lambda(act, n)
            act_mod_turn(act, (1, 2))
            fence(act, n)
            act_attn(act, n, *da_spec())
            rms_heads(act, "a", n, LAT, hv(DQ, 4, 128), 4, 128, subln)
            fence(act, n)
            act_gates(act, n)
            fence(act, n)
            act_dec(act, n)
            fence(act, n)
            each_states(act, n, "a")
            fence(act, n)
            act_glao(act, n)
            fence(act, n)
            each_turn(act, n, "a", KT, LAT, hT_dst)
            fence(act, n)
            plan_lin(n, WO1)
            fence(act, n)
            act_norm(act, n, TL, 0, 1)
            fence(act, n)
            act_route(act, n)
            act.sem_inc(y_out, 16)
            fence(act, n)
            act_moe(act)
            fence(act, n)
            fence(act, n)
            act_final(act, n)
            fence(act, n)
            act.wait_ge(x_in, 48)
            for l in range(2):
                act_layer(act, n, l)

        @block.vector
        def _(dve):
            n = tally()
            dve_first(dve)
            fence(dve, n)
            dve.wait_ge(x_in, 32)
            dve_norm(dve, n, TA, 0, 0)
            fence(dve, n)
            each_lin(dve, n, BL1, "v", dve_put)
            fence(dve, n)
            dve_mod_turn(dve, (1, 2))
            dve_da_before(dve)
            dve_lambda(dve, n)
            fence(dve, n)
            dve_attn(dve, n, *da_spec(), lam=lam)
            rms_heads(dve, "v", n, LAT, hv(DQ, 4, 128), 4, 128, subln, mul=1.0 - (0.8 - 0.6))
            fence(dve, n)
            dve_gates(dve, n)
            fence(dve, n)
            dve_dec(dve, n)
            fence(dve, n)
            each_states(dve, n, "v")
            fence(dve, n)
            dve_glao(dve, n)
            fence(dve, n)
            each_turn(dve, n, "v", KT, LAT, hT_dst)
            fence(dve, n)
            dve_resid(dve, n, WO1)
            fence(dve, n)
            dve_norm(dve, n, TL, 0, 1, keep=XK)
            fence(dve, n)
            dve_route(dve, n)
            fence(dve, n)
            dve_moe(dve)
            fence(dve, n)
            dve_comb(dve, n)
            fence(dve, n)
            dve.wait_ge(fng_in, 16)
            dve_final(dve, n)
            fence(dve, n)
            dve.wait_ge(x_in, 48)
            for l in range(2):
                dve_layer(dve, n, l)


_INS = ["x", "c", "ctx", "c_ctx", "w_ada", "b_ada", "norm_mix_g", "norm_ffn_g", "w_in", "da_lambda", "da_subln_g",
        "gla_gate_w2", "gla_gate_b", "gla_norm_g", "w_out", "router_group_w", "router_group_b", "router_expert_w",
        "router_expert_b", "expert_w_gate", "expert_w_up", "expert_w_down", "final_norm_g", "c_2", "ctx_2",
        "c_ctx_2", "w_mod_2", "b_mod_2", "g_norm1_2", "g_norm2_2", "w_in_2", "na_q_gain_2", "na_k_gain_2", "na_rpb_2",
        "na_w_o_2", "gm_ln_g_2", "gm_ln_b_2", "gm_w_s_2", "gm_b_s_2", "gm_w_o_2", "mla_cq_gain_2", "mla_ckv_gain_2",
        "mla_w_uq_2", "mla_w_ukv_2", "mla_q_gain_2", "mla_k_gain_2", "mla_w_o_2", "w_out_2", "ffn_w1_2", "ffn_w2_2"]


def kernel(**inputs):
    import concourse.bacc as _bacc
    from concourse.bass_utils import run_bass_kernel_spmd as _run

    nc = _bacc.Bacc("TRN2", target_bir_lowering=False, num_devices=1)
    arrays, aps = {}, {}
    for name in _INS + ["cst"]:
        a = np.ascontiguousarray(constants() if name == "cst" else inputs[name])
        arrays[f"in_{name}_dram"] = a
        aps[name] = nc.dram_tensor(f"in_{name}_dram", a.shape, mybir.dt.from_np(a.dtype), kind="ExternalInput").ap()
    out = nc.dram_tensor("out_0_dram", (1, TL * P, D), F32, kind="ExternalOutput").ap()
    program(nc, aps, out)
    r = _run(nc, [arrays], core_ids=[0])
    return r.results[0]["out_0_dram"]
```

```python
import math
from contextlib import ExitStack

import numpy as np

import concourse.bass as bass
from concourse import mybir

F32 = mybir.dt.float32
F32R = mybir.dt.float32r
I32 = mybir.dt.int32
U32 = mybir.dt.uint32
ALU = mybir.AluOpType
ACT = mybir.ActivationFunctionType
AX = mybir.AxisListType.X

P = 128
D = 1024
KT = D // P
TL, TC = 4, 2
TA = TL + TC
NTOK = TA * P
CHUNK = 64
EPS = 1e-6
NEG = -1e30
BANK = 512

DQ, DK, DV, GQ, GK, GV, GR, LRF, LRB, IN1 = 0, 512, 1024, 1536, 1792, 2048, 2560, 3072, 3088, 3104
NK, NV, CKV, KR, NQ, GU, GMV, CQ, GATES = 0, 512, 1024, 1152, 1184, 1696, 2208, 2720, 2976
PW = IN1
NE, NG, EH = 32, 4, 512
CAP = 64
NBLK = 48
HALF = 4096

C_ID, C_TF, C_TB, C_BLK, C_US, C_CH = 0, 128, 256, 384, 512, 640
C_R1C, C_R1S, C_R2C, C_R2S, C_NM, C_NB = 642, 898, 1154, 1282, 1410, 1474
C_I32, C_E64, C_ONE, C_ROW, C_TA, C_TZ, C_TK, C_N = 1538, 1570, 1602, 1730, 1746, 1874, 2002, 2006

R_C, R_G, R_NAQ, R_NAK, R_BS, R_N, R_MB, R_ALL = 0, 48, 96, 98, 100, 108, 108, 252


def constants():
    c = np.zeros((P, C_N), np.float32)
    i = np.arange(P)
    same = i[:, None] // CHUNK == i[None, :] // CHUNK
    c[:, C_ID:C_ID + P] = np.eye(P)
    c[:, C_TF:C_TF + P] = same & (i[:, None] <= i[None, :])
    c[:, C_TB:C_TB + P] = same & (i[:, None] >= i[None, :])
    c[:, C_TK:C_TK + TL] = i[:, None] + P * np.arange(TL)
    c[:, C_TA:C_TA + P] = same & (i[:, None] > i[None, :])
    c[:, C_TZ:C_TZ + P] = same & (i[:, None] < i[None, :])
    c[:, C_BLK:C_BLK + P] = same
    c[:, C_US:C_US + P] = i[:, None] < i[None, :]
    c[:, C_CH:C_CH + 2] = i[:, None] // CHUNK == np.arange(2)
    tok = np.arange(TL * P)
    pos = np.stack([tok // 64, tok % 64], 1).astype(np.float32)
    for n, (cc, cs) in ((16, (C_R1C, C_R1S)), (8, (C_R2C, C_R2S))):
        inv = np.power(np.float32(10000.0), -np.arange(n, dtype=np.float32) / np.float32(n)).astype(np.float32)
        ang = pos[:, :, None] * inv
        cos = np.repeat(np.cos(ang)[:, :, None, :], 2, 2)
        sin = np.sin(ang)[:, :, None, :] * np.array([-1.0, 1.0], np.float32)[:, None]
        for at, t in ((cc, cos), (cs, sin)):
            c[:, at:at + TL * 4 * n] = t.reshape(TL, P, 4 * n).transpose(1, 0, 2).reshape(P, -1)
    col = i % 64
    c0 = np.clip(col - 8, 0, 48)
    kc = np.arange(64)
    inw = (kc[None] >= c0[:, None]) & (kc[None] < c0[:, None] + 16)
    c[:, C_NM:C_NM + 64] = inw
    c[:, C_NB:C_NB + 64] = np.where(inw, 0.0, NEG)
    c[:, C_I32:C_I32 + 32] = np.arange(32, 0, -1)
    c[:, C_E64:C_E64 + 32] = np.arange(32) * CAP
    c[:, C_ONE:C_ONE + P] = 1.0
    c[:, C_ROW:C_ROW + 16] = np.arange(16)
    return c


class Plan:

    def __init__(self, n, owners):
        self.mm0, self.own, self.val = n["mm"], owners, []
        for o in owners:
            if o != "-":
                n[o] += 1
            self.val.append(n.get(o, 0))
        n["mm"] += len(owners)

    def done(self, i):
        return self.mm0 + i + 1


def program(nc, I, out):
    ctx = ExitStack()
    with ctx:
        at = {}

        def sb(name, shape, dt=F32):
            t = ctx.enter_context(nc.sbuf_tensor(name, shape, dt))
            at[name] = nc.sbuf_base - 4 * shape[-1] * (shape[1] if len(shape) > 2 else 1)
            return t

        def over(name, base, first, width):
            return nc.alloc_sbuf_tensor_at(name, [P, width], F32R, offset=at[base] + 4 * first)

        def sem(name):
            return ctx.enter_context(nc.semaphore(name))

        ring = sb("ring", [P, 2 * HALF])
        xl = sb("xl", [P, TA, D])
        hT = sb("hT", [P, KT * NTOK])
        pj = sb("pj", [P, TA * PW])
        cst = sb("consts", [P, C_N])
        small = sb("small", [P, 1296])
        Z = sb("Z", [P, 10700])
        ps = ctx.enter_context(nc.psum_tensor("ps", [P, 8 * BANK], F32))

        hT_hi, hT_lo = over("hT_hi", "hT", 0, 6144), over("hT_lo", "pj", 12288, 6144)
        h1_hi, h1_lo = over("h1_hi", "pj", 6144, 6144), over("h1_lo", "xl", 0, 6144)
        w_hi, w_lo = over("w_hi", "Z", 0, 4096), over("w_lo", "Z", 4096, 4096)
        hm_lo = over("hm_lo", "xl", 0, 6144)
        wp_hi, wp_lo = over("wp_hi", "ring", 4096, 4096), over("wp_lo", "Z", 2048, 4096)
        wm_hi, wm_lo = over("wm_hi", "pj", 9216, 4096), over("wm_lo", "pj", 13312, 4096)

        hTk = hT[:, :].rearrange("p (k n) -> p k n", k=KT)
        pjt = pj[:, :].rearrange("p (t n) -> p t n", t=TA)

        def bank(b, n=BANK):
            return ps[:, b * BANK:b * BANK + n]

        def C(at, n=P):
            return cst[:, at:at + n]

        ident = C(C_ID)

        cols = small[:, 0:R_ALL]
        modc = small[:, 252:540].rearrange("p (l n) -> p l n", l=3)
        Ac = small[:, 540:636].rearrange("p (l w n k) -> p l w n k", l=3, w=2, n=2)
        st = small[:, 640:1240]

        xspill = nc.dram_tensor("xspill", (P, TA * D), F32, kind="Internal").ap()
        modp = nc.dram_tensor("modp", (3, 2, 6 * D), F32, kind="Internal").ap()
        modd = nc.dram_tensor("modd", (3, 2, 6 * D), F32, kind="Internal").ap()
        hTd = nc.dram_tensor("hTd", (P, KT * NTOK), F32, kind="Internal").ap()
        xnd = nc.dram_tensor("xnd", (TL * P, D), F32, kind="Internal").ap()
        rowtok = nc.dram_tensor("rowtok", (NBLK * CAP, 1), I32, kind="Internal").ap()
        ybuf = nc.dram_tensor("ybuf", (NBLK * CAP, D), F32, kind="Internal").ap()

        stage_done = sem("stage_done")
        mm_done, evac_a, evac_v = sem("mm_done"), sem("evac_a"), sem("evac_v")
        EV = {"a": evac_a, "v": evac_v}
        slot_in = [sem("slot0_in"), sem("slot1_in")]
        params_in, cols_in, mod_st = sem("params_in"), sem("cols_in"), sem("mod_st")
        modr_in, mod_in = [sem(f"modr{l}_in") for l in range(3)], [sem(f"mod_slot{i}_in") for i in range(6)]
        raw_in, w_hi_ok, w_lo_ok = [sem(f"raw_slot{i}_in") for i in range(4)], sem("w_hi_ok"), sem("w_lo_ok")
        hh_ok, ht_tmp, h1_read, out_read, h1_hi_ok, h1_lo_ok = (sem(x) for x in ("hh_ok", "ht_tmp", "h1_read", "out_read", "h1_hi_ok", "h1_lo_ok"))
        hl_ok, half_used, hh_back = sem("hl_ok"), sem("half_used"), [sem("hh_back_a"), sem("hh_back_v")]
        wr_ok = sem("wr_ok")
        proj_in = [sem("proj_slot0_in"), sem("proj_slot1_in")]
        x_out, x_back = sem("x_out"), sem("x_back")
        mring_in = [sem(f"merge_slot{i}_in") for i in range(5)]
        mod_done, mod_out, modT_done, modc_ok = sem("mod_done"), sem("mod_out"), sem("modT_done"), sem("modc_ok")
        modb_ok, modd_in, cols_done, cols_ok = sem("modb_ok"), sem("modd_in"), sem("cols_done"), sem("cols_ok")
        x_in = sem("x_in")
        silu_c = sem("silu_c")
        sumsq, var, std, xn_ok = sem("sumsq"), sem("var"), sem("std"), sem("xn_ok")
        s_done, s_free_v = sem("s_done"), sem("s_free_v")
        mx_ok, e_ok, a_ok, t_done = sem("mx_ok"), sem("e_ok"), sem("a_ok"), sem("t_done")
        et_a, et_v, o_done, y_ok = sem("et_a"), sem("et_v"), sem("o_done"), sem("y_ok")
        prep_done, prep_a, prep_v = sem("prep_done"), sem("prep_a"), sem("prep_v")
        v2a, a2v, v2p, prm = sem("v2a"), sem("a2v"), sem("v2p"), sem("prm")
        out_in, gate_in = sem("out_in"), sem("gate_in")
        rparams, zero_ok, rowz, idx_ok = sem("rparams"), sem("zero_ok"), sem("rowz"), sem("idx_ok")
        scat, rows_in, xg_in, xn_st = sem("scat"), sem("rows_in"), sem("xg_in"), sem("xn_st")
        w_used = [sem(f"w_used{m}") for m in range(3)]
        w_in_ = [sem(f"w_in{m}") for m in range(6)]
        xt_done, xt_a, xt_v, silu_ok = sem("xt_done"), sem("xt_a"), sem("xt_v"), sem("silu_ok")
        hu_ok, ht_done, ht_a = sem("hu_ok"), sem("ht_done"), sem("ht_a")
        y_a, y_v, y_out, yg_free = sem("y_a"), sem("y_v"), sem("y_out"), sem("yg_free")
        prm2, rp_ok, rp_in, tb_free, tb_ok = sem("prm2"), sem("rp_ok"), sem("rp_in"), sem("tb_free"), sem("tb_ok")
        tb_in = [sem("tb_in0"), sem("tb_in1")]
        spill, unspill = sem("spill"), sem("unspill")
        y_stored = sem("y_stored")
        ex_used, ybz = sem("ex_used"), sem("ybz")
        yg_in, fng_in = [sem("yg_in0"), sem("yg_in1")], sem("fng_in")

        def tally():
            return {k: 0 for k in ("mm", "a", "v", "fence", "chunk", "ss", "var", "std", "xn", "at", "a2v", "v2a", "v2p", "prm")}

        def fence(eng, n):
            eng.drain().then_inc(stage_done, 1)
            n["fence"] += 4
            eng.wait_ge(stage_done, n["fence"])

        def load_chunk(sp, n, dst, src, rel):
            c = n["chunk"]
            if rel[c % 2]:
                sp.wait_ge(mm_done, rel[c % 2])
            o = (c % 2) * HALF
            sp.dma_start(dst(ring[:, o:o + HALF]), src).then_inc(slot_in[c % 2], 16)
            n["chunk"] += 1

        def take_chunk(pe, n):
            c = n["chunk"]
            pe.wait_ge(slot_in[c % 2], 16 * (c // 2 + 1))
            n["chunk"] += 1
            o = (c % 2) * HALF
            return ring[:, o:o + HALF]

        WM = [I["w_ada"][0], I["w_mod_2"][0], I["w_mod_2"][1]]
        BM = [I["b_ada"][0], I["b_mod_2"][0], I["b_mod_2"][1]]
        sT = small[:, 1240:1288]
        rows = Z[:, 0:P]
        brows = Z[:, P:4 * P]
        mstage = [Z[:, 8192:8704], Z[:, 8704:9216]]
        modr = Z[:, 9216:9600]
        MSTEPS = 12

        def mod_slot(c):
            if c < MSTEPS:
                return pj[:, HALF * (c % 4):HALF * (c % 4) + HALF], mod_in[c % 4], 16 * (c // 4 + 1)
            c -= MSTEPS
            return Z[:, HALF * (c % 2):HALF * (c % 2) + HALF], mod_in[4 + c % 2], 16 * (c // 2 + 1)

        def load_mod(eng, c):
            depth = 4 if c < MSTEPS else 2
            if c % MSTEPS >= depth or c >= 2 * MSTEPS:
                eng.wait_ge(mod_done, c - depth + 1)
            l, r, q = c // MSTEPS, c // 4 % 3, c % 4
            slot, ready, _ = mod_slot(c)
            eng.dma_start(slot.rearrange("p (k n) -> p k n", k=2),
                          WM[l][256 * q:256 * q + 256, 2048 * r:2048 * r + 2048].rearrange("(k p) n -> p k n", p=P)).then_inc(ready, 16)

        def pe_mod(pe, c):
            g, q = c // 4, c % 4
            slot, ready, value = mod_slot(c)
            if q == 0 and g >= 2:
                pe.wait_ge(mod_out, g - 1)
            pe.wait_ge(ready, value)
            for kk in range(2):
                k = 2 * q + kk
                for j in range(4):
                    last = nc.tensor.matmul(ps[32 * j:32 * j + 2, (6 + g % 2) * BANK:(7 + g % 2) * BANK],
                                            sT[:, 16 * (c // MSTEPS) + k:16 * (c // MSTEPS) + k + 9:8],
                                            slot[:, 2048 * kk + 512 * j:2048 * kk + 512 * j + 512],
                                            start=(k == 0), stop=(k == KT - 1))
            last.then_inc(mod_done, 1)

        def dve_mod(dve, g):
            dve.wait_ge(mod_done, 4 * g + 4)
            if g >= 2:
                dve.wait_ge(mod_st, 64 * (g - 1))
            for j in range(4):
                last = nc.vector.tensor_copy(mstage[g % 2][32 * j:32 * j + 2, :], ps[32 * j:32 * j + 2, (6 + g % 2) * BANK:(7 + g % 2) * BANK])
            last.then_inc(mod_out, 1)

        def act_mod(act, g):
            l, r = g // 3, g % 3
            act.wait_ge(mod_out, g + 1)
            for j in range(4):
                act.dma_start(modp[l][:, 2048 * r + 512 * j:2048 * r + 512 * j + 512], mstage[g % 2][32 * j:32 * j + 2, :]).then_inc(mod_st, 16)
            act.wait_ge(mod_st, 64 * (g + 1))
            if r == 2:
                act.dma_start(modr[0:96, P * l:P * l + P], modp[l].rearrange("w (s q) -> (w s) q", q=P)).then_inc(modr_in[l], 16)

        def pe_mod_turn(pe, layers):
            for l in layers:
                pe.wait_ge(modr_in[l], 16)
                nc.tensor.transpose(bank(l, 96), modr[0:96, P * l:P * l + P], ident[0:96, 0:96]).then_inc(modT_done, 1)
            for l in layers:
                pe.wait_ge(modc_ok, l + 1)
                nc.tensor.transpose(bank(3 + l, P)[0:96, :], modc[:, l, :], ident).then_inc(modT_done, 1)

        def dve_mod_turn(dve, layers):
            for i, l in enumerate(layers):
                dve.wait_ge(modT_done, 2 * layers[0] + i + 1)
                b = cols[:, R_MB + 48 * l:R_MB + 48 * l + 48].unsqueeze(1).broadcast_to([P, 2, 48])
                nc.vector.tensor_tensor(modc[:, l, :].rearrange("p (w n) -> p w n", w=2), bank(l, 96).rearrange("p (w n) -> p w n", w=2),
                                        b, ALU.add).then_inc(modc_ok, 1)
                dve.drain()
                for w in range(2):
                    for m in range(2):
                        s = modc[:, l, 48 * w + 8 * (1 + 3 * m):48 * w + 8 * (1 + 3 * m) + 8]
                        g = cols[:, R_G + 16 * l + 8 * m:R_G + 16 * l + 8 * m + 8]
                        nc.vector.scalar_tensor_tensor(Ac[:, l, w, m, :], s, 1.0, g, ALU.add, ALU.mult)

        def act_mod_turn(act, layers):
            for i, l in enumerate(layers):
                act.wait_ge(modT_done, 2 * layers[0] + len(layers) + i + 1)
                act.activation(modr[0:96, P * l:P * l + P], bank(3 + l, P)[0:96, :], ACT.Copy).then_inc(modb_ok, 1)
                act.wait_ge(modb_ok, l + 1)
                act.dma_start(modd[l].rearrange("w (s q) -> (w s) q", q=P), modr[0:96, P * l:P * l + P]).then_inc(modd_in, 16)
            act.wait_ge(modd_in, 16 * (layers[-1] + 1))

        def sp_first(sp):
            sp.dma_start(cst[:, :], I["cst"]).then_inc(params_in, 16)
            for c in range(MSTEPS):
                load_mod(sp, c)

        def pe_first(pe):
            pe.wait_ge(params_in, 16)
            pe.wait_ge(cols_in, 16 * N_COLS)
            nc.tensor.transpose(bank(0, R_N), rows[0:R_N, :], ident[0:R_N, 0:R_N])
            for l in range(3):
                last = nc.tensor.transpose(bank(0)[:, R_MB + 48 * l:R_MB + 48 * l + 48], brows[0:48, P * l:P * l + P], ident[0:48, 0:48])
            last.then_inc(cols_done, 1)
            pe.wait_ge(silu_c, 1)
            for c in range(MSTEPS):
                pe_mod(pe, c)
            pe_mod_turn(pe, (0,))

        def act_first(act):
            act.wait_ge(cols_done, 1)
            act.activation(cols, bank(0, R_ALL), ACT.Copy).then_inc(cols_ok, 1)
            act.wait_ge(cols_ok, 1)
            act.activation(sT, cols[:, 0:48], ACT.Silu).then_inc(silu_c, 1)
            for g in range(3):
                act_mod(act, g)
            act_mod_turn(act, (0,))

        def dve_first(dve):
            for g in range(3):
                dve_mod(dve, g)
            dve.wait_ge(cols_ok, 1)
            dve_mod_turn(dve, (0,))

        N_COLS = 6 + 6 + 4 + 2 + 3

        def load_rows(eng):
            def row(at, src, k):
                eng.dma_start(rows[at:at + k, :], src).then_inc(cols_in, 16)

            flat = lambda a: a.rearrange("(k p) -> k p", p=P)
            row(0, flat(I["c"][0]), 8)
            row(8, flat(I["c_ctx"]), 8)
            row(16, flat(I["c_2"][0]), 8)
            row(24, flat(I["c_ctx_2"]), 8)
            row(32, flat(I["c_2"][0]), 8)
            row(40, flat(I["c_ctx_2"]), 8)
            row(48, flat(I["norm_mix_g"][0]), 8)
            row(56, flat(I["norm_ffn_g"][0]), 8)
            for l in range(2):
                row(64 + 16 * l, flat(I["g_norm1_2"][l]), 8)
                row(72 + 16 * l, flat(I["g_norm2_2"][l]), 8)
            for m in range(2):
                eng.dma_start(rows[R_NAQ:R_NAQ + 2, 64 * m:64 * m + 64], I["na_q_gain_2"]).then_inc(cols_in, 16)
                eng.dma_start(rows[R_NAK:R_NAK + 2, 64 * m:64 * m + 64], I["na_k_gain_2"]).then_inc(cols_in, 16)
            for l in range(2):
                row(R_BS + 4 * l, I["gm_b_s_2"][l], 4)
            for l in range(3):
                eng.dma_start(brows[0:48, P * l:P * l + P], flat(BM[l])).then_inc(cols_in, 16)

        junk = Z[:, 0:D]
        xn = [Z[:, D:2 * D], Z[:, 2 * D:3 * D]]

        def plan_norm(n, nt):
            return Plan(n, "av" * nt)

        def pe_norm(pe, n, nt, keep=None):
            p = plan_norm(n, nt)
            for t in range(nt):
                pe.wait_ge(xn_ok, n["xn"] + t + 1)
                src = xn[t % 2] if keep is None else keep(t)
                for h in range(2):
                    i = 2 * t + h
                    if i >= 4:
                        pe.wait_ge(EV[p.own[i - 4]], p.val[i - 4])
                    for k in range(4):
                        last = nc.tensor.transpose(bank(i % 4)[:, 128 * k:128 * k + 128],
                                                   src[:, 512 * h + 128 * k:512 * h + 128 * k + 128], ident)
                    last.then_inc(mm_done, 1)
            n["xn"] += nt

        def act_norm(act, n, nt, l, m):
            p = plan_norm(n, nt)
            n["xn"] += nt
            for t in range(nt):
                last = act.activation(junk, xl[:, t, :], ACT.Square, accum_out=st[:, t:t + 1])
                act.drain()
            last = act.activation(st[:, 16:16 + nt], st[:, 0:nt], ACT.Copy)
            last.then_inc(sumsq, 1)
            n["var"] += 1
            act.wait_ge(var, n["var"])
            act.activation(st[:, 24:24 + nt], st[:, 8:8 + nt], ACT.Sqrt).then_inc(std, 1)
            for t in range(nt):
                i = 2 * t
                act.wait_ge(mm_done, p.done(i))
                for k in range(4):
                    last = act.activation(hTk[:, k, 128 * t:128 * t + 128], bank(i % 4)[:, 128 * k:128 * k + 128], ACT.Identity,
                                          scale=Ac[:, l, t // TL, m, k:k + 1],
                                          bias=modc[:, l, 48 * (t // TL) + 24 * m + k:48 * (t // TL) + 24 * m + k + 1])
                last.then_inc(evac_a, 1)

        def dve_norm(dve, n, nt, l, m, keep=None):
            p = plan_norm(n, nt)
            n["ss"] += 1
            dve.wait_ge(sumsq, n["ss"])
            nc.vector.tensor_scalar(st[:, 8:8 + nt], st[:, 16:16 + nt], 1.0 / D, EPS, ALU.mult, ALU.add).then_inc(var, 1)
            n["std"] += 1
            dve.wait_ge(std, n["std"])
            nc.vector.reciprocal(st[:, 32:32 + nt], st[:, 24:24 + nt])
            dve.drain()
            for t in range(nt + 1):
                if t < nt:
                    if t >= 2 and keep is None:
                        dve.wait_ge(mm_done, p.done(2 * t - 3))
                    dst = xn[t % 2] if keep is None else keep(t)
                    nc.vector.tensor_scalar(dst, xl[:, t, :], st[:, 32 + t:33 + t], None, ALU.mult).then_inc(xn_ok, 1)
                if t >= 1:
                    u = t - 1
                    i = 2 * u + 1
                    dve.wait_ge(mm_done, p.done(i))
                    for k in range(4):
                        kk = 4 + k
                        c = 48 * (u // TL) + 24 * m + kk
                        last = nc.vector.tensor_scalar(hTk[:, kk, 128 * u:128 * u + 128], bank(i % 4)[:, 128 * k:128 * k + 128],
                                                       Ac[:, l, u // TL, m, kk:kk + 1], modc[:, l, c:c + 1], ALU.mult, ALU.add)
                    last.then_inc(evac_v, 1)

        def lin_banks(blocks):
            return 6 if blocks is BL1 else 8

        def plan_lin(n, blocks, own="av"):
            g = "".join(b[3] * len(b[2]) if len(b) > 3 else "." * len(b[2]) for b in blocks)
            return Plan(n, "".join(own[i % 2] if o == "." else o for i, o in enumerate(g)))

        def sp_lin(sp, n, rel, w, blocks):
            p = plan_lin(n, blocks)
            i = 0
            for c0, c1, ts, *_ in blocks:
                c = n["chunk"]
                load_chunk(sp, n, lambda s: s[:, 0:w.shape[0] // P * (c1 - c0)].rearrange("p (k n) -> p k n", n=c1 - c0),
                           w[:, c0:c1].rearrange("(k p) n -> p k n", p=P), rel)
                i += len(ts)
                rel[c % 2] = p.done(i - 1)

        def pe_lin(pe, n, blocks, lhs):
            p, nb = plan_lin(n, blocks), lin_banks(blocks)
            i = 0
            nk = lhs(None, None)
            for c0, c1, ts, *_ in blocks:
                s = take_chunk(pe, n)
                w = c1 - c0
                for t in ts:
                    if i >= nb:
                        pe.wait_ge(EV[p.own[i - nb]], p.val[i - nb])
                    for k in range(nk):
                        last = nc.tensor.matmul(bank(i % nb, w), lhs(k, t), s[:, k * w:k * w + w], start=(k == 0), stop=(k == nk - 1))
                    last.then_inc(mm_done, 1)
                    i += 1
                    if nb == 6 and i <= 2 * MSTEPS:
                        pe_mod(pe, MSTEPS + i - 1)

        def each_lin(eng, n, blocks, who, put):
            p, nb = plan_lin(n, blocks), lin_banks(blocks)
            i = 0
            for c0, c1, ts, *_ in blocks:
                for t in ts:
                    if p.own[i] == who:
                        eng.wait_ge(mm_done, p.done(i))
                        put(c0, c1, t, bank(i % nb, c1 - c0)).then_inc(EV[who], 1)
                    i += 1
                    if nb == 6 and i % 4 == 0 and i <= 2 * MSTEPS:
                        (act_mod if who == "a" else dve_mod)(eng, 3 + i // 4 - 1)

        def h_lhs(k, t):
            return KT if k is None else hTk[:, k, 128 * t:128 * t + 128]

        ALLT, LAT = tuple(range(TA)), tuple(range(TL))
        BL1 = [(0, 512, LAT), (512, 1024, ALLT), (1024, 1536, ALLT), (1536, 2048, ALLT), (2048, 2560, ALLT),
               (2560, 3072, LAT), (3072, 3104, ALLT)]

        def act_put(c0, c1, t, b):
            return nc.scalar.activation(pjt[:, t, c0:c1], b, ACT.Copy)

        def dve_put(c0, c1, t, b):
            return nc.vector.tensor_copy(pjt[:, t, c0:c1], b)

        kT = [Z[:, 0:768], Z[:, 768:1536]]
        qT = [Z[:, 1536:2304], Z[:, 2304:3072]]
        qz = [[Z[:, 1536:2304], Z[:, 2304:3072]], [hT[:, 4608:5376], hT[:, 5376:6144]]]
        EB = [[Z[:, 3072 + 1536 * u + 768 * m:3840 + 1536 * u + 768 * m] for m in range(2)] for u in range(2)]
        ET = [Z[:, 6144:6912], Z[:, 6912:7680]]

        class Attn:

            def __init__(self, n, heads, units):
                self.heads, self.units = heads, units
                self.nm = 2 if units[0]["combine"] else 1
                self.split = units[0]["rows"][0] == (0, 64)
                self.depth = 2 if self.nm == 2 else 4
                self.preps = [(h, side, ts) for h, (_, _, qts, _) in enumerate(heads) for side in ("k", "q")
                              for ts in ((0, 1, 2, 3), (4, 5)) if side == "k" or set(ts) <= set(qts)]
                first = {}
                for i, u in enumerate(units):
                    first.setdefault(u["head"], i)
                self.at = {}
                seen = {}
                for j, (h, _, _) in enumerate(self.preps):
                    k = seen[h] = seen.get(h, -1) + 1
                    self.at.setdefault(-1 if h == 0 else first[h - 1] + k, []).append(j)
                c = lambda key, k=1: n.__setitem__(key, n.get(key, 0) + k) or n[key]
                self.s, self.e, self.mx, self.free, self.t, self.et, self.a, self.o, self.y = ([] for _ in range(9))
                for u in units:
                    for _ in range(self.nm):
                        self.s.append(c("s"))
                        self.mx.append(c("mx"))
                        self.e.append(c("e"))
                        self.free.append((s_free_v, c("sf")) if u["bias"] is not None else (e_ok, n["e"]))
                    full = len(u["keys"]) == 6
                    self.t.append((c("t"), c("t")) if full else (None, c("t")))
                    self.et.append((c("eta") if full else None, c("etv")))
                    self.a.append(c("acomb") if u["combine"] else None)
                    self.o.append(c("o"))
                    self.y.append(c("y"))
                self.pd, self.pe_ = [], []
                for j in range(len(self.preps)):
                    self.pd.append(c("pd"))
                    self.pe_.append((prep_a, c("pa")) if j % 2 == 0 else (prep_v, c("pv")))

            def E(self, i, m):
                return EB[i % 2][m] if self.nm == 2 else EB[i % 4 // 2][i % 2]

        def pe_attn(pe, n, heads, units):
            A = Attn(n, heads, units)

            def prep(j):
                h, side, ts = A.preps[j]
                rows_, src, _, _ = heads[h]
                if j:
                    pe.wait_ge(*A.pe_[j - 1])
                for t in ts:
                    last = nc.tensor.transpose(bank(7)[0:rows_, 128 * (t - ts[0]):128 * (t - ts[0]) + 128], src(side, t), ident)
                last.then_inc(prep_done, 1)

            def scores(i):
                u = units[i]
                for j, (h, _, _) in enumerate(A.preps):
                    if h == u["head"]:
                        pe.wait_ge(*A.pe_[j])
                for m in range(A.nm):
                    g = A.nm * i + m
                    if g >= 2:
                        pe.wait_ge(*A.free[g - 2])
                    b = ps[:, 1024 * (g % 2):1024 * (g % 2) + 1024]
                    rs = slice(*u["rows"][m])
                    q = qT[u["head"] % 2]
                    if A.split:
                        q = qz[u["head"] % 2][rs.start // 64]
                        rs = slice(0, P)
                    q = q[rs, 128 * u["qt"]:128 * u["qt"] + 128]
                    if len(u["keys"]) == 6:
                        nc.tensor.matmul(b[:, 0:512], q, kT[u["head"] % 2][rs, 0:512], start=True, stop=True)
                    nc.tensor.matmul(b[:, 512:768], q, kT[u["head"] % 2][rs, 512:768], start=True, stop=True).then_inc(s_done, 1)

            def transp(i):
                u = units[i]
                if u["combine"]:
                    pe.wait_ge(a_ok, A.a[i])
                else:
                    pe.wait_ge(e_ok, A.e[i])
                E = A.E(i, 0)
                if len(u["keys"]) == 6:
                    prev = [x[0] for x in A.et[:i] if x[0] is not None]
                    if prev:
                        pe.wait_ge(et_a, prev[-1])
                    for t in range(4):
                        last = nc.tensor.transpose(bank(4)[:, 128 * t:128 * t + 128], E[:, 128 * t:128 * t + 128], ident)
                    last.then_inc(t_done, 1)
                if i:
                    pe.wait_ge(et_v, A.et[i - 1][1])
                for t in (4, 5):
                    last = nc.tensor.transpose(bank(5)[:, 128 * (t - 4):128 * (t - 4) + 128], E[:, 128 * t:128 * t + 128], ident)
                last.then_inc(t_done, 1)

            def values(i):
                u = units[i]
                if A.et[i][0] is not None:
                    pe.wait_ge(et_a, A.et[i][0])
                pe.wait_ge(et_v, A.et[i][1])
                if i:
                    pe.wait_ge(y_ok, A.y[i - 1])
                for t in u["keys"]:
                    last = nc.tensor.matmul(bank(6, u["dv"]), ET[i % 2][:, 128 * t:128 * t + 128], u["v"](t),
                                            start=(t == u["keys"][0]), stop=(t == u["keys"][-1]))
                last.then_inc(o_done, 1)

            for j in A.at.get(-1, []):
                prep(j)
            for i in range(len(units) + 3):
                if i < len(units):
                    scores(i)
                for j in A.at.get(i, []):
                    prep(j)
                if 0 <= i - 2 < len(units):
                    transp(i - 2)
                if i >= 3:
                    values(i - 3)

        def prep_out(eng, A, j, who):
            h, side, ts = A.preps[j]
            if A.pe_[j][0] is not (prep_a if who == "a" else prep_v):
                return
            rows_, _, _, gain = A.heads[h]
            eng.wait_ge(prep_done, A.pd[j])
            dst = (kT if side == "k" else qT)[h % 2][0:rows_, 128 * ts[0]:128 * ts[-1] + 128]
            src = bank(7, 128 * len(ts))[0:rows_, :]
            parts = [(slice(0, rows_), dst)]
            if A.split and side == "q":
                parts = [(slice(64 * x, 64 * x + 64), qz[h % 2][x][64 * x:64 * x + 64, 128 * ts[0]:128 * ts[-1] + 128]) for x in range(2)]
            for rs, dst in parts:
                if who == "a":
                    last = nc.scalar.activation(dst, src[rs], ACT.Copy, **({} if gain is None else {"scale": gain(side)[rs]}))
                elif gain is None:
                    last = nc.vector.tensor_copy(dst, src[rs])
                else:
                    last = nc.vector.tensor_scalar(dst, src[rs], gain(side)[rs], None, ALU.mult)
            last.then_inc(prep_a if who == "a" else prep_v, 1)

        def stat(i, k):
            at = 100 + 8 * (i % 4) + k
            return st[:, at:at + 1]

        def act_attn(act, n, heads, units):
            A = Attn(n, heads, units)

            def exps(i):
                u = units[i]
                k0 = 128 * u["keys"][0]
                for m in range(A.nm):
                    g = A.nm * i + m
                    if i >= A.depth:
                        act.wait_ge(t_done, A.t[i - A.depth][1])
                    act.wait_ge(mx_ok, A.mx[g])
                    E = A.E(i, m)[:, k0:768]
                    src = E if u["bias"] is not None else ps[:, 1024 * (g % 2) + k0:1024 * (g % 2) + 768]
                    act.activation(E, src, ACT.Exp, bias=stat(i, m), scale=1.0 if u["bias"] is not None else u["scale"],
                                   accum_out=stat(i, 2 + m)).then_inc(e_ok, 1)

            def et(i):
                if A.et[i][0] is None:
                    return
                act.wait_ge(t_done, A.t[i][0])
                if i >= 2:
                    act.wait_ge(o_done, A.o[i - 2])
                act.activation(ET[i % 2][:, 0:512], bank(4), ACT.Copy).then_inc(et_a, 1)

            for j in A.at.get(-1, []):
                prep_out(act, A, j, "a")
            for i in range(len(units) + 2):
                if i < len(units):
                    exps(i)
                for j in A.at.get(i, []):
                    prep_out(act, A, j, "a")
                if i >= 2:
                    et(i - 2)

        def dve_attn(dve, n, heads, units, lam=None, tables=None):
            A = Attn(n, heads, units)

            def maxima(i):
                u = units[i]
                k0 = 128 * u["keys"][0]
                for m in range(A.nm):
                    g = A.nm * i + m
                    dve.wait_ge(s_done, A.s[g])
                    src = ps[:, 1024 * (g % 2) + k0:1024 * (g % 2) + 768]
                    if u["bias"] is not None:
                        if i >= A.depth:
                            dve.wait_ge(t_done, A.t[i - A.depth][1])
                        E = A.E(i, m)
                        dve.wait_ge(tb_ok, tables + u["head"] + 1)
                        u["bias"](E, ps[:, 1024 * (g % 2):1024 * (g % 2) + 768]).then_inc(s_free_v, 1)
                        dve.drain()
                        src = E[:, k0:768]
                    nc.vector.reduce_max(stat(i, 6 + m), src, AX)
                    dve.drain()
                    nc.vector.tensor_scalar(stat(i, m), stat(i, 6 + m), -1.0 if u["bias"] is not None else -u["scale"],
                                            None, ALU.mult).then_inc(mx_ok, 1)

            def norms(i):
                u = units[i]
                dve.wait_ge(e_ok, A.e[A.nm * i + A.nm - 1])
                nc.vector.reciprocal(st[:, 100 + 8 * (i % 4) + 4:100 + 8 * (i % 4) + 4 + A.nm],
                                     st[:, 100 + 8 * (i % 4) + 2:100 + 8 * (i % 4) + 2 + A.nm])
                if u["combine"]:
                    dve.drain()
                    E0, E1 = EB[i % 2]
                    nc.vector.tensor_scalar(E1, E1, stat(i, 5), lam, ALU.mult, ALU.mult)
                    dve.drain()
                    nc.vector.scalar_tensor_tensor(E0, E0, stat(i, 4), E1, ALU.mult, ALU.subtract).then_inc(a_ok, 1)

            def et(i):
                dve.wait_ge(t_done, A.t[i][1])
                if i >= 2:
                    dve.wait_ge(o_done, A.o[i - 2])
                nc.vector.tensor_copy(ET[i % 2][:, 512:768], bank(5, 256)).then_inc(et_v, 1)

            def outs(i):
                u = units[i]
                dve.wait_ge(o_done, A.o[i])
                if u["combine"]:
                    nc.vector.tensor_copy(u["y"], bank(6, u["dv"])).then_inc(y_ok, 1)
                else:
                    nc.vector.tensor_scalar(u["y"], bank(6, u["dv"]), stat(i, 4), None, ALU.mult).then_inc(y_ok, 1)

            if A.split:
                for b in range(2):
                    for x in range(2):
                        nc.vector.memset(qz[b][x][64 - 64 * x:128 - 64 * x, :], 0.0)
            for j in A.at.get(-1, []):
                prep_out(dve, A, j, "v")
            for i in range(len(units) + 3):
                if i < len(units):
                    maxima(i)
                for j in A.at.get(i, []):
                    prep_out(dve, A, j, "v")
                if 0 <= i - 1 < len(units):
                    norms(i - 1)
                if 0 <= i - 2 < len(units):
                    et(i - 2)
                if i >= 3:
                    outs(i - 3)
                if tables is not None and i < len(units) and (i + 1 == len(units) or units[i + 1]["head"] != units[i]["head"]):
                    dve.drain().then_inc(tb_free, 1)

        def da_spec():
            def src(h):
                return lambda side, t: pjt[:, t, (DK if side == "k" else DQ) + 128 * h:(DK if side == "k" else DQ) + 128 * h + 128]
            heads = [(P, src(h), LAT, None) for h in range(4)]
            units = [dict(head=h, rows=((0, 64), (64, 128)), qt=t, keys=ALLT, bias=None, scale=64 ** -0.5, combine=True,
                          v=lambda kt, h=h: pjt[:, kt, DV + 128 * h:DV + 128 * h + 128], dv=128,
                          y=pjt[:, t, DQ + 128 * h:DQ + 128 * h + 128]) for h in range(4) for t in LAT]
            return heads, units

        def dve_rope(dve, t, v, g, f, cc, cs, A_, B_):
            cosb = C(cc + 4 * f * t, 4 * f).unsqueeze(1).broadcast_to([P, g, 4 * f])
            sin4 = C(cs + 4 * f * t, 4 * f).rearrange("p (a s f) -> p a s f", a=2, s=2)
            v5 = v.rearrange("p g (a s f) -> p g a s f", a=2, s=2)
            A3, B5 = A_.rearrange("p (g n) -> p g n", g=g), B_.rearrange("p (g a s f) -> p g a s f", g=g, a=2, s=2)
            nc.vector.tensor_tensor(A3, v, cosb, ALU.mult)
            for s in range(2):
                nc.vector.tensor_tensor(B5[:, :, :, s, :], v5[:, :, :, 1 - s, :],
                                        sin4[:, :, s, :].unsqueeze(1).broadcast_to([P, g, 2, f]), ALU.mult)
            dve.drain()
            nc.vector.tensor_tensor(v, A3, B_.rearrange("p (g n) -> p g n", g=g), ALU.add)

        lamt, lam = Z[:, 9600:9856], st[:, 180:181]
        subln, glag = Z[:, 9856:9984], Z[:, 9984:10112]
        w2a = Z[:, 10112:10624]

        def rms_heads(eng, who, n, tiles, view, H, dh, gain, mul=1.0, at=0):
            nt = len(tiles)
            ss = st[:, 200:200 + nt * H]
            vv = st[:, 260:260 + nt * H]
            sd = st[:, 320:320 + nt * H]
            rr = st[:, 380:380 + nt * H]
            sq = [Z[:, at:at + H * dh], Z[:, at + 1024:at + 1024 + H * dh]]
            if who == "v":
                for i, t in enumerate(tiles):
                    v = view(t)
                    s3 = sq[i % 2].rearrange("p (h d) -> p h d", h=H)
                    nc.vector.tensor_tensor(s3, v, v, ALU.mult)
                    eng.drain()
                    nc.vector.tensor_reduce(ss[:, H * i:H * i + H], s3, AX, ALU.add)
                eng.drain()
                nc.vector.tensor_scalar(vv, ss, 1.0 / dh, EPS, ALU.mult, ALU.add).then_inc(var, 1)
                n["std"] += 1
                eng.wait_ge(std, n["std"])
                nc.vector.reciprocal(rr, sd)
                eng.drain()
                if mul != 1.0:
                    nc.vector.tensor_scalar(rr, rr, mul, None, ALU.mult)
                    eng.drain()
                for i, t in enumerate(tiles):
                    v = view(t)
                    nc.vector.tensor_tensor(v, v, rr[:, H * i:H * i + H].unsqueeze(2).broadcast_to([P, H, dh]), ALU.mult)
                if gain is not None:
                    eng.drain()
                    for i, t in enumerate(tiles):
                        v = view(t)
                        nc.vector.tensor_tensor(v, v, gain.unsqueeze(1).broadcast_to([P, H, dh]), ALU.mult)
            else:
                n["var"] += 1
                eng.wait_ge(var, n["var"])
                eng.activation(sd, vv, ACT.Sqrt).then_inc(std, 1)

        def hv(c0, H, dh):
            return lambda t: pjt[:, t, c0:c0 + H * dh].rearrange("p (h d) -> p h d", h=H)

        def dve_da_before(dve):
            dve.wait_ge(prm, 16 * 7)
            for t in LAT:
                dve_rope(dve, t, hv(DQ, 16, 64)(t), 16, 16, C_R1C, C_R1S, Z[:, 2048 * (t % 2):2048 * (t % 2) + 1024],
                         Z[:, 2048 * (t % 2) + 1024:2048 * (t % 2) + 2048])
            l4 = lamt.rearrange("p (a b d) -> p a b d", a=2, b=2)
            pr = Z[:, 9000:9128].rearrange("p (a d) -> p a d", a=2)
            nc.vector.tensor_tensor(pr, l4[:, :, 0, :], l4[:, :, 1, :], ALU.mult)
            dve.drain()
            nc.vector.tensor_reduce(st[:, 182:184], pr, AX, ALU.add).then_inc(v2a, 1)

        def act_lambda(act, n):
            n["v2a"] += 1
            act.wait_ge(v2a, n["v2a"])
            act.activation(st[:, 184:186], st[:, 182:184], ACT.Exp).then_inc(a2v, 1)

        def dve_lambda(dve, n):
            n["a2v"] += 1
            dve.wait_ge(a2v, n["a2v"])
            nc.vector.scalar_tensor_tensor(lam, st[:, 184:185], 0.8 - 0.6 * math.exp(-0.0), st[:, 185:186], ALU.add, ALU.subtract)
            dve.drain()

        Gg = Z[:, 0:3072].rearrange("p (t n) -> p t n", t=TA)
        zc = Z[:, 3072:6144].rearrange("p (t n) -> p t n", t=TA)
        sp_ = Z[:, 6144:9216].rearrange("p (t n) -> p t n", t=TA)
        lrT = hT[0:32, 0:1536].rearrange("p (t n) -> p t n", t=TA)
        qdT = hT[:, 1536:3584].rearrange("p (t n) -> p t n", t=TL)
        kiT = hT[:, 3584:5632].rearrange("p (t n) -> p t n", t=TL)
        ex = [[Z[:, 3072 + 1536 * i + 512 * j:3584 + 1536 * i + 512 * j] for j in range(3)] for i in range(2)]
        qk = [Z[:, 6144 + 1024 * i:7168 + 1024 * i] for i in range(2)]
        DD = Z[:, 0:6144].rearrange("p (c d q n) -> p c d q n", c=12, d=2, q=2)
        SM = [[Z[:, 6144 + 1024 * i + 512 * d:6656 + 1024 * i + 512 * d] for d in range(2)] for i in range(2)]
        dec = st[:, 440:488]
        FWD = [8, 9, 10, 11] + list(range(8))
        BWD = [11, 10, 9, 8] + list(range(7, -1, -1))
        TRI = (C_TF, C_TB)
        AFTER = (C_TA, C_TZ)

        def plan_gate(n):
            return Plan(n, "a" * (2 * TA))

        def pe_gates(pe, n):
            p = plan_gate(n)
            n["v2p"] += 1
            pe.wait_ge(v2p, n["v2p"])
            for i in range(2 * TA):
                t = i % TA
                if i >= 4:
                    pe.wait_ge(evac_a, p.val[i - 4])
                if i < TA:
                    for d in range(2):
                        last = nc.tensor.transpose(bank(i % 4)[0:16, 128 * d:128 * d + 128], pjt[:, t, LRF + 16 * d:LRF + 16 * d + 16], ident)
                else:
                    pe.wait_ge(evac_a, p.val[t])
                    for d in range(2):
                        last = nc.tensor.matmul(bank(i % 4)[:, 256 * d:256 * d + 256], lrT[0:17, t, 128 * d:128 * d + 128],
                                                w2a[0:17, 256 * d:256 * d + 256], start=True, stop=True)
                last.then_inc(mm_done, 1)

        def act_gates(act, n):
            p = plan_gate(n)
            n["v2a"] += 1
            act.wait_ge(v2a, n["v2a"])
            for i in range(2 * TA):
                t = i % TA
                act.wait_ge(mm_done, p.done(i))
                if i < TA:
                    act.activation(lrT[0:16, t, :], bank(i % 4)[0:16, 0:256], ACT.Copy).then_inc(evac_a, 1)
                else:
                    act.activation(zc[:, t, :], bank(i % 4), ACT.Copy).then_inc(evac_a, 1)
            act.drain()
            act.activation(sp_, zc, ACT.Abs)
            act.drain()
            act.activation(sp_, sp_, ACT.Exp, scale=-1.0)
            act.drain()
            act.activation(sp_, sp_, ACT.Ln, bias=1.0).then_inc(a2v, 1)

        def dve_gates(dve, n):
            plan_gate(n)
            nc.vector.memset(hT[0:32, 0:1536], 1.0).then_inc(v2p, 1)
            nc.vector.memset(st[0:1, 599:600], 0.0).then_inc(v2a, 1)
            n["a2v"] += 1
            dve.wait_ge(a2v, n["a2v"])
            nc.vector.scalar_tensor_tensor(Gg, zc, 0.0, sp_, ALU.min, ALU.subtract)

        def plan_dec(n):
            return Plan(n, "aa" * TA + "va" * TL + "a")

        def pe_dec(pe, n):
            p = plan_dec(n)
            for t in range(TA):
                for j, tri in enumerate((TRI, AFTER)):
                    i = 2 * t + j
                    if t >= 2:
                        pe.wait_ge(evac_a, dec_s(p, t - 2, j))
                    for d in range(2):
                        last = nc.tensor.matmul(bank(i % 4)[:, 256 * d:256 * d + 256], C(tri[d]), Gg[:, t, 256 * d:256 * d + 256],
                                                start=True, stop=True)
                    last.then_inc(mm_done, 1)
                if 1 <= t <= TL:
                    turn_dec(pe, n, p, t - 1)
            for t in range(TA):
                for d in range(2):
                    for q in range(2):
                        k = 8 * t + 4 * d + 2 * q
                        last = nc.tensor.matmul(bank(6)[:, k:k + 2], Gg[:, t, 256 * d + 128 * q:256 * d + 128 * q + 128], C(C_CH, 2),
                                                start=True, stop=True)
            last.then_inc(mm_done, 1)

        def dec_order():
            o = []
            for t in range(TA):
                o += [("s", t, 0), ("s", t, 1)]
                if 1 <= t <= TL:
                    o += [("t", t - 1, 0), ("t", t - 1, 1)]
            return {k: i for i, k in enumerate(o)}

        DECO = dec_order()

        def turn_dec(pe, n, p, t):
            n["v2p"] += 1
            pe.wait_ge(v2p, n["v2p"])
            for j in range(2):
                if t >= 1:
                    pe.wait_ge(*((evac_v, p.val[2 * TA + 2 * (t - 1)]) if j == 0 else (evac_a, dec_a(p, t - 1))))
                for x in range(4):
                    last = nc.tensor.transpose(bank(4 + j)[:, 128 * x:128 * x + 128], qk[t % 2][:, 512 * j + 128 * x:512 * j + 128 * x + 128], ident)
                last.then_inc(mm_done, 1)

        def dec_a(p, t):
            k = DECO[("t", t, 1)]
            return p.val[0] - 1 + sum(1 for x, i in DECO.items() if i <= k and (x[0] == "s" or x[2] == 1))

        def dec_s(p, t, j):
            k = DECO[("s", t, j)]
            return p.val[0] - 1 + sum(1 for x, i in DECO.items() if i <= k and (x[0] == "s" or x[2] == 1))

        def act_dec(act, n):
            p = plan_dec(n)
            for (kind, t, j), i in DECO.items():
                act_need = kind == "s" or j == 1
                if not act_need:
                    continue
                act.wait_ge(mm_done, p.done(i))
                if kind == "t":
                    act.activation(kiT[:, t, :], bank(5), ACT.Copy).then_inc(evac_a, 1)
                elif j == 0:
                    if t >= 2:
                        act.wait_ge(ex_used, t - 1)
                    act.activation(ex[t % 2][0], bank((2 * t) % 4), ACT.Exp, scale=1 / 16)
                    act.activation(ex[t % 2][1], bank((2 * t) % 4), ACT.Exp, scale=-1 / 16).then_inc(evac_a, 1)
                else:
                    act.activation(ex[t % 2][2], bank((2 * t + 1) % 4), ACT.Exp, scale=1 / 16).then_inc(evac_a, 1)
            act.wait_ge(mm_done, p.done(len(DECO)))
            act.activation(dec, bank(6, 48), ACT.Exp, scale=1 / 16).then_inc(evac_a, 1)

        def dve_dec(dve, n):
            p = plan_dec(n)
            for t in range(TA):
                dve.wait_ge(evac_a, dec_s(p, t, 1))
                k2 = pjt[:, t, GK:GK + 256].unsqueeze(1).broadcast_to([P, 2, 256])
                q2 = pjt[:, t, GQ:GQ + 256].unsqueeze(1).broadcast_to([P, 2, 256])
                e3 = [e.rearrange("p (d n) -> p d n", d=2) for e in ex[t % 2]]
                if t < TL:
                    if t >= 2:
                        dve.wait_ge(mm_done, p.done(DECO[("t", t - 2, 1)]))
                    a = qk[t % 2].rearrange("p (j d n) -> p j d n", j=2, d=2)
                    nc.vector.scalar_tensor_tensor(a[:, 0], q2, 64 ** -0.5, e3[0], ALU.mult, ALU.mult)
                    nc.vector.tensor_tensor(a[:, 1], k2, e3[1], ALU.mult).then_inc(v2p, 1)
                nc.vector.tensor_tensor(pjt[:, t, DK:DK + 512].rearrange("p (d n) -> p d n", d=2), k2, e3[2], ALU.mult).then_inc(ex_used, 1)
                if 1 <= t <= TL:
                    dve.wait_ge(mm_done, p.done(DECO[("t", t - 1, 0)]))
                    nc.vector.tensor_copy(qdT[:, t - 1, :], bank(4)).then_inc(evac_v, 1)

        def plan_st(n):
            return Plan(n, "av" * 6)

        def pe_states(pe, n):
            p = plan_st(n)
            for ci in range(12):
                t, c = ci // 2, ci % 2
                if ci >= 8:
                    pe.wait_ge(EV[p.own[ci - 8]], p.val[ci - 8])
                rs = slice(64 * c, 64 * c + 64)
                for d in range(2):
                    for h in range(4):
                        last = nc.tensor.matmul(bank(ci % 8)[64 * (h % 2):64 * (h % 2) + 64, 256 * d + 128 * (h // 2):256 * d + 128 * (h // 2) + 128],
                                                pjt[rs, t, DK + 256 * d + 64 * h:DK + 256 * d + 64 * h + 64],
                                                pjt[rs, t, GV + 128 * h:GV + 128 * h + 128], start=True, stop=True)
                last.then_inc(mm_done, 1)

        def each_states(eng, n, who):
            p = plan_st(n)
            for ci in range(12):
                if p.own[ci] == who:
                    eng.wait_ge(mm_done, p.done(ci))
                    dst = Z[:, 512 * ci:512 * ci + 512]
                    if who == "a":
                        nc.scalar.activation(dst, bank(ci % 8), ACT.Copy).then_inc(evac_a, 1)
                    else:
                        nc.vector.tensor_copy(dst, bank(ci % 8)).then_inc(evac_v, 1)
            if who == "v":
                eng.wait_ge(evac_a, p.val[10])
                eng.drain()
                for s in range(1, 12):
                    for d, order in enumerate((FWD, BWD)):
                        a, b = order[s - 1], order[s]
                        for q in range(2):
                            k = 8 * (b // 2) + 4 * d + 2 * q + b % 2
                            nc.vector.scalar_tensor_tensor(DD[:, b, d, q, :], DD[:, a, d, q, :], dec[:, k:k + 1], DD[:, b, d, q, :],
                                                           ALU.mult, ALU.add)
                    eng.drain()

        def plan_o(n):
            return Plan(n, "vvvvaa" * TL)

        def pe_glao(pe, n):
            p = plan_o(n)
            for t in range(TL):
                for g in range(4):
                    d, par = g // 2, g % 2
                    rs = slice(64 * par, 64 * par + 64)
                    if t:
                        pe.wait_ge(evac_v, p.val[6 * (t - 1) + g])
                    for q in range(2):
                        x = 256 * d + 128 * q
                        last = nc.tensor.matmul(bank(g)[:, 128 * q:128 * q + 128], kiT[rs, t, x:x + 128], qdT[rs, t, x:x + 128],
                                                start=True, stop=True)
                    last.then_inc(mm_done, 1)
                for par in range(2):
                    rs = slice(64 * par, 64 * par + 64)
                    pe.wait_ge(evac_v, p.val[6 * t + 2 + par])
                    if t >= 2:
                        pe.wait_ge(evac_a, p.val[6 * (t - 2) + 4 + par])
                    for q in range(2):
                        h = 2 * q + par
                        o = bank(4 + 2 * (t % 2) + par)[:, 128 * q:128 * q + 128]
                        for d in range(2):
                            nc.tensor.matmul(o, SM[t % 2][d][:, 128 * h:128 * h + 128], pjt[:, t, GV + 128 * h:GV + 128 * h + 128],
                                             start=(d == 0), stop=False)
                        for d, order in enumerate((FWD, BWD)):
                            for c in range(2):
                                prev = order[order.index(2 * t + c) - 1]
                                x = 256 * d + 128 * q
                                last = nc.tensor.matmul(o[64 * c:64 * c + 64, :], qdT[rs, t, x + 64 * c:x + 64 * c + 64], DD[rs, prev, d, q, :],
                                                        start=False, stop=(d == 1))
                    last.then_inc(mm_done, 1)

        def dve_glao(dve, n):
            p = plan_o(n)
            for t in range(TL):
                if t >= 2:
                    dve.wait_ge(mm_done, p.done(6 * (t - 2) + 5))
                for g in range(4):
                    d, par = g // 2, g % 2
                    dve.wait_ge(mm_done, p.done(6 * t + g))
                    m = C(TRI[d]).unsqueeze(1).broadcast_to([P, 2, P])
                    nc.vector.tensor_tensor(SM[t % 2][d].rearrange("p (q a n) -> p a q n", q=2, a=2)[:, par],
                                            bank(g, 256).rearrange("p (q n) -> p q n", q=2), m, ALU.mult).then_inc(evac_v, 1)
            dve.wait_ge(evac_a, p.val[6 * (TL - 1) + 5])
            rms_heads(dve, "v", n, LAT, hv(DK, 4, 128), 4, 128, glag)
            dve.drain()
            n["a2v"] += 1
            dve.wait_ge(a2v, n["a2v"])
            for t in LAT:
                nc.vector.tensor_tensor(pjt[:, t, DK:DK + 512], pjt[:, t, DK:DK + 512], pjt[:, t, GR:GR + 512], ALU.mult)

        def act_glao(act, n):
            p = plan_o(n)
            for t in range(TL):
                for par in range(2):
                    act.wait_ge(mm_done, p.done(6 * t + 4 + par))
                    act.activation(pjt[:, t, DK:DK + 512].rearrange("p (q a n) -> p a q n", q=2, a=2)[:, par],
                                   bank(4 + 2 * (t % 2) + par, 256).rearrange("p (q n) -> p q n", q=2), ACT.Copy).then_inc(evac_a, 1)
            rms_heads(act, "a", n, LAT, hv(DK, 4, 128), 4, 128, glag)
            act.activation(pjt[:, 0:TL, GR:GR + 512], pjt[:, 0:TL, GR:GR + 512], ACT.Silu).then_inc(a2v, 1)

        def plan_turn(n, nk, tiles):
            return Plan(n, "av" * (nk * len(tiles) // 8) if (nk * len(tiles)) % 8 == 0 else "a" * (nk * len(tiles) // 4))

        def pe_turn(pe, n, nk, tiles, src):
            p = plan_turn(n, nk, tiles)
            i = 0
            for t in tiles:
                for k0 in range(0, nk, 4):
                    if i >= 8:
                        pe.wait_ge(EV[p.own[i - 8]], p.val[i - 8])
                    for k in range(4):
                        last = nc.tensor.transpose(bank(i % 8)[:, 128 * k:128 * k + 128], src(k0 + k, t), ident)
                    last.then_inc(mm_done, 1)
                    i += 1

        def each_turn(eng, n, who, nk, tiles, dst):
            p = plan_turn(n, nk, tiles)
            i = 0
            for t in tiles:
                for k0 in range(0, nk, 4):
                    if p.own[i] == who:
                        eng.wait_ge(mm_done, p.done(i))
                        b = bank(i % 8).rearrange("p (k n) -> p k n", k=4)
                        if who == "a":
                            nc.scalar.activation(dst(k0, t), b, ACT.Copy).then_inc(evac_a, 1)
                        else:
                            nc.vector.tensor_copy(dst(k0, t), b).then_inc(evac_v, 1)
                    i += 1

        def hT_dst(k0, t):
            return hTk[:, k0:k0 + 4, 128 * t:128 * t + 128]

        gtb = Z[:, 8192:10240].rearrange("p (w n) -> p w n", w=2)

        def load_gate(eng, l, s):
            for w in range(2):
                eng.dma_start(gtb[:, w, :], modd[l, w, D * s:D * s + D].partition_broadcast(P)).then_inc(gate_in, 16)

        def dve_resid(dve, n, blocks):
            p = plan_lin(n, blocks)
            i = 0
            tmp = [Z[:, 7168:7680], Z[:, 7680:8192]]
            n["gate"] = n.get("gate", 0) + 32
            dve.wait_ge(gate_in, n["gate"])
            for c0, c1, ts, *_ in blocks:
                for t in ts:
                    dve.wait_ge(mm_done, p.done(i))
                    nc.vector.tensor_tensor(tmp[i % 2], bank(i % 8), gtb[:, t // TL, c0:c1], ALU.mult).then_inc(evac_v, 1)
                    dve.drain()
                    nc.vector.tensor_tensor(xl[:, t, c0:c1], xl[:, t, c0:c1], tmp[i % 2], ALU.add)
                    i += 1

        XK = lambda t: Z[:, 1024 + 1024 * t:2048 + 1024 * t]
        rw = Z[:, 5200:5488].rearrange("p (k n) -> p k n", k=KT)
        rb = Z[:, 5488:5524]

        def rt(i, w=32):
            return Z[:, 5600 + 128 * i:5600 + 128 * i + TL * w].rearrange("p (t n) -> p t n", t=TL)

        LG = Z[:, 7400:7400 + 36 * TL].rearrange("p (t n) -> p t n", t=TL)
        sc = lambda i: Z[:, 7600 + TL * i:7600 + TL * i + TL]
        WT = [Z[:, 7700:7704], Z[:, 7704:7708]]
        IDX = Z[:, 7712:7720].bitcast(I32).rearrange("p (c t) -> p c t", c=2)
        TOK = Z[:, 7720:7724].bitcast(I32)
        ROWS = Z[:, 7724:7748].bitcast(I32)
        IDC = Z[:, 7748:7749].bitcast(I32)
        ZERO = Z[:, 7750:7774].bitcast(I32)
        EID = Z[0:1, 7780:7828].bitcast(I32)
        NIT = Z[0:1, 7828:7829].bitcast(I32)

        def pool_route_params(pool):
            pool.dma_start(rw[:, :, 0:NG], I["router_group_w"][0].rearrange("(k p) n -> p k n", p=P)).then_inc(rparams, 16)
            pool.dma_start(rw[:, :, NG:NG + NE], I["router_expert_w"][0].rearrange("(k p) n -> p k n", p=P)).then_inc(rparams, 16)
            pool.dma_start(rb[:, 0:NG], I["router_group_b"][0].partition_broadcast(P)).then_inc(rparams, 16)
            pool.dma_start(rb[:, NG:NG + NE], I["router_expert_b"][0].partition_broadcast(P)).then_inc(rparams, 16)
            pool.memset(ZERO, 0).then_inc(zero_ok, 1)
            pool.wait_ge(zero_ok, 2)
            pool.dma_start(rowtok.rearrange("(c p) a -> p (c a)", c=24), ZERO, allow_slow_non_contiguous=True).then_inc(rowz, 16)

        def plan_route(n):
            return Plan(n, "vvv")

        def pe_route(pe, n):
            p = plan_route(n)
            pe.wait_ge(rparams, 64)
            for t in range(TL):
                for k in range(KT):
                    last = nc.tensor.matmul(bank(0)[:, 36 * t:36 * t + 36], hTk[:, k, 128 * t:128 * t + 128], rw[:, k, :],
                                            start=(k == 0), stop=(k == KT - 1))
            last.then_inc(mm_done, 1)
            n["v2p"] += 1
            pe.wait_ge(v2p, n["v2p"])
            oh = rt(2)
            for t in range(TL):
                for u in range(t + 1):
                    last = nc.tensor.matmul(bank(1)[:, 32 * t:32 * t + 32], C(C_US) if u == t else C(C_ONE), oh[:, u, :],
                                            start=(u == 0), stop=(u == t))
            last.then_inc(mm_done, 1)
            for u in range(TL):
                last = nc.tensor.matmul(bank(2)[:, 0:32], C(C_ONE), oh[:, u, :], start=(u == 0), stop=(u == TL - 1))
            last.then_inc(mm_done, 1)

        def act_route(act, n):
            plan_route(n)
            for src, dst in ((LG[:, :, 0:NG], rt(6, NG)), (sc(5), sc(6))):
                n["v2a"] += 1
                act.wait_ge(v2a, n["v2a"])
                act.activation(dst, src, ACT.Exp).then_inc(a2v, 1)

        def dve_route(dve, n):
            p = plan_route(n)
            V = nc.vector
            D_ = dve.drain

            def bc(a, w):
                return a.unsqueeze(2).broadcast_to([P, TL, w])

            def first(dst, src, mx, w):
                V.tensor_reduce(mx, src, AX, ALU.max)
                D_()
                V.tensor_tensor(rt(7, w), src, bc(mx, w), ALU.is_equal)
                D_()
                V.tensor_tensor(rt(8, w), rt(7, w), C(C_I32 + 32 - w, w).unsqueeze(1).broadcast_to([P, TL, w]), ALU.mult)
                D_()
                V.tensor_reduce(sc(9), rt(8, w), AX, ALU.max)
                D_()
                V.tensor_tensor(dst, rt(8, w), bc(sc(9), w), ALU.is_equal)
                D_()

            V.tensor_copy(TOK, C(C_TK, TL))
            dve.wait_ge(rparams, 64)
            dve.wait_ge(mm_done, p.done(0))
            V.tensor_tensor(LG, bank(0)[:, 0:36 * TL].rearrange("p (t n) -> p t n", t=TL), rb.unsqueeze(1).broadcast_to([P, TL, 36]),
                            ALU.add).then_inc(evac_v, 1)
            D_()
            g, e = LG[:, :, 0:NG], LG[:, :, NG:NG + NE]
            ohg, em, oh1, oh2, oh = rt(9, NG), rt(3), rt(0), rt(1), rt(2)
            first(ohg, g, sc(0), NG)
            V.tensor_tensor(g, g, bc(sc(0), NG), ALU.subtract).then_inc(v2a, 1)
            n["a2v"] += 1
            dve.wait_ge(a2v, n["a2v"])
            V.tensor_reduce(sc(1), rt(6, NG), AX, ALU.add)
            D_()
            V.reciprocal(sc(2), sc(1))
            V.tensor_scalar(rt(10, NG), ohg, -1.0, -NEG, ALU.add, ALU.mult)
            v4 = lambda a: a.rearrange("p t (g x) -> p (t g) x", g=NG)
            b4 = lambda a: a.rearrange("p t g -> p (t g)").unsqueeze(2).broadcast_to([P, TL * NG, 8])
            for t in range(TL):
                V.tensor_tensor(em[:, t, :].rearrange("p (g x) -> p g x", g=NG), e[:, t, :].rearrange("p (g x) -> p g x", g=NG),
                                ohg[:, t, :].unsqueeze(2).broadcast_to([P, NG, 8]), ALU.mult)
            D_()
            V.tensor_tensor(v4(em), v4(em), b4(rt(10, NG)), ALU.add)
            D_()
            first(oh1, em, sc(3), 32)
            V.scalar_tensor_tensor(em, oh1, 2 * NEG, em, ALU.mult, ALU.add)
            D_()
            first(oh2, em, sc(4), 32)
            V.tensor_tensor(oh, oh1, oh2, ALU.add).then_inc(v2p, 1)
            V.tensor_tensor(sc(5), sc(4), sc(3), ALU.subtract).then_inc(v2a, 1)
            n["a2v"] += 1
            dve.wait_ge(a2v, n["a2v"])
            V.tensor_scalar(sc(7), sc(6), 1.0, None, ALU.add)
            D_()
            V.reciprocal(sc(8), sc(7))
            D_()
            V.tensor_tensor(WT[0], sc(8), sc(2), ALU.mult)
            D_()
            V.tensor_tensor(WT[1], WT[0], sc(6), ALU.mult)
            cnt, ov, oe, A_ = (Z[:, 7900 + 32 * i:7932 + 32 * i] for i in range(4))
            pos, gq, slot = rt(4), rt(5), rt(6)
            dve.wait_ge(mm_done, p.done(2))
            V.tensor_copy(pos, bank(1)[:, 0:128].rearrange("p (t n) -> p t n", t=TL)).then_inc(evac_v, 1)
            V.tensor_copy(cnt, bank(2)[:, 0:32]).then_inc(evac_v, 1)
            D_()
            V.tensor_scalar(ov, cnt, float(CAP), None, ALU.is_gt)
            for k in range(2, TL * P // CAP):
                D_()
                V.scalar_tensor_tensor(ov, cnt, float(CAP * k), ov, ALU.is_gt, ALU.add)
            D_()
            V.tensor_tensor_scan(oe, C(C_ONE, 32), ov, 0.0, ALU.mult, ALU.add)
            D_()
            V.tensor_tensor(A_, oe, ov, ALU.subtract)
            D_()
            V.tensor_scalar(A_, A_, float(NE - 1), float(CAP), ALU.add, ALU.mult)
            D_()
            V.tensor_tensor(A_, A_, C(C_E64, 32), ALU.subtract)
            V.tensor_scalar(gq, pos, float(CAP), None, ALU.is_ge)
            D_()
            V.tensor_tensor(gq, gq, A_.unsqueeze(1).broadcast_to([P, TL, 32]), ALU.mult)
            V.tensor_tensor(slot, pos, C(C_E64, 32).unsqueeze(1).broadcast_to([P, TL, 32]), ALU.add)
            D_()
            V.tensor_tensor(slot, slot, gq, ALU.add)
            D_()
            for c, o in enumerate((oh1, oh2)):
                V.tensor_tensor(rt(7 + c), slot, o, ALU.mult)
            D_()
            for c in range(2):
                V.tensor_reduce(sc(10 + c), rt(7 + c), AX, ALU.add)
            D_()
            for c in range(2):
                last = V.tensor_copy(IDX[:, c, :], sc(10 + c))
            last.then_inc(idx_ok, 1)
            ef = Z[0:1, 8100:8148]
            cm = Z[0:1, 8200:8712].rearrange("p (j e) -> p j e", j=16)
            V.tensor_scalar(ef[:, 0:32], C(C_E64, 32)[0:1], 1.0 / CAP, None, ALU.mult)
            V.tensor_tensor(cm, oe[0:1].unsqueeze(1).broadcast_to([1, 16, 32]), C(C_ROW, 16)[0:1].unsqueeze(2).broadcast_to([1, 16, 32]), ALU.is_le)
            V.tensor_scalar(Z[0:1, 8150:8158], C(C_ROW, 16)[0:1, 0:16:2], oe[0:1, 31:32], None, ALU.is_lt)
            D_()
            V.tensor_reduce(ef[:, 32:48], cm, AX, ALU.add)
            V.tensor_reduce(Z[0:1, 8160:8161], Z[0:1, 8150:8158], AX, ALU.add)
            D_()
            V.tensor_scalar(ef[:, 32:48], ef[:, 32:48], float(NE - 1), None, ALU.min)
            V.tensor_scalar(NIT, Z[0:1, 8160:8161], float(NE // 2), None, ALU.add)
            D_()
            V.tensor_copy(EID, ef)

        def pool_route(pool):
            pool.wait_ge(idx_ok, 1)
            pool.wait_ge(rowz, 16)
            for c in range(2):
                for t in range(TL):
                    pool.indirect_dma_start(rowtok, bass.IndirectOffsetOnAxis(ap=IDX[:, c, t:t + 1].bitcast(U32), axis=0),
                                            TOK[:, t:t + 1], None).then_inc(scat, 16)
            pool.wait_ge(scat, 16 * 2 * TL)
            pool.dma_start(ROWS, rowtok.rearrange("(c p) a -> p (c a)", c=24), allow_slow_non_contiguous=True).then_inc(rows_in, 16)
            pool.wait_ge(rows_in, 16)

        mslot = [ring[:, 0:HALF], ring[:, HALF:2 * HALF]] + [pj[:, HALF * i:HALF * i + HALF] for i in range(4)]
        xg = Z[:, 0:1024]
        xgT = Z[:, 1024:2048].rearrange("p (k n) -> p k n", k=KT)
        hg, hu, hd, yo = Z[:, 2048:2560], Z[:, 2560:3072], Z[:, 3072:3584], Z[:, 3584:4608]
        WE = [I["expert_w_gate"][0], I["expert_w_up"][0], I["expert_w_down"][0]]

        def trips(eng):
            return eng.value_load(NIT, min_val=NE // 2, max_val=NBLK // 2)

        def load_expert(sp, m, x, e):
            dst = mslot[2 * m + x].rearrange("p (k n) -> p k n", n=EH if m < 2 else D)
            sp.dma_start(dst, WE[m][e].rearrange("a (k p) n -> p (a k) n", p=P)).then_inc(w_in_[2 * m + x], 16)

        def sp_moe(sp):
            with sp.Fori(1, trips(sp)) as i:
                e = [sp.value_load(EID[:, bass.ds(2 * i + x, 1)], min_val=0, max_val=NE - 1) for x in range(2)]
                for m in range(3):
                    sp.wait_ge(w_used[m], i + 1)
                    for x in range(2):
                        load_expert(sp, m, x, bass.ds(e[x], 1))

        def pool_moe(pool):
            with pool.Fori(0, trips(pool)) as i:
                pool.wait_ge(xt_done, 2 * i + 2)
                pool.tensor_copy(IDC, ROWS[:, bass.ds(i, 1)])
                pool.drain()
                pool.indirect_dma_start(xg, None, xnd, bass.IndirectOffsetOnAxis(ap=IDC.bitcast(U32), axis=0)).then_inc(xg_in, 16)

        def pe_moe(pe):
            nit = trips(pe)
            for s in w_used:
                pe.sem_inc(s, 1)
            pe.sem_inc(xt_done, 2)
            with pe.Fori(0, nit) as i:
                pe.wait_ge(xg_in, 16 * i + 16)
                for b in range(2):
                    for k in range(4):
                        last = nc.tensor.transpose(bank(b)[:, 128 * k:128 * k + 128], xg[:, 512 * b + 128 * k:512 * b + 128 * k + 128], ident)
                    last.then_inc(xt_done, 1)
                pe.wait_ge(xt_a, i + 1)
                pe.wait_ge(xt_v, i + 1)
                for m in range(2):
                    for x in range(2):
                        pe.wait_ge(w_in_[2 * m + x], 16 * i + 16)
                    for k in range(KT):
                        for x in range(2):
                            last = nc.tensor.matmul(bank(2 + m)[64 * x:64 * x + 64, :], xgT[:, k, 64 * x:64 * x + 64],
                                                    mslot[2 * m + x][:, 512 * k:512 * k + 512], start=(k == 0), stop=(k == KT - 1))
                    last.then_inc(w_used[m], 1)
                pe.wait_ge(hu_ok, i + 1)
                for k in range(4):
                    last = nc.tensor.transpose(bank(4)[:, 128 * k:128 * k + 128], hu[:, 128 * k:128 * k + 128], ident)
                last.then_inc(ht_done, 1)
                pe.wait_ge(ht_a, i + 1)
                for x in range(2):
                    pe.wait_ge(w_in_[4 + x], 16 * i + 16)
                for b in range(2):
                    for k in range(4):
                        for x in range(2):
                            last = nc.tensor.matmul(bank(5 + b)[64 * x:64 * x + 64, :], hd[:, 128 * k + 64 * x:128 * k + 64 * x + 64],
                                                    mslot[4 + x][:, 1024 * k + 512 * b:1024 * k + 512 * b + 512], start=(k == 0), stop=(k == 3))
                last.then_inc(w_used[2], 1)

        def act_moe(act):
            nit = trips(act)
            with act.Fori(0, nit) as i:
                act.wait_ge(xt_done, 2 * i + 3)
                for k in range(4):
                    last = act.activation(xgT[:, k, :], bank(0)[:, 128 * k:128 * k + 128], ACT.Identity,
                                          scale=Ac[:, 0, 0, 1, k:k + 1], bias=modc[:, 0, 24 + k:25 + k])
                last.then_inc(xt_a, 1)
                act.wait_ge(w_used[0], i + 2)
                act.activation(hg, bank(2), ACT.Silu).then_inc(silu_ok, 1)
                act.wait_ge(ht_done, i + 1)
                act.activation(hd, bank(4), ACT.Copy).then_inc(ht_a, 1)
                act.wait_ge(w_used[2], i + 2)
                act.wait_ge(y_out, 16 * i + 16)
                act.activation(yo[:, 0:512], bank(5), ACT.Copy).then_inc(y_a, 1)
                act.wait_ge(y_a, i + 1)
                act.wait_ge(y_v, i + 1)
                act.dma_start(ybuf[bass.ds(i * P, P), :], yo).then_inc(y_out, 16)
            act.wait_ge(y_out, 16 * nit + 16)
            act.sem_inc(y_stored, 1)

        def dve_moe(dve):
            with dve.Fori(0, trips(dve)) as i:
                dve.wait_ge(xt_done, 2 * i + 4)
                for k in range(4):
                    last = nc.vector.tensor_scalar(xgT[:, 4 + k, :], bank(1)[:, 128 * k:128 * k + 128], Ac[:, 0, 0, 1, 4 + k:5 + k],
                                                   modc[:, 0, 28 + k:29 + k], ALU.mult, ALU.add)
                last.then_inc(xt_v, 1)
                dve.wait_ge(silu_ok, i + 1)
                dve.wait_ge(w_used[1], i + 2)
                nc.vector.tensor_tensor(hu, hg, bank(3), ALU.mult).then_inc(hu_ok, 1)
                dve.wait_ge(w_used[2], i + 2)
                dve.wait_ge(y_out, 16 * i + 16)
                nc.vector.tensor_copy(yo[:, 512:1024], bank(6)).then_inc(y_v, 1)

        yg = [[Z[:, 1024 * (2 * i + c):1024 * (2 * i + c) + 1024] for c in range(2)] for i in range(2)]
        fng = Z[:, 4608:5632]

        def pool_comb(pool, n):
            for t in range(TL):
                if t >= 2:
                    pool.wait_ge(yg_free, t - 1)
                for c in range(2):
                    pool.indirect_dma_start(yg[t % 2][c], None, ybuf, bass.IndirectOffsetOnAxis(ap=IDX[:, c, t:t + 1].bitcast(U32), axis=0)
                                            ).then_inc(yg_in[t % 2], 16)

        def dve_comb(dve, n):
            n["gate"] += 32
            dve.wait_ge(gate_in, n["gate"])
            for t in range(TL):
                dve.wait_ge(yg_in[t % 2], 32 * (t // 2 + 1))
                y0, y1 = yg[t % 2]
                nc.vector.tensor_scalar(y0, y0, WT[0][:, t:t + 1], None, ALU.mult)
                dve.drain()
                nc.vector.scalar_tensor_tensor(y0, y1, WT[1][:, t:t + 1], y0, ALU.mult, ALU.add)
                dve.drain()
                nc.vector.tensor_tensor(y0, y0, gtb[:, 0, :], ALU.mult)
                dve.drain()
                nc.vector.tensor_tensor(xl[:, t, :], xl[:, t, :], y0, ALU.add).then_inc(yg_free, 1)

        def act_final(act, n):
            act.wait_ge(yg_free, TL)
            for t in range(TL):
                act.activation(junk, xl[:, t, :], ACT.Square, accum_out=st[:, t:t + 1])
                act.drain()
            act.activation(st[:, 16:20], st[:, 0:4], ACT.Copy).then_inc(sumsq, 1)
            n["var"] += 1
            act.wait_ge(var, n["var"])
            act.activation(st[:, 24:28], st[:, 8:12], ACT.Sqrt).then_inc(std, 1)

        def dve_final(dve, n):
            n["ss"] += 1
            dve.wait_ge(sumsq, n["ss"])
            nc.vector.tensor_scalar(st[:, 8:12], st[:, 16:20], 1.0 / D, EPS, ALU.mult, ALU.add).then_inc(var, 1)
            n["std"] += 1
            dve.wait_ge(std, n["std"])
            nc.vector.reciprocal(st[:, 32:36], st[:, 24:28])
            dve.drain()
            for t in range(TL):
                nc.vector.scalar_tensor_tensor(xl[:, t, :], xl[:, t, :], st[:, 32 + t:33 + t], fng, ALU.mult, ALU.mult)

        TQ = (ALLT, LAT)
        BL2 = [[(NK, NV, ALLT, "a"), (NQ, GU, TQ[l], "a"), (GMV, CQ, TQ[l], "a"), (CQ, GATES, TQ[l], "a"), (CKV, NQ, ALLT, "a"),
                (GU, GMV, TQ[l], "a"), (NV, CKV, ALLT, "a")] for l in range(2)]
        lng, lnb = Z[:, 8588:9100], Z[:, 9100:9612]
        cqg, ckg, qg, kg = Z[:, 9612:9868], Z[:, 9868:9996], Z[:, 9996:10092], Z[:, 10092:10188]
        wsr = Z[:, 10188:10700].rearrange("p (g q) -> p g q", g=4)
        wsT = Z[:, 8076:8588]
        rpt = Z[:, 7948:8076]
        tbt = [hT[:, 0:1792], hT[:, 1792:3584]]
        Qf = hT[:, 0:4608].rearrange("p (t n) -> p t n", t=TA)
        cqT = Z[:, 0:1536].rearrange("p (k n) -> p k n", k=2)
        ckT = Z[:, 1536:2304].rearrange("p (k n) -> p k n", k=1)
        rpbd = nc.dram_tensor("rpbd", (2, 120, 64 * P), F32, kind="Internal")

        def pool_params2(pool, l):
            for dst, name in ((lng, "gm_ln_g_2"), (lnb, "gm_ln_b_2"), (cqg, "mla_cq_gain_2"), (ckg, "mla_ckv_gain_2"),
                              (qg, "mla_q_gain_2"), (kg, "mla_k_gain_2")):
                pool.dma_start(dst, I[name][l].partition_broadcast(P)).then_inc(prm2, 16)
            pool.dma_start(wsr, I["gm_w_s_2"][l].rearrange("g p q -> p g q")).then_inc(prm2, 16)
            pool.memset(rpt, 0.0).then_inc(rp_ok, 1)
            pool.wait_ge(rp_ok, l + 1)
            pool.dma_start(rpt[0:120, 48:79], I["na_rpb_2"][l].rearrange("h r c -> (h r) c")).then_inc(rp_in, 16)
            pool.wait_ge(rp_in, 32 * l + 16)
            pool.dma_start(rpbd.ap()[l].rearrange("r (m n) -> r m n", n=P), rpt[0:120, :].unsqueeze(1).broadcast_to([120, 64, P])).then_inc(rp_in, 16)
            pool.wait_ge(rp_in, 32 * l + 32)

        def pool_bias(pool, l, pairs):
            for q in pairs:
                if q >= 2:
                    pool.wait_ge(tb_free, 4 * l + q - 1)
                t4 = tbt[q % 2].rearrange("p (h j c) -> p h j c", h=2, j=14)
                for h in range(2):
                    for half in range(2):
                        off = (l * 120 + (2 * q + h) * 15 + 1 - half) * 64 * P + 63
                        src = bass.AP(tensor=rpbd, offset=off, ap=[[P - 1, 64], [64 * P, 14], [1, 64]])
                        pool.dma_start(t4[64 * half:64 * half + 64, h], src).then_inc(tb_in[q % 2], 16)
                pool.wait_ge(tb_in[q % 2], 64 * (2 * l + q // 2 + 1))
                m = C(C_NM, 64).unsqueeze(1).broadcast_to([P, 28, 64])
                b = C(C_NB, 64).unsqueeze(1).broadcast_to([P, 28, 64])
                t3 = tbt[q % 2].rearrange("p (j c) -> p j c", c=64)
                pool.tensor_tensor(t3, t3, m, ALU.mult)
                pool.drain()
                pool.tensor_tensor(t3, t3, b, ALU.add).then_inc(tb_ok, 1)

        raw = [ring[:, 2048 * i:2048 * i + 2048] for i in range(4)]

        WP = [[w[:, 2048 * i:2048 * i + 2048] for w in (wp_hi, wp_lo)] for i in range(2)]

        class Proj:
            def __init__(self, n, l):
                self.fp, self.hu = n.get("fp", 0), n.get("hu", 0)
                self.plan = plan_lin(n, BL2[l])
                self.pieces, self.used, i, halves = [], [], 0, self.hu
                for j, (c0, c1, ts, _) in enumerate(BL2[l]):
                    for k0, k1 in ((0, 4), (4, 8)) if c1 - c0 > 256 else ((0, 8),):
                        self.pieces.append((j, k0, k1, i))
                        if k1 == KT:
                            self.used.append((mm_done, self.plan.done(i + len(ts) - 1)))
                        else:
                            halves += 1
                            self.used.append((half_used, halves))
                    i += len(ts)
                n["fp"], n["hu"] = self.fp + len(self.pieces), halves

        def sp_proj(sp, n, l, rel):
            R = Proj(n, l)
            for x, (j, k0, k1, _) in enumerate(R.pieces):
                c0, c1 = BL2[l][j][:2]
                if x >= 2:
                    sp.wait_ge(w_lo_ok, R.fp + x - 1)
                sp.dma_start(raw[x % 2][:, 0:(k1 - k0) * (c1 - c0)].rearrange("p (k n) -> p k n", n=c1 - c0),
                             I["w_in_2"][l][P * k0:P * k1, c0:c1].rearrange("(k p) n -> p k n", p=P)).then_inc(proj_in[x % 2], 16)
            sp.wait_ge(*R.used[-1])
            sp.wait_ge(*R.used[-2])
            rel[0] = rel[1] = 0

        def proj_width(l, R, x):
            j, k0, k1, _ = R.pieces[x]
            return (k1 - k0) * (BL2[l][j][1] - BL2[l][j][0])

        def proj_round(act, n, l, R, x):
            if x >= len(R.pieces):
                return
            w = proj_width(l, R, x)
            act.wait_ge(proj_in[x % 2], 16 * (len(R.pieces) // 2 * l + x // 2 + 1))
            if x >= 2:
                act.wait_ge(*R.used[x - 2])
            act.activation(WP[x % 2][0][:, 0:w], raw[x % 2][:, 0:w], ACT.Copy).then_inc(wr_ok, 1)

        def pool_proj(pool, n, l):
            R = Proj(n, l)
            for x in range(len(R.pieces)):
                w = proj_width(l, R, x)
                n["wr"] = n.get("wr", 0) + 1
                pool.wait_ge(wr_ok, n["wr"])
                pool.tensor_tensor(WP[x % 2][1][:, 0:w], raw[x % 2][:, 0:w], WP[x % 2][0][:, 0:w], ALU.subtract).then_inc(w_lo_ok, 1)

        def pe_proj(pe, n, l):
            R = Proj(n, l)
            for x, (j, k0, k1, g0) in enumerate(R.pieces):
                c0, c1, ts, _ = BL2[l][j]
                pe.wait_ge(w_lo_ok, R.fp + x + 1)
                W = [w[:, 0:(k1 - k0) * (c1 - c0)].rearrange("p (k n) -> p k n", n=c1 - c0) for w in WP[x % 2]]
                for i, t in enumerate(ts, g0):
                    if k0 == 0 and i >= 8:
                        pe.wait_ge(evac_a, R.plan.val[i - 8])
                    for k in range(k0, k1):
                        last = three(bank(i % 8, c1 - c0), hhk[:, k, P * t:P * t + P], hmk[:, k, P * t:P * t + P],
                                     W[0][:, k - k0, :], W[1][:, k - k0, :], k == 0, k == KT - 1)
                    if k1 == KT:
                        last.then_inc(mm_done, 1)
                    elif t == ts[-1]:
                        last.then_inc(half_used, 1)

        def three(out_, a_hi, a_lo, b_hi, b_lo, first, final):
            nc.tensor.matmul(out_, a_hi, b_hi, start=first, stop=False)
            nc.tensor.matmul(out_, a_hi, b_lo, start=False, stop=False)
            return nc.tensor.matmul(out_, a_lo, b_hi, start=False, stop=final)

        def act_project(act, n, l):
            R = Proj(n, l)
            p = R.plan
            i, x = 0, 0
            proj_round(act, n, l, R, 0)
            proj_round(act, n, l, R, 1)
            for j, (c0, c1, ts, _) in enumerate(BL2[l]):
                if R.pieces[x][2] < KT:
                    proj_round(act, n, l, R, x + 2)
                    x += 1
                for m, t in enumerate(ts):
                    if j == 5 and m == 2:
                        rms_heads(act, "a", n, ALLT, hv(CKV, 1, 128), 1, 128, ckg)
                    act.wait_ge(mm_done, p.done(i))
                    f = ACT.Gelu if c0 in (GU, GMV) else ACT.Copy
                    act.activation(pjt[:, t, c0:c1], bank(i % 8, c1 - c0), f).then_inc(evac_a, 1)
                    i += 1
                proj_round(act, n, l, R, x + 2)
                x += 1
                if j == 1:
                    rms_heads(act, "a", n, ALLT, hv(NK, 8, 64), 8, 64, None)
                elif j == 2:
                    rms_heads(act, "a", n, TQ[l], hv(NQ, 8, 64), 8, 64, None)
                elif j == 3:
                    n["var"] += 1
                    act.wait_ge(var, n["var"])
                    act.activation(st[:, 320:320 + len(TQ[l])], st[:, 260:260 + len(TQ[l])], ACT.Sqrt).then_inc(std, 1)
                elif j == 4:
                    rms_heads(act, "a", n, TQ[l], hv(CQ, 1, 256), 1, 256, cqg)

        def dve_project(dve, n, l):
            V = nc.vector
            p = Proj(n, l).plan
            ends, i = [], 0
            for b in BL2[l]:
                i += len(b[2])
                ends.append(p.val[i - 1])
            nt = len(TQ[l])
            dve.wait_ge(prm2, 16 * 7 * (l + 1))
            dve.wait_ge(evac_a, ends[0])
            rms_heads(dve, "v", n, ALLT, hv(NK, 8, 64), 8, 64, None)
            dve.drain()
            dve.wait_ge(evac_a, ends[1])
            rms_heads(dve, "v", n, TQ[l], hv(NQ, 8, 64), 8, 64, None)
            dve.drain()
            dve.wait_ge(evac_a, ends[2])
            vv = lambda t: pjt[:, t, GMV:GMV + 512]
            sq = [Z[:, 0:512], Z[:, 512:1024]]
            for t in TQ[l]:
                V.tensor_reduce(st[:, 500 + t:501 + t], vv(t), AX, ALU.add)
            dve.drain()
            V.tensor_scalar(st[:, 510:510 + nt], st[:, 500:500 + nt], 1.0 / 512, None, ALU.mult)
            dve.drain()
            for t in TQ[l]:
                V.tensor_scalar(vv(t), vv(t), st[:, 510 + t:511 + t], None, ALU.subtract)
            dve.drain()
            for t in TQ[l]:
                V.tensor_tensor(sq[t % 2], vv(t), vv(t), ALU.mult)
                dve.drain()
                V.tensor_reduce(st[:, 200 + t:201 + t], sq[t % 2], AX, ALU.add)
            dve.drain()
            V.tensor_scalar(st[:, 260:260 + nt], st[:, 200:200 + nt], 1.0 / 512, EPS, ALU.mult, ALU.add).then_inc(var, 1)
            n["std"] += 1
            dve.wait_ge(std, n["std"])
            V.reciprocal(st[:, 380:380 + nt], st[:, 320:320 + nt])
            dve.drain()
            for t in TQ[l]:
                V.scalar_tensor_tensor(vv(t), vv(t), st[:, 380 + t:381 + t], lng, ALU.mult, ALU.mult)
            dve.drain()
            for t in TQ[l]:
                V.tensor_tensor(vv(t), vv(t), lnb, ALU.add)
            dve.drain()
            dve.wait_ge(evac_a, ends[3])
            rms_heads(dve, "v", n, TQ[l], hv(CQ, 1, 256), 1, 256, cqg)
            dve.drain()
            dve.wait_ge(evac_a, ends[4])
            rms_heads(dve, "v", n, ALLT, hv(CKV, 1, 128), 1, 128, ckg)

        def na_spec(l):
            def src(q):
                return lambda side, t: pjt[:, t, (NK if side == "k" else NQ) + 128 * q:(NK if side == "k" else NQ) + 128 * q + 128]

            def gain(side):
                r = (R_NAK if side == "k" else R_NAQ) + l
                return cols[:, r:r + 1]

            def biased(q, h, t):
                def f(E, b):
                    nc.vector.scalar_tensor_tensor(E[:, 0:512], b[:, 0:512], 64 ** -0.5,
                                                   tbt[q % 2][:, 896 * (h % 2) + 64 * (6 - 2 * t):896 * (h % 2) + 64 * (6 - 2 * t) + 512],
                                                   ALU.mult, ALU.add)
                    return nc.vector.tensor_scalar(E[:, 512:768], b[:, 512:768], 64 ** -0.5, None, ALU.mult)
                return f
            heads = [(P, src(q), TQ[l], gain) for q in range(4)]
            units = [dict(head=h // 2, rows=((64 * (h % 2), 64 * (h % 2) + 64),), qt=t, keys=ALLT if t < TL else (4, 5),
                          bias=biased(h // 2, h, t) if t < TL else None, scale=64 ** -0.5, combine=False,
                          v=lambda kt, h=h: pjt[:, kt, NV + 64 * h:NV + 64 * h + 64], dv=64,
                          y=pjt[:, t, NQ + 64 * h:NQ + 64 * h + 64]) for h in range(8) for t in TQ[l]]
            return heads, units

        def mla_spec(l):
            def src(h):
                return lambda side, t: pjt[:, t, GMV + 96 * h:GMV + 96 * h + 96] if side == "k" else Qf[:, t, 96 * h:96 * h + 96]
            heads = [(96, src(h), TQ[l], None) for h in range(8)]
            units = [dict(head=h, rows=((0, 96),), qt=t, keys=ALLT if t < TL else (4, 5), bias=None, scale=96 ** -0.5, combine=False,
                          v=lambda kt, h=h: pjt[:, kt, 128 * h + 64:128 * h + 128], dv=64,
                          y=Qf[:, t, 64 * h:64 * h + 64]) for h in range(8) for t in TQ[l]]
            return heads, units

        def plan_gm(n, l):
            return Plan(n, "a" + "v" * len(TQ[l]))

        def pe_gm(pe, n, l):
            p = plan_gm(n, l)
            pe.wait_ge(prm2, 16 * 7 * (l + 1))
            for g in range(4):
                last = nc.tensor.transpose(bank(7)[:, P * g:P * g + P], wsr[:, g, :], ident)
            last.then_inc(mm_done, 1)
            pe.wait_ge(evac_a, p.val[0])
            for i, t in enumerate(TQ[l]):
                for g in range(4):
                    last = nc.tensor.matmul(bank(i)[:, P * g:P * g + P], wsT[:, P * g:P * g + P], pjt[:, t, GMV + P * g:GMV + P * g + P],
                                            start=True, stop=True)
                last.then_inc(mm_done, 1)

        def act_gm(act, n, l):
            p = plan_gm(n, l)
            act.wait_ge(mm_done, p.done(0))
            act.activation(wsT, bank(7), ACT.Copy).then_inc(evac_a, 1)

        def dve_gm(dve, n, l):
            p = plan_gm(n, l)
            for i, t in enumerate(TQ[l]):
                dve.wait_ge(mm_done, p.done(1 + i))
                for g in range(4):
                    u = pjt[:, t, GU + P * g:GU + P * g + P]
                    last = nc.vector.scalar_tensor_tensor(u, bank(i)[:, P * g:P * g + P], cols[:, R_BS + 4 * l + g:R_BS + 4 * l + g + 1], u,
                                                          ALU.add, ALU.mult)
                last.then_inc(evac_v, 1)

        def plan_t(n, pairs):
            return Plan(n, ("av" * len(pairs))[:-(-len(pairs) // 4)])

        def pe_t(pe, n, pairs):
            p = plan_t(n, pairs)
            for i in range(len(p.own)):
                if i >= 8:
                    pe.wait_ge(EV[p.own[i - 8]], p.val[i - 8])
                for j, (src, _) in enumerate(pairs[4 * i:4 * i + 4]):
                    last = nc.tensor.transpose(bank(i % 8)[:, P * j:P * j + P], src, ident)
                last.then_inc(mm_done, 1)

        def each_t(eng, n, who, pairs):
            p = plan_t(n, pairs)
            for i in range(len(p.own)):
                if p.own[i] == who:
                    eng.wait_ge(mm_done, p.done(i))
                    for j, (_, dst) in enumerate(pairs[4 * i:4 * i + 4]):
                        b = bank(i % 8)[:, P * j:P * j + P]
                        last = nc.scalar.activation(dst, b, ACT.Copy) if who == "a" else nc.vector.tensor_copy(dst, b)
                    last.then_inc(EV[who], 1)

        def cqkv_pairs(l):
            return ([(pjt[:, t, CQ + P * k:CQ + P * k + P], cqT[:, k, P * t:P * t + P]) for t in TQ[l] for k in range(2)]
                    + [(pjt[:, t, CKV:CKV + P], ckT[:, 0, P * t:P * t + P]) for t in ALLT])

        def BUQ(l):
            return [(0, 512, TQ[l]), (512, 768, TQ[l])]

        BUKV = [(0, 512, ALLT, "a"), (512, 1024, ALLT, "a")]
        q_lhs = lambda k, t: 2 if k is None else cqT[:, k, P * t:P * t + P]
        kv_lhs = lambda k, t: 1 if k is None else ckT[:, 0, P * t:P * t + P]
        act_q = lambda c0, c1, t, b: nc.scalar.activation(Qf[:, t, c0:c1], b, ACT.Copy)
        dve_q = lambda c0, c1, t, b: nc.vector.tensor_copy(Qf[:, t, c0:c1], b)

        kview = lambda t: pjt[:, t, GMV:GMV + 768].rearrange("p (h d) -> p h d", h=8)
        qview = lambda t: Qf[:, t, :].rearrange("p (h d) -> p h d", h=8)

        def rope_heads(dve, view, x0):
            for t in LAT:
                x = x0 + 512 * (t % 2)
                dve_rope(dve, t, view(t)[:, :, 64:96], 8, 8, C_R2C, C_R2S, Z[:, x:x + 256], Z[:, x + 256:x + 512])

        def dve_mla_queries(dve, n, l):
            plan_lin(n, BUKV)
            rms_heads(dve, "v", n, TQ[l], qview, 8, 96, qg, at=3072)
            dve.drain()
            rope_heads(dve, qview, 5120)

        def dve_mla_keys(dve, n, l):
            for t in ALLT:
                nc.vector.tensor_copy(kview(t)[:, :, 0:64], pjt[:, t, 0:1024].rearrange("p (h d) -> p h d", h=8)[:, :, 0:64])
                nc.vector.tensor_copy(kview(t)[:, :, 64:96], pjt[:, t, KR:KR + 32].unsqueeze(1).broadcast_to([P, 8, 32]))
            dve.drain()
            rms_heads(dve, "v", n, ALLT, kview, 8, 96, kg)
            dve.drain()
            rope_heads(dve, kview, 2048)

        yT = [Z[:, 0:3072].rearrange("p (k n) -> p k n", k=4), Z[:, 3072:6144].rearrange("p (k n) -> p k n", k=4),
              pj[:, 0:3072].rearrange("p (k n) -> p k n", k=4)]
        acc = pj[:, 3072:3072 + TA * D].rearrange("p (t n) -> p t n", t=TA)

        def nagm_pairs(l):
            return [(pjt[:, t, c + P * k:c + P * k + P], yT[b][:, k, P * t:P * t + P])
                    for t in TQ[l] for b, c in ((0, NQ), (1, GU)) for k in range(4)]

        def mla_pairs(l):
            return [(Qf[:, t, P * k:P * k + P], yT[2][:, k, P * t:P * t + P]) for t in TQ[l] for k in range(4)]

        sg = [Z[:, 6144:6656], Z[:, 6656:7168]]
        mtmp = [Z[:, 7168:7680], Z[:, 7680:8192]]
        WO = ("na_w_o_2", "gm_w_o_2", "mla_w_o_2")

        def plan_merge(n, l):
            return Plan(n, "av" * (6 * len(TQ[l])))

        mring = [ring[:, 2048 * i:2048 * i + 2048] for i in range(4)] + [Z[:, 8192:10240]]

        WM2 = [[w[:, 2048 * i:2048 * i + 2048].rearrange("p (k n) -> p k n", n=512) for w in (wm_hi, wm_lo)] for i in range(2)]

        def merge_counts(n, l):
            p = plan_merge(n, l)
            p.fp, p.hu = n.get("fp", 0), n.get("hu", 0)
            n["fp"], n["hu"] = p.fp + 12, p.hu + 6
            return p

        def sp_merge(sp, n, rel, l):
            p = merge_counts(n, l)
            nt = len(TQ[l])
            for x in range(18):
                j, y = x // 3, x % 3
                nb, b = j // 3, j % 3
                if x >= 5:
                    j0, y0 = (x - 5) // 3, (x - 5) % 3
                    if y0 == 2:
                        sp.wait_ge(mm_done, p.done(2 * nt * (j0 + 1) - 1))
                    else:
                        sp.wait_ge(w_lo_ok, p.fp + 2 * j0 + y0 + 1)
                if y < 2:
                    w = I["w_in_2"][l][512 * y:512 * y + 512, GATES + D * b + 512 * nb:GATES + D * b + 512 * nb + 512]
                else:
                    w = I[WO[b]][l][:, 512 * nb:512 * nb + 512]
                if x < 4 and rel[x // 2]:
                    sp.wait_ge(mm_done, rel[x // 2])
                sp.dma_start(mring[x % 5].rearrange("p (k n) -> p k n", n=512), w.rearrange("(k p) n -> p k n", p=P)).then_inc(mring_in[x % 5], 16)
            rel[0] = rel[1] = p.done(12 * nt - 1)

        def mring_value(l, x):
            return 16 * ((4 if x % 5 < 3 else 3) * l + x // 5 + 1)

        def merge_round(act, p, l, j, y):
            if j == 6:
                return
            x = 3 * j + y
            act.wait_ge(mring_in[x % 5], mring_value(l, x))
            if j:
                if y == 0:
                    act.wait_ge(half_used, p.hu + j)
                else:
                    act.wait_ge(mm_done, p.done(2 * len(TQ[l]) * j - 2))
            act.activation(wm_hi[:, 2048 * y:2048 * y + 2048], mring[x % 5], ACT.Copy).then_inc(wr_ok, 1)

        def pool_merge(pool, n, l):
            merge_counts(n, l)
            for j in range(6):
                for y in range(2):
                    n["wr"] += 1
                    pool.wait_ge(wr_ok, n["wr"])
                    pool.tensor_tensor(wm_lo[:, 2048 * y:2048 * y + 2048], mring[(3 * j + y) % 5], wm_hi[:, 2048 * y:2048 * y + 2048],
                                       ALU.subtract).then_inc(w_lo_ok, 1)

        def pe_merge(pe, n, l):
            p = merge_counts(n, l)
            nt = len(TQ[l])

            def half(y, k0, b, t):
                for k in range(4):
                    last = three(bank(b), hhk[:, k0 + k, P * t:P * t + P], hmk[:, k0 + k, P * t:P * t + P],
                                 WM2[y][0][:, k, :], WM2[y][1][:, k, :], k0 + k == 0, k0 + k == KT - 1)
                return last

            for j in range(6):
                pe.wait_ge(w_lo_ok, p.fp + 2 * j + 1)
                for t in TQ[l]:
                    if j:
                        pe.wait_ge(evac_a, p.val[2 * (nt * (j - 1) + t)])
                    last = half(0, 0, t, t)
                last.then_inc(half_used, 1)
                pe.wait_ge(w_lo_ok, p.fp + 2 * j + 2)
                x = 3 * j + 2
                pe.wait_ge(mring_in[x % 5], mring_value(l, x))
                w = mring[x % 5]
                for t in TQ[l]:
                    u = nt * j + t
                    half(1, 4, t, t).then_inc(mm_done, 1)
                    if u >= 2:
                        pe.wait_ge(evac_v, p.val[2 * (u - 2) + 1])
                    for k in range(4):
                        last = nc.tensor.matmul(bank(6 + u % 2), yT[j % 3][:, k, P * t:P * t + P], w[:, 512 * k:512 * k + 512], start=(k == 0), stop=(k == 3))
                    last.then_inc(mm_done, 1)

        def act_merge(act, n, l):
            p = merge_counts(n, l)
            act.wait_ge(unspill, 32 * (l + 1))
            act.activation(hT_hi[:, 0:3072], hT[:, 0:3072], ACT.Copy).then_inc(hh_back[0], 1)
            merge_round(act, p, l, 0, 0)
            merge_round(act, p, l, 0, 1)
            nt = len(TQ[l])
            for u in range(6 * nt):
                if u % nt == 0:
                    merge_round(act, p, l, u // nt + 1, 0)
                act.wait_ge(mm_done, p.done(2 * u))
                if u >= 2:
                    act.wait_ge(evac_v, p.val[2 * u - 3])
                act.activation(sg[u % 2], bank(u % nt), ACT.Sigmoid).then_inc(evac_a, 1)
                if u % nt == nt - 1:
                    merge_round(act, p, l, u // nt + 1, 1)

        def dve_merge(dve, n, l):
            p = merge_counts(n, l)
            nt = len(TQ[l])
            dve.wait_ge(unspill, 32 * (l + 1))
            nc.vector.tensor_copy(hT_hi[:, 3072:6144], hT[:, 3072:6144]).then_inc(hh_back[1], 1)
            for u in range(6 * nt):
                j, t = u // nt, u % nt
                nb, b = j // 3, j % 3
                dve.wait_ge(evac_a, p.val[2 * u])
                dve.wait_ge(mm_done, p.done(2 * u + 1))
                a = acc[:, t, 512 * nb:512 * nb + 512]
                dst = a if b == 0 else mtmp[u % 2]
                nc.vector.tensor_tensor(dst, sg[u % 2], bank(6 + u % 2), ALU.mult).then_inc(evac_v, 1)
                if b:
                    dve.drain()
                    nc.vector.tensor_tensor(a, a, mtmp[u % 2], ALU.add)

        hhk = hT_hi[:, :].rearrange("p (k n) -> p k n", k=KT)
        hlk = hT_lo[:, :].rearrange("p (k n) -> p k n", k=KT)
        hmk = hm_lo[:, :].rearrange("p (k n) -> p k n", k=KT)
        XM = lambda t: pj[:, D * t:D * t + D]
        NTMP = [[Z[:, 6144 - 3072 * m + 512 * i:6656 - 3072 * m + 512 * i] for i in range(3)] for m in range(2)]

        def plan_split(n, nt):
            p = Plan(n, "-" * (2 * nt))
            p.g0 = n.get("split", 0)
            n["split"] = p.g0 + 2 * nt
            return p

        def pe_norm_split(pe, n, nt, m):
            p = plan_split(n, nt)
            src = XM if m == 0 else lambda t: xn[t % 2]
            for t in range(nt):
                pe.wait_ge(xn_ok, n["xn"] + t + 1)
                for h in range(2):
                    i = 2 * t + h
                    if i >= 8:
                        pe.wait_ge(ht_tmp, p.g0 + i - 7)
                    for k in range(4):
                        last = nc.tensor.transpose(bank(i % 8)[:, 128 * k:128 * k + 128],
                                                   src(t)[:, 512 * h + 128 * k:512 * h + 128 * k + 128], ident)
                    last.then_inc(mm_done, 1)
            n["xn"] += nt

        def act_norm_split(act, n, nt, l, m):
            p = plan_split(n, nt)
            n["xn"] += nt
            act.dma_start(xspill[:, 0:nt * D], xl[:, 0:nt, :].rearrange("p t d -> p (t d)")).then_inc(x_out, 16)
            for t in range(nt):
                act.activation(junk, xl[:, t, :], ACT.Square, accum_out=st[:, t:t + 1])
                act.drain()
            act.activation(st[:, 16:16 + nt], st[:, 0:nt], ACT.Copy).then_inc(sumsq, 1)
            n["var"] += 1
            act.wait_ge(var, n["var"])
            act.activation(st[:, 24:24 + nt], st[:, 8:8 + nt], ACT.Sqrt).then_inc(std, 1)
            for i in range(2 * nt):
                t, h = i // 2, i % 2
                act.wait_ge(mm_done, p.done(i))
                if i >= 3:
                    act.wait_ge(hl_ok, p.g0 + i - 2)
                for k in range(4):
                    kk = 4 * h + k
                    c = 48 * (t // TL) + 24 * m + kk
                    last = act.activation(NTMP[m][i % 3][:, 128 * k:128 * k + 128], bank(i % 8)[:, 128 * k:128 * k + 128], ACT.Identity,
                                          scale=Ac[:, l, t // TL, m, kk:kk + 1], bias=modc[:, l, c:c + 1])
                last.then_inc(ht_tmp, 1)
                act.drain()
                act.activation(hhk[:, 4 * h:4 * h + 4, 128 * t:128 * t + 128], NTMP[m][i % 3].rearrange("p (k n) -> p k n", k=4),
                               ACT.Copy).then_inc(hh_ok, 1)
            act.wait_ge(x_out, 16 * (2 * l - 1 + m))

        def dve_norm_split(dve, n, nt, l, m):
            p = plan_split(n, nt)
            lo = (hmk, hlk)[m]
            n["ss"] += 1
            dve.wait_ge(sumsq, n["ss"])
            nc.vector.tensor_scalar(st[:, 8:8 + nt], st[:, 16:16 + nt], 1.0 / D, EPS, ALU.mult, ALU.add).then_inc(var, 1)
            n["std"] += 1
            dve.wait_ge(std, n["std"])
            nc.vector.reciprocal(st[:, 32:32 + nt], st[:, 24:24 + nt])
            dve.drain()
            def rest(u):
                for h in range(2):
                    i = 2 * u + h
                    dve.wait_ge(hh_ok, p.g0 + i + 1)
                    nc.vector.tensor_tensor(lo[:, 4 * h:4 * h + 4, 128 * u:128 * u + 128], NTMP[m][i % 3].rearrange("p (k n) -> p k n", k=4),
                                            hhk[:, 4 * h:4 * h + 4, 128 * u:128 * u + 128], ALU.subtract).then_inc(hl_ok, 1)

            if m == 0:
                for t in range(nt):
                    nc.vector.tensor_scalar(XM(t), xl[:, t, :], st[:, 32 + t:33 + t], None, ALU.mult).then_inc(xn_ok, 1)
                dve.drain()
                dve.wait_ge(x_out, 16 * (2 * l - 1))
                for t in range(nt):
                    rest(t)
                return
            for t in range(nt + 1):
                if t < nt:
                    if t >= 2:
                        dve.wait_ge(mm_done, p.done(2 * t - 3))
                    nc.vector.tensor_scalar(xn[t % 2], xl[:, t, :], st[:, 32 + t:33 + t], None, ALU.mult).then_inc(xn_ok, 1)
                if t >= 1:
                    rest(t - 1)

        WHI = [w_hi[:, 2048 * i:2048 * i + 2048] for i in range(2)]
        WLO = [w_lo[:, 2048 * i:2048 * i + 2048] for i in range(2)]
        H1 = [[h[:, 3072 * i:3072 * i + 3072].rearrange("p (m n) -> p m n", m=4) for h in (h1_hi, h1_lo)] for i in range(2)]
        yacc = pj[:, 0:6144].rearrange("p (t n) -> p t n", t=TA)
        rl = [Z[:, 8192:8704], Z[:, 8704:9216]]
        sqr = [Z[:, 9216:9728], Z[:, 9728:10240]]
        FH = D * 4 // 512

        class Ffn:

            def __init__(self, n, l):
                self.base = {k: n.get(k, 0) for k in ("fr", "fo", "fh", "fp")}
                spans = ((0, 512), (512, 768))[:2 if len(TQ[l]) > TL else 1]
                steps = [("h", 0)] + [x for hb in range(1, FH) for x in (("h", hb), ("y", hb - 1))] + [("y", FH - 1)]
                i, h, self.pieces, self.hcount, self.kind = 0, 0, [], [], []
                self.h_end = {}
                for kind, hb in steps:
                    for half in range(2):
                        gs = []
                        for what in ([(2 * half + m, c) for m in range(2) for c in spans] if kind == "h" else list(TQ[l])):
                            gs.append((i, what))
                            h += kind == "h"
                            self.hcount.append(h)
                            self.kind.append(kind)
                            i += 1
                        self.pieces.append((kind, hb, half, gs))
                    if kind == "h":
                        self.h_end[hb] = h
                self.plan = Plan(n, "-" * i)
                n["fr"], n["fo"], n["fh"], n["fp"] = self.base["fr"] + h, self.base["fo"] + i - h, self.base["fh"] + h, self.base["fp"] + len(self.pieces)

            def last(self, x):
                return self.plan.done(self.pieces[x][3][-1][0])

        def sp_ffn(sp, n, rel, l):
            F = Ffn(n, l)
            for x, (kind, hb, half, _) in enumerate(F.pieces):
                if x >= 4:
                    sp.wait_ge(w_lo_ok, F.base["fp"] + x - 3)
                elif rel[x // 2]:
                    sp.wait_ge(mm_done, rel[x // 2])
                if kind == "h":
                    w, d = I["ffn_w1_2"][l][:, 512 * hb + 256 * half:512 * hb + 256 * half + 256], 256
                else:
                    w, d = I["ffn_w2_2"][l][512 * hb:512 * hb + 512, 512 * half:512 * half + 512], 512
                sp.dma_start(raw[x % 4].rearrange("p (k n) -> p k n", n=d), w.rearrange("(k p) n -> p k n", p=P)).then_inc(raw_in[x % 4], 16)
            sp.wait_ge(w_lo_ok, n["fp"])
            rel[0] = rel[1] = 0

        def pe_ffn(pe, n, l):
            F = Ffn(n, l)
            for x, (kind, hb, half, groups) in enumerate(F.pieces):
                pe.wait_ge(w_lo_ok, F.base["fp"] + x + 1)
                if kind == "y":
                    pe.wait_ge(h1_lo_ok, F.base["fh"] + F.h_end[hb])
                for i, what in groups:
                    if i >= 8:
                        if F.kind[i - 8] == "h":
                            pe.wait_ge(h1_read, F.base["fr"] + F.hcount[i - 8])
                        else:
                            pe.wait_ge(out_read, F.base["fo"] + i - 7 - F.hcount[i - 8])
                    if kind == "h":
                        m, (c0, c1) = what
                        W = [w[x % 2].rearrange("p (k n) -> p k n", k=KT)[:, :, P * (m % 2):P * (m % 2) + P] for w in (WHI, WLO)]
                        for k in range(KT):
                            for a, r in ((0, hhk), (0, hlk), (1, hhk)):
                                last = nc.tensor.matmul(bank(i % 8, c1 - c0), W[a][:, k, :], r[:, k, c0:c1],
                                                        start=(k == 0 and r is hhk and a == 0), stop=(k == KT - 1 and a == 1))
                    else:
                        W = [w[x % 2].rearrange("p (k n) -> p k n", k=4) for w in (WHI, WLO)]
                        for k in range(4):
                            for a, b in ((0, 0), (0, 1), (1, 0)):
                                last = nc.tensor.matmul(bank(i % 8), H1[hb % 2][a][:, k, P * what:P * what + P], W[b][:, k, :],
                                                        start=(k == 0 and a == b), stop=(k == 3 and a == 1))
                    last.then_inc(mm_done, 1)

        def raw_slot_value(l, x):
            return 16 * (8 * l + x // 4 + 1)

        def act_ffn(act, n, l):
            F = Ffn(n, l)

            def split(x):
                if x >= len(F.pieces):
                    return
                act.wait_ge(raw_in[x % 4], raw_slot_value(l, x))
                if x >= 2:
                    act.wait_ge(mm_done, F.last(x - 2))
                act.activation(WHI[x % 2], raw[x % 4], ACT.Copy).then_inc(w_hi_ok, 1)

            split(0)
            split(1)
            for x, (kind, hb, half, groups) in enumerate(F.pieces):
                if kind == "h":
                    for i, (m, (c0, c1)) in groups:
                        act.wait_ge(mm_done, F.plan.done(i))
                        u = F.hcount[i] - 1
                        if u >= 2:
                            act.wait_ge(h1_lo_ok, F.base["fh"] + u - 1)
                        r = rl[u % 2][:, 0:c1 - c0]
                        act.activation(r, bank(i % 8, c1 - c0), ACT.Relu).then_inc(h1_read, 1)
                        act.drain()
                        act.activation(H1[hb % 2][0][:, m, c0:c1], r, ACT.Square).then_inc(h1_hi_ok, 1)
                split(x + 2)
            act.wait_ge(h1_lo_ok, n["fh"])
            load_gate(act, l + 1, 5)
            act.wait_ge(mm_done, F.last(len(F.pieces) - 1))
            nt = len(TQ[l])
            act.dma_start(xl[:, 0:nt, :].rearrange("p t d -> p (t d)"), xspill[:, 0:nt * D]).then_inc(x_back, 16)

        def dve_ffn(dve, n, l):
            F = Ffn(n, l)
            seen = F.base["fh"]

            def split(x):
                if x >= len(F.pieces):
                    return
                dve.wait_ge(w_hi_ok, len(F.pieces) * l + x + 1)
                nc.vector.tensor_tensor(WLO[x % 2], raw[x % 4], WHI[x % 2], ALU.subtract).then_inc(w_lo_ok, 1)

            split(0)
            split(1)
            for x, (kind, hb, half, groups) in enumerate(F.pieces):
                for i, what in groups:
                    if kind == "h":
                        m, (c0, c1) = what
                        u = F.hcount[i] - 1
                        q, r = (b[u % 2][:, 0:c1 - c0] for b in (sqr, rl))
                        dve.wait_ge(h1_read, F.base["fr"] + u + 1)
                        nc.vector.tensor_tensor(q, r, r, ALU.mult)
                        dve.drain()
                        seen += 1
                        dve.wait_ge(h1_hi_ok, seen)
                        nc.vector.tensor_tensor(H1[hb % 2][1][:, m, c0:c1], q, H1[hb % 2][0][:, m, c0:c1], ALU.subtract).then_inc(h1_lo_ok, 1)
                    else:
                        dve.wait_ge(mm_done, F.plan.done(i))
                        y = yacc[:, what, 512 * half:512 * half + 512]
                        if hb == 0:
                            nc.vector.tensor_copy(y, bank(i % 8)).then_inc(out_read, 1)
                        else:
                            nc.vector.tensor_tensor(y, y, bank(i % 8), ALU.add).then_inc(out_read, 1)
                if kind == "y" and half == 1:
                    dve.drain()
                split(x + 2)
            n["gate"] += 32
            dve.wait_ge(gate_in, n["gate"])
            for t in TQ[l]:
                nc.vector.tensor_tensor(yacc[:, t, :], yacc[:, t, :], gtb[:, t // TL, :], ALU.mult)
            dve.drain()
            dve.wait_ge(x_back, 16 * (2 * l + 2))
            for t in TQ[l]:
                nc.vector.tensor_tensor(xl[:, t, :], xl[:, t, :], yacc[:, t, :], ALU.add)

        def WO2(l):
            return [(0, 512, TQ[l], "v"), (512, 1024, TQ[l], "v")]

        def acc_pairs(l):
            return [(acc[:, t, P * k:P * k + P], hTk[:, k, P * t:P * t + P]) for t in TQ[l] for k in range(KT)]

        STAGES2 = 16

        def sp_layer(sp, n, rel, l):
            f0 = n["fence"]
            plan_split(n, TA)
            sp_proj(sp, n, l, rel)
            plan_attn(n, *na_spec(l))
            plan_gm(n, l)
            plan_t(n, cqkv_pairs(l))
            sp_lin(sp, n, rel, I["mla_w_uq_2"][l], BUQ(l))
            sp_lin(sp, n, rel, I["mla_w_ukv_2"][l], BUKV)
            plan_attn(n, *mla_spec(l))
            plan_t(n, nagm_pairs(l))
            plan_t(n, mla_pairs(l))
            sp.wait_ge(stage_done, f0 + 4 * 9)
            sp.dma_start(hT[:, 4608:6144], hTd[:, 4608:6144]).then_inc(unspill, 16)
            sp.wait_ge(stage_done, f0 + 4 * 11)
            sp.dma_start(hT[:, 0:4608], hTd[:, 0:4608]).then_inc(unspill, 16)
            sp_merge(sp, n, rel, l)
            plan_t(n, acc_pairs(l))
            sp_lin(sp, n, rel, I["w_out_2"][l], WO2(l))
            sp.wait_ge(stage_done, f0 + 4 * 12)
            sp.dma_start(xl[:, :, :].rearrange("p t d -> p (t d)"), xspill).then_inc(x_back, 16)
            plan_split(n, len(TQ[l]))
            sp_ffn(sp, n, rel, l)
            n["fence"] = f0 + 4 * STAGES2

        def plan_attn(n, heads, units):
            Attn(n, heads, units)

        def pool_layer(pool, n, l):
            plan_split(n, TA)
            pool_params2(pool, l)
            fence(pool, n)
            pool_proj(pool, n, l)
            fence(pool, n)
            pool.wait_ge(spill, 16 * (l + 1))
            pool_bias(pool, l, (0, 1))
            pool_bias(pool, l, (2, 3))
            for _ in range(8):
                fence(pool, n)
            plan_gm(n, l)
            plan_t(n, cqkv_pairs(l))
            plan_lin(n, BUQ(l))
            plan_lin(n, BUKV)
            plan_t(n, nagm_pairs(l))
            plan_t(n, mla_pairs(l))
            p = merge_counts(n, l)
            fence(pool, n)
            pool_merge(pool, n, l)
            fence(pool, n)
            plan_t(n, acc_pairs(l))
            fence(pool, n)
            fence(pool, n)
            plan_lin(n, WO2(l))
            plan_split(n, len(TQ[l]))
            fence(pool, n)
            Ffn(n, l)
            fence(pool, n)

        def pe_layer(pe, n, l):
            pe_norm_split(pe, n, TA, 0)
            fence(pe, n)
            pe_proj(pe, n, l)
            fence(pe, n)
            pe_attn(pe, n, *na_spec(l))
            fence(pe, n)
            pe_gm(pe, n, l)
            fence(pe, n)
            pe_t(pe, n, cqkv_pairs(l))
            fence(pe, n)
            pe_lin(pe, n, BUQ(l), q_lhs)
            fence(pe, n)
            pe_lin(pe, n, BUKV, kv_lhs)
            fence(pe, n)
            fence(pe, n)
            pe_attn(pe, n, *mla_spec(l))
            fence(pe, n)
            pe_t(pe, n, nagm_pairs(l))
            fence(pe, n)
            pe_t(pe, n, mla_pairs(l))
            fence(pe, n)
            for s in hh_back:
                pe.wait_ge(s, l + 1)
            pe_merge(pe, n, l)
            fence(pe, n)
            pe_t(pe, n, acc_pairs(l))
            fence(pe, n)
            pe_lin(pe, n, WO2(l), h_lhs)
            fence(pe, n)
            pe_norm_split(pe, n, len(TQ[l]), 1)
            fence(pe, n)
            pe_ffn(pe, n, l)
            fence(pe, n)

        def act_layer(act, n, l):
            act_norm_split(act, n, TA, l + 1, 0)
            fence(act, n)
            act.dma_start(hTd, hT_hi[:, :].bitcast(F32)).then_inc(spill, 16)
            act_project(act, n, l)
            act.wait_ge(spill, 16 * (l + 1))
            fence(act, n)
            act_attn(act, n, *na_spec(l))
            fence(act, n)
            act_gm(act, n, l)
            fence(act, n)
            each_t(act, n, "a", cqkv_pairs(l))
            fence(act, n)
            each_lin(act, n, BUQ(l), "a", act_q)
            fence(act, n)
            each_lin(act, n, BUKV, "a", act_put)
            rms_heads(act, "a", n, TQ[l], qview, 8, 96, qg)
            fence(act, n)
            rms_heads(act, "a", n, ALLT, kview, 8, 96, kg)
            fence(act, n)
            act_attn(act, n, *mla_spec(l))
            fence(act, n)
            each_t(act, n, "a", nagm_pairs(l))
            fence(act, n)
            each_t(act, n, "a", mla_pairs(l))
            fence(act, n)
            act_merge(act, n, l)
            fence(act, n)
            load_gate(act, l + 1, 2)
            each_t(act, n, "a", acc_pairs(l))
            fence(act, n)
            plan_lin(n, WO2(l))
            fence(act, n)
            act_norm_split(act, n, len(TQ[l]), l + 1, 1)
            fence(act, n)
            act_ffn(act, n, l)
            fence(act, n)

        def dve_layer(dve, n, l):
            dve_norm_split(dve, n, TA, l + 1, 0)
            fence(dve, n)
            dve_project(dve, n, l)
            fence(dve, n)
            dve_attn(dve, n, *na_spec(l), tables=4 * l)
            fence(dve, n)
            dve_gm(dve, n, l)
            fence(dve, n)
            each_t(dve, n, "v", cqkv_pairs(l))
            fence(dve, n)
            each_lin(dve, n, BUQ(l), "v", dve_q)
            fence(dve, n)
            dve_mla_queries(dve, n, l)
            fence(dve, n)
            dve_mla_keys(dve, n, l)
            fence(dve, n)
            dve_attn(dve, n, *mla_spec(l))
            fence(dve, n)
            each_t(dve, n, "v", nagm_pairs(l))
            fence(dve, n)
            each_t(dve, n, "v", mla_pairs(l))
            fence(dve, n)
            dve_merge(dve, n, l)
            fence(dve, n)
            each_t(dve, n, "v", acc_pairs(l))
            fence(dve, n)
            dve.wait_ge(x_back, 16 * (2 * l + 1))
            dve_resid(dve, n, WO2(l))
            fence(dve, n)
            dve_norm_split(dve, n, len(TQ[l]), l + 1, 1)
            fence(dve, n)
            dve_ffn(dve, n, l)
            fence(dve, n)

        block = ctx.enter_context(nc.Block())
        W_IN = I["w_in"][0]
        NF = 16 + 2 * STAGES2
        WO1 = [(0, 512, LAT, "v"), (512, 1024, LAT, "v")]

        @block.sync
        def _(sp):
            n, rel = tally(), [0, 0]
            sp_first(sp)
            sp.dma_start(xl[:, 0:TL, :], I["x"][0].rearrange("(t p) d -> p t d", p=P)).then_inc(x_in, 16)
            sp.dma_start(xl[:, TL:TA, :], I["ctx"][0].rearrange("(t p) d -> p t d", p=P)).then_inc(x_in, 16)
            plan_norm(n, TA)
            sp_lin(sp, n, rel, W_IN, BL1)
            for plan in (plan_gate, plan_dec, plan_st, plan_o):
                plan(n)
            plan_turn(n, KT, LAT)
            sp_lin(sp, n, rel, I["w_out"][0], WO1)
            sp.wait_ge(stage_done, 4 * 10)
            for m in (1, 2):
                for x in range(2):
                    load_expert(sp, m, x, slice(x, x + 1))
            sp.wait_ge(stage_done, 4 * 11)
            for x in range(2):
                load_expert(sp, 0, x, slice(x, x + 1))
            for t in range(TL):
                sp.wait_ge(xn_ok, TA + t + 1)
                sp.dma_start(xnd[P * t:P * t + P, :], XK(t)).then_inc(xn_st, 16)
            plan_norm(n, TL)
            plan_route(n)
            sp.wait_ge(stage_done, 4 * 13)
            sp_moe(sp)
            n["fence"] = 4 * 16
            sp.wait_ge(stage_done, 4 * 16)
            sp.dma_start(xl[:, TL:TA, :], I["ctx_2"][0].rearrange("(t p) d -> p t d", p=P)).then_inc(x_in, 16)
            for l in range(2):
                sp_layer(sp, n, rel, l)
            F = 4 * NF
            sp.wait_ge(stage_done, F)
            sp.dma_start(out[0].rearrange("(t p) d -> p t d", p=P), xl[:, 0:TL, :]).then_inc(out_in, 16)
            sp.wait_ge(out_in, 16)

        @block.gpsimd
        def _(pool):
            n = tally()
            pool.dma_start(lamt, I["da_lambda"][0].rearrange("a d -> (a d)").partition_broadcast(P)).then_inc(prm, 16)
            pool.dma_start(subln, I["da_subln_g"][0].partition_broadcast(P)).then_inc(prm, 16)
            pool.dma_start(glag, I["gla_norm_g"][0].partition_broadcast(P)).then_inc(prm, 16)
            for m in range(2):
                pool.dma_start(w2a[16 * 0:16, 256 * m:256 * m + 256], I["gla_gate_w2"][0][m]).then_inc(prm, 16)
                pool.dma_start(w2a[16:17, 256 * m:256 * m + 256], I["gla_gate_b"][0][m:m + 1, :]).then_inc(prm, 16)
            fence(pool, n)
            fence(pool, n)
            for c in range(MSTEPS, 3 * MSTEPS):
                load_mod(pool, c)
            fence(pool, n)
            pool.memset(hT[:, 0:D], 0.0).then_inc(zero_ok, 1)
            pool.wait_ge(zero_ok, 1)
            for r in range(NE * CAP, NBLK * CAP, P):
                pool.dma_start(ybuf[r:r + P, :], hT[:, 0:D]).then_inc(ybz, 16)
            pool.wait_ge(ybz, 16 * (NBLK - NE) * CAP // P)
            for _ in range(6):
                fence(pool, n)
            for _ in range(2):
                fence(pool, n)
            pool_route_params(pool)
            fence(pool, n)
            pool_route(pool)
            pool.wait_ge(xn_st, 64)
            fence(pool, n)
            pool_moe(pool)
            fence(pool, n)
            pool.dma_start(fng, I["final_norm_g"].partition_broadcast(P)).then_inc(fng_in, 16)
            pool_comb(pool, n)
            fence(pool, n)
            fence(pool, n)
            plan_norm(n, TA)
            plan_lin(n, BL1)
            for plan in (plan_gate, plan_dec, plan_st, plan_o):
                plan(n)
            plan_turn(n, KT, LAT)
            plan_lin(n, WO1)
            plan_norm(n, TL)
            plan_route(n)
            for l in range(2):
                pool_layer(pool, n, l)

        @block.tensor
        def _(pe):
            n = tally()
            pe_first(pe)
            fence(pe, n)
            pe_norm(pe, n, TA)
            fence(pe, n)
            pe_lin(pe, n, BL1, h_lhs)
            fence(pe, n)
            pe_mod_turn(pe, (1, 2))
            fence(pe, n)
            pe_attn(pe, n, *da_spec())
            fence(pe, n)
            pe_gates(pe, n)
            fence(pe, n)
            pe_dec(pe, n)
            fence(pe, n)
            pe_states(pe, n)
            fence(pe, n)
            pe_glao(pe, n)
            fence(pe, n)
            pe_turn(pe, n, KT, LAT, lambda k, t: pjt[:, t, 128 * k:128 * k + 128])
            fence(pe, n)
            pe_lin(pe, n, WO1, h_lhs)
            fence(pe, n)
            pe_norm(pe, n, TL, keep=XK)
            fence(pe, n)
            pe_route(pe, n)
            fence(pe, n)
            pe_moe(pe)
            fence(pe, n)
            fence(pe, n)
            fence(pe, n)
            for l in range(2):
                pe_layer(pe, n, l)

        @block.scalar
        def _(act):
            n = tally()
            load_rows(act)
            act_first(act)
            fence(act, n)
            act.wait_ge(x_in, 32)
            act_norm(act, n, TA, 0, 0)
            fence(act, n)
            each_lin(act, n, BL1, "a", act_put)
            fence(act, n)
            act_lambda(act, n)
            act_mod_turn(act, (1, 2))
            fence(act, n)
            act_attn(act, n, *da_spec())
            rms_heads(act, "a", n, LAT, hv(DQ, 4, 128), 4, 128, subln)
            fence(act, n)
            act_gates(act, n)
            fence(act, n)
            act_dec(act, n)
            fence(act, n)
            each_states(act, n, "a")
            fence(act, n)
            act_glao(act, n)
            fence(act, n)
            load_gate(act, 0, 2)
            each_turn(act, n, "a", KT, LAT, hT_dst)
            fence(act, n)
            plan_lin(n, WO1)
            fence(act, n)
            act_norm(act, n, TL, 0, 1)
            fence(act, n)
            act_route(act, n)
            act.sem_inc(y_out, 16)
            fence(act, n)
            act_moe(act)
            fence(act, n)
            load_gate(act, 0, 5)
            fence(act, n)
            act_final(act, n)
            fence(act, n)
            act.wait_ge(x_in, 48)
            for l in range(2):
                act_layer(act, n, l)

        @block.vector
        def _(dve):
            n = tally()
            dve_first(dve)
            fence(dve, n)
            dve.wait_ge(x_in, 32)
            dve_norm(dve, n, TA, 0, 0)
            fence(dve, n)
            each_lin(dve, n, BL1, "v", dve_put)
            fence(dve, n)
            dve_mod_turn(dve, (1, 2))
            dve_da_before(dve)
            dve_lambda(dve, n)
            fence(dve, n)
            dve_attn(dve, n, *da_spec(), lam=lam)
            rms_heads(dve, "v", n, LAT, hv(DQ, 4, 128), 4, 128, subln, mul=1.0 - (0.8 - 0.6))
            fence(dve, n)
            dve_gates(dve, n)
            fence(dve, n)
            dve_dec(dve, n)
            fence(dve, n)
            each_states(dve, n, "v")
            fence(dve, n)
            dve_glao(dve, n)
            fence(dve, n)
            each_turn(dve, n, "v", KT, LAT, hT_dst)
            fence(dve, n)
            dve_resid(dve, n, WO1)
            fence(dve, n)
            dve_norm(dve, n, TL, 0, 1, keep=XK)
            fence(dve, n)
            dve_route(dve, n)
            fence(dve, n)
            dve_moe(dve)
            fence(dve, n)
            dve_comb(dve, n)
            fence(dve, n)
            dve.wait_ge(fng_in, 16)
            dve_final(dve, n)
            fence(dve, n)
            dve.wait_ge(x_in, 48)
            for l in range(2):
                dve_layer(dve, n, l)


_INS = ["x", "c", "ctx", "c_ctx", "w_ada", "b_ada", "norm_mix_g", "norm_ffn_g", "w_in", "da_lambda", "da_subln_g",
        "gla_gate_w2", "gla_gate_b", "gla_norm_g", "w_out", "router_group_w", "router_group_b", "router_expert_w",
        "router_expert_b", "expert_w_gate", "expert_w_up", "expert_w_down", "final_norm_g", "c_2", "ctx_2",
        "c_ctx_2", "w_mod_2", "b_mod_2", "g_norm1_2", "g_norm2_2", "w_in_2", "na_q_gain_2", "na_k_gain_2", "na_rpb_2",
        "na_w_o_2", "gm_ln_g_2", "gm_ln_b_2", "gm_w_s_2", "gm_b_s_2", "gm_w_o_2", "mla_cq_gain_2", "mla_ckv_gain_2",
        "mla_w_uq_2", "mla_w_ukv_2", "mla_q_gain_2", "mla_k_gain_2", "mla_w_o_2", "w_out_2", "ffn_w1_2", "ffn_w2_2"]


def kernel(**inputs):
    import concourse.bacc as _bacc
    from concourse.bass_utils import run_bass_kernel_spmd as _run

    nc = _bacc.Bacc("TRN2", target_bir_lowering=False, num_devices=1)
    arrays, aps = {}, {}
    for name in _INS + ["cst"]:
        a = np.ascontiguousarray(constants() if name == "cst" else inputs[name])
        arrays[f"in_{name}_dram"] = a
        aps[name] = nc.dram_tensor(f"in_{name}_dram", a.shape, mybir.dt.from_np(a.dtype), kind="ExternalInput").ap()
    out = nc.dram_tensor("out_0_dram", (1, TL * P, D), F32, kind="ExternalOutput").ap()
    program(nc, aps, out)
    r = _run(nc, [arrays], core_ids=[0])
    return r.results[0]["out_0_dram"]
```
